# Optimizing a Trainium2 kernel written in Bass

```python
import jax, jax.numpy as jnp
from jax import lax
import numpy as np
import jax
import jax.numpy as jnp

D_MODEL = 1024
BATCH = 1
SEQ = 256
DEPTH = 2

N_META = 16
GRID_W = 64
BLOCK = 128
FRONT_PAD = BLOCK - N_META
EPS = 1e-6
D_FF = 4 * D_MODEL

A_HEADS = 4
A_DK = 128
A_DV = 128
A_CHUNK = 64
A_CONV = 5
A_QKW = A_HEADS * A_DK
A_VW = A_HEADS * A_DV

B_HEADS = 8
B_KV = 2
B_HD = 64
B_WIN = 128
B_QW = B_HEADS * B_HD
B_KVW = B_KV * B_HD

C_HEADS = 8
C_KV = 2
C_HD = 128
C_QW = C_HEADS * C_HD
C_KVW = C_KV * C_HD
ROPE_THETA = 10000.0

MIX_AB = A_VW + B_QW
AB_SIZES = (A_QKW, A_QKW, A_VW, A_VW, 2 * A_HEADS, 2 * A_HEADS, B_QW, B_KVW, B_KVW)
IN_AB = sum(AB_SIZES)
IN_C = C_QW + 2 * C_KVW


def rmsnorm(x, g):
    xf = x.astype(jnp.float32)
    y = xf * lax.rsqrt(jnp.mean(xf * xf, axis=-1, keepdims=True) + EPS)
    return (y * g.astype(jnp.float32)).astype(x.dtype)

def l2norm(x):
    return x * lax.rsqrt(jnp.sum(x * x, axis=-1, keepdims=True) + EPS)

def front_pad(t, n):
    return jnp.pad(t, [(0, 0), (n, 0)] + [(0, 0)] * (t.ndim - 2))

def split_cols(t, sizes):
    idx = np.cumsum(np.array(sizes))[:-1].tolist()
    return jnp.split(t, idx, axis=-1)

def centred_conv(x, w):
    k = w.shape[0]
    h = k // 2
    n = x.shape[1]
    xp = jnp.pad(x, ((0, 0), (h, h), (0, 0)))
    y = xp[:, 0:n] * w[0]
    for j in range(1, k):
        y = y + xp[:, j:j + n] * w[j]
    return y

def gated_delta_chunked(q, k, v, beta, g):
    f32 = jnp.float32
    q, k, v, beta, g = (t.astype(f32) for t in (q, k, v, beta, g))
    bsz, t_len, nh, dk = q.shape
    dv = v.shape[-1]
    c = A_CHUNK
    nc = t_len // c

    def blk(t):
        return jnp.moveaxis(t.reshape(bsz, nc, c, nh, *t.shape[3:]), 3, 1)

    q, k, v, beta, g = blk(q), blk(k), blk(v), blk(beta), blk(g)
    gc = jnp.cumsum(g, axis=-1)
    incl = jnp.tril(jnp.ones((c, c), bool))
    strict = jnp.tril(jnp.ones((c, c), bool), -1)
    decay = jnp.exp(jnp.where(incl, gc[..., :, None] - gc[..., None, :], -jnp.inf))
    kb = k * beta[..., None]
    a_mat = jnp.where(strict, jnp.einsum('bhnid,bhnjd->bhnij', kb, k) * decay, 0.0)
    rhs = jnp.concatenate([v * beta[..., None], kb * jnp.exp(gc)[..., None]], axis=-1)
    sol = lax.linalg.triangular_solve(a_mat, rhs, left_side=True, lower=True,
                                      unit_diagonal=True)
    u, w = sol[..., :dv], sol[..., dv:]
    qk = jnp.einsum('bhnid,bhnjd->bhnij', q, k) * decay
    q_dec = q * jnp.exp(gc)[..., None]
    k_dec = k * jnp.exp(gc[..., -1:] - gc)[..., None]
    g_last = jnp.exp(gc[..., -1])

    def step(s, xs):
        q_n, k_n, u_n, w_n, qk_n, gl_n = xs
        v_new = u_n - jnp.einsum('bhck,bhkv->bhcv', w_n, s)
        o = jnp.einsum('bhck,bhkv->bhcv', q_n, s) + jnp.einsum('bhij,bhjv->bhiv', qk_n, v_new)
        s = s * gl_n[..., None, None] + jnp.einsum('bhck,bhcv->bhkv', k_n, v_new)
        return s, o

    xs = tuple(jnp.moveaxis(t, 2, 0) for t in (q_dec, k_dec, u, w, qk, g_last))
    s0 = jnp.zeros((bsz, nh, dk, dv), f32)
    _, o = lax.scan(step, s0, xs)
    return jnp.transpose(o, (1, 0, 3, 2, 4)).reshape(bsz, t_len, nh, dv)

def delta_mixer(hq, hk, hv, hz, hb, ha, conv_w, a_log, dt_bias, o_gain):
    bsz, n, _ = hq.shape
    qkv = jax.nn.silu(centred_conv(jnp.concatenate([hq, hk, hv], axis=-1), conv_w))
    q, k, v = split_cols(qkv, (A_QKW, A_QKW, A_VW))
    q = l2norm(q.reshape(bsz, n, A_HEADS, A_DK).astype(jnp.float32)) * (A_DK ** -0.5)
    k = l2norm(k.reshape(bsz, n, A_HEADS, A_DK).astype(jnp.float32))
    v = v.reshape(bsz, n, A_HEADS, A_DV).astype(jnp.float32)
    beta = jax.nn.sigmoid(hb.astype(jnp.float32)).reshape(bsz, n, 2, A_HEADS)
    g = -jnp.exp(a_log.astype(jnp.float32)) * jax.nn.softplus(
        ha.astype(jnp.float32).reshape(bsz, n, 2, A_HEADS) + dt_bias.astype(jnp.float32))
    q, k, v, beta, g = (front_pad(t, FRONT_PAD) for t in (q, k, v, beta, g))
    fwd = gated_delta_chunked(q, k, v, beta[:, :, 0], g[:, :, 0])
    rev = lambda t: jnp.flip(t, axis=1)
    bwd = rev(gated_delta_chunked(rev(q), rev(k), rev(v), rev(beta[:, :, 1]), rev(g[:, :, 1])))
    o = (fwd + bwd)[:, FRONT_PAD:]
    o = rmsnorm(o, o_gain) * jax.nn.silu(hz.reshape(bsz, n, A_HEADS, A_DV).astype(jnp.float32))
    return o.reshape(bsz, n, A_VW).astype(hq.dtype)

def window_mixer(q, k, v, sink):
    bsz, n = q.shape[:2]
    grp = B_HEADS // B_KV
    lp = n + FRONT_PAD
    nb = lp // BLOCK
    qb = front_pad(q, FRONT_PAD).reshape(bsz, nb, BLOCK, B_KV, grp, B_HD)

    def ext(t):
        t = jnp.pad(t, ((0, 0), (FRONT_PAD + BLOCK, BLOCK), (0, 0), (0, 0)))
        t = t.reshape(bsz, nb + 2, BLOCK, B_KV, B_HD)
        return jnp.concatenate([t[:, :-2], t[:, 1:-1], t[:, 2:]], axis=2)

    kw, vw = ext(k), ext(v)
    mk, mv = k[:, :N_META], v[:, :N_META]
    s_win = jnp.einsum('bnqkgd,bnskd->bnkgqs', qb, kw).astype(jnp.float32)
    s_meta = jnp.einsum('bnqkgd,bmkd->bnkgqm', qb, mk).astype(jnp.float32)
    r = jnp.arange(BLOCK)[:, None]
    cpos = jnp.arange(3 * BLOCK)[None, :]
    dist = jnp.abs(BLOCK + r - cpos)
    pk = (jnp.arange(nb)[:, None] - 1) * BLOCK + cpos
    in_seq = (pk >= BLOCK) & (pk < lp)
    valid = (dist <= B_WIN)[None] & in_seq[:, None, :]
    slopes = jnp.exp2(-8.0 * (jnp.arange(B_HEADS, dtype=jnp.float32) + 1.0) / B_HEADS)
    bias = -slopes.reshape(B_KV, grp, 1, 1) * dist.astype(jnp.float32)
    s_win = jnp.where(valid[None, :, None, None], s_win + bias, -jnp.inf)
    s_sink = jnp.broadcast_to(sink.astype(jnp.float32).reshape(B_KV, grp, 1, 1),
                              (bsz, nb, B_KV, grp, BLOCK, 1))
    p = jax.nn.softmax(jnp.concatenate([s_win, s_meta, s_sink], axis=-1), axis=-1)
    p_win = p[..., :3 * BLOCK].astype(v.dtype)
    p_meta = p[..., 3 * BLOCK:3 * BLOCK + N_META].astype(v.dtype)
    o = (jnp.einsum('bnkgqs,bnskd->bnqkgd', p_win, vw)
         + jnp.einsum('bnkgqm,bmkd->bnqkgd', p_meta, mv))
    return o.reshape(bsz, lp, B_HEADS * B_HD)[:, FRONT_PAD:]

def ab_mixer(u, w_in, conv_w, a_log, dt_bias, a_out_g, bq_g, bk_g, sink, w_out):
    bsz, n, _ = u.shape
    proj = u @ w_in
    qa, ka, va, za, ba, aa, qb, kb, vb = split_cols(proj, AB_SIZES)
    ya = delta_mixer(qa, ka, va, za, ba, aa, conv_w, a_log, dt_bias, a_out_g)
    qb = rmsnorm(qb.reshape(bsz, n, B_HEADS, B_HD), bq_g) * (B_HD ** -0.5)
    kb = rmsnorm(kb.reshape(bsz, n, B_KV, B_HD), bk_g)
    vb = vb.reshape(bsz, n, B_KV, B_HD)
    yb = window_mixer(qb, kb, vb, sink)
    return jnp.concatenate([ya, yb.astype(ya.dtype)], axis=-1) @ w_out

def axial_rope(rows):
    row = jnp.repeat(jnp.arange(rows), GRID_W)
    col = jnp.tile(jnp.arange(GRID_W), rows)
    meta = jnp.arange(N_META) - N_META
    row = jnp.concatenate([meta, row]).astype(jnp.float32)
    col = jnp.concatenate([meta, col]).astype(jnp.float32)
    axis_dim = C_HD // 2
    freqs = ROPE_THETA ** (-jnp.arange(0, axis_dim, 2, dtype=jnp.float32) / axis_dim)
    ang = jnp.concatenate([row[:, None] * freqs, col[:, None] * freqs], axis=-1)
    return jnp.cos(ang), jnp.sin(ang)

def apply_rope(x, cos, sin):
    xf = x.astype(jnp.float32).reshape(*x.shape[:-1], x.shape[-1] // 2, 2)
    x0, x1 = xf[..., 0], xf[..., 1]
    c = cos[None, :, None, :]
    s = sin[None, :, None, :]
    out = jnp.stack([x0 * c - x1 * s, x0 * s + x1 * c], axis=-1)
    return out.reshape(x.shape).astype(x.dtype)

def dense_mixer(q, k, v):
    bsz, n = q.shape[:2]
    grp = C_HEADS // C_KV
    lp = n + FRONT_PAD
    nb = lp // BLOCK
    qb = jnp.moveaxis(front_pad(q, FRONT_PAD).reshape(bsz, nb, BLOCK, C_KV, grp, C_HD), 1, 0)

    def one_block(qi):
        s = jnp.einsum('bqkgd,bskd->bkgqs', qi, k).astype(jnp.float32)
        p = jax.nn.softmax(s, axis=-1).astype(v.dtype)
        return jnp.einsum('bkgqs,bskd->bqkgd', p, v)

    o = lax.map(one_block, qb)
    return jnp.moveaxis(o, 0, 1).reshape(bsz, lp, C_QW)[:, FRONT_PAD:]

def c_mixer(u, w_qkv, qg, kg, w_out, cos, sin):
    bsz, n, _ = u.shape
    q, k, v = split_cols(u @ w_qkv, (C_QW, C_KVW, C_KVW))
    q = apply_rope(rmsnorm(q.reshape(bsz, n, C_HEADS, C_HD), qg), cos, sin) * (C_HD ** -0.5)
    k = apply_rope(rmsnorm(k.reshape(bsz, n, C_KV, C_HD), kg), cos, sin)
    v = v.reshape(bsz, n, C_KV, C_HD)
    return dense_mixer(q, k, v) @ w_out

def first_inputs(seed: int = 0) -> dict:
    key = jax.random.key(seed)
    ks = jax.random.split(key, 20)
    n_even = (DEPTH + 1) // 2
    n_odd = DEPTH // 2
    nrm = lambda k, shape, scale: jax.random.normal(k, shape, jnp.float32) * scale
    gain = lambda k, shape: 1.0 + 0.02 * jax.random.normal(k, shape, jnp.float32)
    dt = jnp.exp(jax.random.uniform(ks[6], (n_even, 2, A_HEADS), jnp.float32,
                                    np.log(1e-3), np.log(1e-1)))
    return {
        "x": nrm(ks[0], (BATCH, SEQ, D_MODEL), 1.0),
        "meta_tokens": nrm(ks[1], (N_META, D_MODEL), 1.0),
        "attn_norm_g": gain(ks[2], (DEPTH, D_MODEL)),
        "mlp_norm_g": gain(ks[3], (DEPTH, D_MODEL)),
        "w_in_ab": nrm(ks[4], (n_even, D_MODEL, IN_AB), D_MODEL ** -0.5),
        "conv_w_a": nrm(ks[5], (n_even, A_CONV, 2 * A_QKW + A_VW), A_CONV ** -0.5),
        "a_log": jnp.log(jax.random.uniform(ks[7], (n_even, 2, A_HEADS), jnp.float32, 1.0, 16.0)),
        "dt_bias": dt + jnp.log(-jnp.expm1(-dt)),
        "a_out_norm_g": gain(ks[8], (n_even, A_DV)),
        "b_q_norm_g": gain(ks[9], (n_even, B_HD)),
        "b_k_norm_g": gain(ks[10], (n_even, B_HD)),
        "b_sink": nrm(ks[11], (n_even, B_HEADS), 0.5),
        "w_out_ab": nrm(ks[12], (n_even, MIX_AB, D_MODEL), MIX_AB ** -0.5),
        "w_qkv_c": nrm(ks[13], (n_odd, D_MODEL, IN_C), D_MODEL ** -0.5),
        "c_q_norm_g": gain(ks[14], (n_odd, C_HD)),
        "c_k_norm_g": gain(ks[15], (n_odd, C_HD)),
        "w_out_c": nrm(ks[16], (n_odd, C_QW, D_MODEL), C_QW ** -0.5),
        "w_ff1": nrm(ks[17], (DEPTH, D_MODEL, D_FF), D_MODEL ** -0.5),
        "w_ff2": nrm(ks[18], (DEPTH, D_FF, D_MODEL), D_FF ** -0.5),
    }

def first_block(x, meta_tokens, attn_norm_g, mlp_norm_g, w_in_ab, conv_w_a, a_log, dt_bias,
              a_out_norm_g, b_q_norm_g, b_k_norm_g, b_sink, w_out_ab, w_qkv_c, c_q_norm_g,
              c_k_norm_g, w_out_c, w_ff1, w_ff2):
    bsz, n_tok, _ = x.shape
    rows = n_tok // GRID_W
    meta = jnp.broadcast_to(meta_tokens.astype(x.dtype)[None], (bsz, N_META, x.shape[-1]))
    h = jnp.concatenate([meta, x], axis=1)
    cos, sin = axial_rope(rows)
    for layer in range(DEPTH):
        i = layer // 2
        u = rmsnorm(h, attn_norm_g[layer])
        if layer % 2 == 0:
            mix = ab_mixer(u, w_in_ab[i], conv_w_a[i], a_log[i], dt_bias[i], a_out_norm_g[i],
                           b_q_norm_g[i], b_k_norm_g[i], b_sink[i], w_out_ab[i])
        else:
            mix = c_mixer(u, w_qkv_c[i], c_q_norm_g[i], c_k_norm_g[i], w_out_c[i], cos, sin)
        h = h + mix.astype(h.dtype)
        u = rmsnorm(h, mlp_norm_g[layer])
        h = h + jnp.square(jax.nn.relu(u @ w_ff1[layer])) @ w_ff2[layer]
    return h[:, N_META:]


N_MEM = 256
NEG_INF = -1e30

HEAD_DIM = 64
ROPE_DIM = HEAD_DIM // 4
ROPE_THETA_2 = 500000.0

A_HEADS_2 = 8
A_WIDTH = A_HEADS_2 * HEAD_DIM
MOBA_BLOCK = 256
MOBA_TOPK = 3
MOBA_QCHUNK = 32

B_GROUPS = 8
B_WIDTH = B_GROUPS * HEAD_DIM
GMLP_CHUNK = 128

GLA_HEADS = 4
GLA_DK = (D_MODEL // 2) // GLA_HEADS
GLA_DV = D_MODEL // GLA_HEADS
GLA_LOWRANK = 16
GLA_TAU = 16.0
GLA_CHUNK = 64

X_HEADS = 4
X_HEAD_DIM = D_MODEL // X_HEADS

D_FF_2 = -(-8 * D_MODEL // (3 * 256)) * 256

EV_IN = 3 * A_WIDTH + 2 * B_WIDTH
OD_IN = 2 * GLA_HEADS * GLA_DK + 2 * GLA_HEADS * GLA_DV


def rmsnorm_2(x, g):
    xf = x.astype(jnp.float32)
    y = xf * lax.rsqrt(jnp.mean(xf * xf, axis=-1, keepdims=True) + EPS)
    return (y * g.astype(jnp.float32)).astype(x.dtype)

def layernorm(x, g, b):
    xf = x.astype(jnp.float32)
    mu = jnp.mean(xf, axis=-1, keepdims=True)
    var = jnp.mean(jnp.square(xf - mu), axis=-1, keepdims=True)
    y = (xf - mu) * lax.rsqrt(var + EPS) * g.astype(jnp.float32) + b.astype(jnp.float32)
    return y.astype(x.dtype)

def partial_rope(x, positions):
    half = ROPE_DIM // 2
    inv_freq = ROPE_THETA_2 ** (-jnp.arange(half, dtype=jnp.float32) * 2.0 / ROPE_DIM)
    ang = positions.astype(jnp.float32)[:, None, :, None] * inv_freq
    cos, sin = jnp.cos(ang), jnp.sin(ang)
    xf = x.astype(jnp.float32)
    x1, x2 = xf[..., :half], xf[..., half:ROPE_DIM]
    out = jnp.concatenate([x1 * cos - x2 * sin, x2 * cos + x1 * sin, xf[..., ROPE_DIM:]], axis=-1)
    return out.astype(x.dtype)

def moba_attention(q, k, v):
    Bn, H, S, Dh = q.shape
    S_pad = -(-S // MOBA_BLOCK) * MOBA_BLOCK
    pad = [(0, 0), (0, 0), (0, S_pad - S), (0, 0)]
    q, k, v = jnp.pad(q, pad), jnp.pad(k, pad), jnp.pad(v, pad)
    nb = S_pad // MOBA_BLOCK
    topk = min(MOBA_TOPK, nb)
    scale = Dh ** -0.5
    kb = k.reshape(Bn, H, nb, MOBA_BLOCK, Dh)
    vb = v.reshape(Bn, H, nb, MOBA_BLOCK, Dh)
    k_mean = jnp.mean(kb.astype(jnp.float32), axis=3)
    gate = jnp.einsum('bhsd,bhnd->bhsn', q.astype(jnp.float32), k_mean)
    own = jnp.arange(S_pad) // MOBA_BLOCK
    past = jnp.arange(nb)[None, :] < own[:, None]
    gate = jnp.where(past[None, None], gate, NEG_INF)
    _, sel = lax.top_k(gate, topk)
    valid = sel < own[None, None, :, None]

    nq = S_pad // MOBA_QCHUNK
    q_c = q.reshape(Bn, H, nq, MOBA_QCHUNK, Dh).transpose(2, 0, 1, 3, 4)
    sel_c = sel.reshape(Bn, H, nq, MOBA_QCHUNK, topk).transpose(2, 0, 1, 3, 4)
    valid_c = valid.reshape(Bn, H, nq, MOBA_QCHUNK, topk).transpose(2, 0, 1, 3, 4)
    chunk_ids = jnp.arange(nq, dtype=jnp.int32)
    bi = jnp.arange(Bn)[:, None, None, None]
    hi = jnp.arange(H)[None, :, None, None]
    key_idx = jnp.arange(MOBA_BLOCK)

    def one_chunk(args):
        qc, selc, validc, ci = args
        blk = (ci * MOBA_QCHUNK) // MOBA_BLOCK
        k_own = lax.dynamic_index_in_dim(kb, blk, axis=2, keepdims=False)
        v_own = lax.dynamic_index_in_dim(vb, blk, axis=2, keepdims=False)
        qpos = (ci * MOBA_QCHUNK) % MOBA_BLOCK + jnp.arange(MOBA_QCHUNK)
        causal = key_idx[None, :] <= qpos[:, None]
        s_own = jnp.einsum('bhqd,bhkd->bhqk', qc, k_own, preferred_element_type=jnp.float32) * scale
        s_own = jnp.where(causal[None, None], s_own, NEG_INF)
        k_sel = kb[bi, hi, selc]
        v_sel = vb[bi, hi, selc]
        s_sel = jnp.einsum('bhqd,bhqnkd->bhqnk', qc, k_sel, preferred_element_type=jnp.float32) * scale
        s_sel = jnp.where(validc[..., None], s_sel, NEG_INF)
        logits = jnp.concatenate([s_own, s_sel.reshape(Bn, H, MOBA_QCHUNK, topk * MOBA_BLOCK)], axis=-1)
        p = jax.nn.softmax(logits, axis=-1)
        p_own = p[..., :MOBA_BLOCK].astype(v.dtype)
        p_sel = p[..., MOBA_BLOCK:].reshape(Bn, H, MOBA_QCHUNK, topk, MOBA_BLOCK).astype(v.dtype)
        out = (jnp.einsum('bhqk,bhkd->bhqd', p_own, v_own, preferred_element_type=jnp.float32)
               + jnp.einsum('bhqnk,bhqnkd->bhqd', p_sel, v_sel, preferred_element_type=jnp.float32))
        return out.astype(q.dtype)

    out = lax.map(one_chunk, (q_c, sel_c, valid_c, chunk_ids))
    out = out.transpose(1, 2, 0, 3, 4).reshape(Bn, H, S_pad, Dh)
    return out[:, :, :S]

def chunked_spatial_gating(u, v, w_s, b_s, ln_g, ln_b):
    Bn, S, G, Dg = v.shape
    nc = S // GMLP_CHUNK
    vn = layernorm(v, ln_g, ln_b).reshape(Bn, nc, GMLP_CHUNK, G, Dg)
    mask = jnp.tril(jnp.ones((GMLP_CHUNK, GMLP_CHUNK), dtype=w_s.dtype))
    ws = w_s * mask[None]
    mixed = jnp.einsum('gij,bcjgd->bcigd', ws, vn) + b_s.T[None, None, :, :, None]
    return u * mixed.reshape(Bn, S, G, Dg).astype(u.dtype)

def even_mixer(h, positions, w_in, q_gain, k_gain, w_s, b_s, ln_g, ln_b, w_out):
    Bn, S, _ = h.shape
    proj = h @ w_in
    q, k, v, pu, pv = jnp.split(proj, [A_WIDTH, 2 * A_WIDTH, 3 * A_WIDTH, 3 * A_WIDTH + B_WIDTH], axis=-1)

    def heads(t):
        return t.reshape(Bn, S, A_HEADS_2, HEAD_DIM).transpose(0, 2, 1, 3)

    q = partial_rope(rmsnorm_2(heads(q), q_gain), positions)
    k = partial_rope(rmsnorm_2(heads(k), k_gain), positions)
    a = moba_attention(q, k, heads(v)).transpose(0, 2, 1, 3).reshape(Bn, S, A_WIDTH)
    u = jax.nn.gelu(pu, approximate=False).reshape(Bn, S, B_GROUPS, HEAD_DIM)
    vg = jax.nn.gelu(pv, approximate=False).reshape(Bn, S, B_GROUPS, HEAD_DIM)
    g = chunked_spatial_gating(u, vg, w_s, b_s, ln_g, ln_b).reshape(Bn, S, B_WIDTH)
    return jnp.concatenate([a, g], axis=-1) @ w_out

def gla_chunked(q, k, v, log_a):
    Bn, H, S, dk = q.shape
    dv = v.shape[-1]
    nc = S // GLA_CHUNK
    f32 = jnp.float32
    qc = q.astype(f32).reshape(Bn, H, nc, GLA_CHUNK, dk)
    kc = k.astype(f32).reshape(Bn, H, nc, GLA_CHUNK, dk)
    vc = v.astype(f32).reshape(Bn, H, nc, GLA_CHUNK, dv)
    b = jnp.cumsum(log_a.astype(f32).reshape(Bn, H, nc, GLA_CHUNK, dk), axis=3)
    b_last = b[:, :, :, -1:, :]
    q_in = qc * jnp.exp(b)
    k_in = kc * jnp.exp(-b)
    causal = jnp.tril(jnp.ones((GLA_CHUNK, GLA_CHUNK), dtype=bool))
    att = jnp.where(causal, jnp.einsum('bhnid,bhnjd->bhnij', q_in, k_in), 0.0)
    o_intra = jnp.einsum('bhnij,bhnjv->bhniv', att, vc)
    k_state = kc * jnp.exp(b_last - b)
    d_state = jnp.einsum('bhnjd,bhnjv->bhndv', k_state, vc)
    decay = jnp.exp(b_last[:, :, :, 0, :])

    def step(s_prev, xs):
        ds_n, dec_n = xs
        return dec_n[..., None] * s_prev + ds_n, s_prev

    _, s_before = lax.scan(step, jnp.zeros((Bn, H, dk, dv), f32),
                           (jnp.moveaxis(d_state, 2, 0), jnp.moveaxis(decay, 2, 0)))
    s_before = jnp.moveaxis(s_before, 0, 2)
    o_inter = jnp.einsum('bhnid,bhndv->bhniv', q_in, s_before)
    return (o_intra + o_inter).reshape(Bn, H, S, dv).astype(v.dtype)

def gla_mixer(h, w_in, w_g1, w_g2, b_g, o_gain, w_out):
    Bn, S, _ = h.shape
    qk_w = GLA_HEADS * GLA_DK
    v_w = GLA_HEADS * GLA_DV
    proj = h @ w_in
    q, k, v, r = jnp.split(proj, [qk_w, 2 * qk_w, 2 * qk_w + v_w], axis=-1)
    log_a = jax.nn.log_sigmoid(((h @ w_g1) @ w_g2 + b_g).astype(jnp.float32)) / GLA_TAU

    def heads(t, d):
        return t.reshape(Bn, S, GLA_HEADS, d).transpose(0, 2, 1, 3)

    o = gla_chunked(heads(q, GLA_DK) * (GLA_DK ** -0.5), heads(k, GLA_DK),
                    heads(v, GLA_DV), heads(log_a, GLA_DK))
    o = rmsnorm_2(o, o_gain[:, None, :])
    o = o.transpose(0, 2, 1, 3).reshape(Bn, S, v_w) * jax.nn.silu(r)
    return o @ w_out

def mem_cross_attention(h, mem_n, w_q, w_kv, q_gain, k_gain, w_out):
    Bn, S, _ = h.shape
    M = mem_n.shape[1]
    q = rmsnorm_2((h @ w_q).reshape(Bn, S, X_HEADS, X_HEAD_DIM), q_gain)
    k, v = jnp.split(mem_n @ w_kv, 2, axis=-1)
    k = rmsnorm_2(k.reshape(Bn, M, X_HEADS, X_HEAD_DIM), k_gain)
    v = v.reshape(Bn, M, X_HEADS, X_HEAD_DIM)
    s = jnp.einsum('bqhd,bkhd->bhqk', q, k, preferred_element_type=jnp.float32) * (X_HEAD_DIM ** -0.5)
    p = jax.nn.softmax(s, axis=-1).astype(v.dtype)
    o = jnp.einsum('bhqk,bkhd->bqhd', p, v).reshape(Bn, S, D_MODEL)
    return o @ w_out

def swiglu(h, w_gu, w_down):
    g, u = jnp.split(h @ w_gu, 2, axis=-1)
    return (jax.nn.silu(g) * u) @ w_down

def second_inputs(seed: int = 0) -> dict:
    key = jax.random.key(seed)
    ks = iter(jax.random.split(key, 32))
    f32 = jnp.float32
    n_ev = (DEPTH + 1) // 2
    n_od = DEPTH // 2

    def nrm(shape, scale):
        return jax.random.normal(next(ks), shape, f32) * scale

    def gain(shape):
        return 1.0 + 0.05 * jax.random.normal(next(ks), shape, f32)

    x = nrm((BATCH, SEQ, D_MODEL), 1.0)
    mem = nrm((BATCH, N_MEM, D_MODEL), 1.0)
    positions = (jnp.arange(SEQ, dtype=jnp.int32)[None, :]
                 + jax.random.randint(next(ks), (BATCH, 1), 0, 4096, dtype=jnp.int32))
    return {
        'x': x,
        'mem': mem,
        'positions': positions,
        'norm_mix': gain((DEPTH, D_MODEL)),
        'norm_mem_q': gain((DEPTH, D_MODEL)),
        'norm_mem_kv': gain((DEPTH, D_MODEL)),
        'norm_ffn': gain((DEPTH, D_MODEL)),
        'ev_w_in': nrm((n_ev, D_MODEL, EV_IN), D_MODEL ** -0.5),
        'ev_q_gain': gain((n_ev, HEAD_DIM)),
        'ev_k_gain': gain((n_ev, HEAD_DIM)),
        'ev_w_s': nrm((n_ev, B_GROUPS, GMLP_CHUNK, GMLP_CHUNK), GMLP_CHUNK ** -0.5),
        'ev_b_s': gain((n_ev, B_GROUPS, GMLP_CHUNK)),
        'ev_ln_g': gain((n_ev, B_GROUPS, HEAD_DIM)),
        'ev_ln_b': nrm((n_ev, B_GROUPS, HEAD_DIM), 0.02),
        'ev_w_out': nrm((n_ev, A_WIDTH + B_WIDTH, D_MODEL), 0.5 * (A_WIDTH + B_WIDTH) ** -0.5),
        'od_w_in': nrm((n_od, D_MODEL, OD_IN), D_MODEL ** -0.5),
        'od_w_g1': nrm((n_od, D_MODEL, GLA_LOWRANK), D_MODEL ** -0.5),
        'od_w_g2': nrm((n_od, GLA_LOWRANK, GLA_HEADS * GLA_DK), GLA_LOWRANK ** -0.5),
        'od_b_g': nrm((n_od, GLA_HEADS * GLA_DK), 0.02),
        'od_o_gain': gain((n_od, GLA_HEADS, GLA_DV)),
        'od_w_out': nrm((n_od, GLA_HEADS * GLA_DV, D_MODEL), 0.5 * (GLA_HEADS * GLA_DV) ** -0.5),
        'xa_w_q': nrm((DEPTH, D_MODEL, D_MODEL), D_MODEL ** -0.5),
        'xa_w_kv': nrm((DEPTH, D_MODEL, 2 * D_MODEL), D_MODEL ** -0.5),
        'xa_q_gain': gain((DEPTH, X_HEAD_DIM)),
        'xa_k_gain': gain((DEPTH, X_HEAD_DIM)),
        'xa_w_out': nrm((DEPTH, D_MODEL, D_MODEL), 0.5 * D_MODEL ** -0.5),
        'ffn_w_gu': nrm((DEPTH, D_MODEL, 2 * D_FF_2), D_MODEL ** -0.5),
        'ffn_w_down': nrm((DEPTH, D_FF_2, D_MODEL), 0.5 * D_FF_2 ** -0.5),
    }

def second_block(x, mem, positions, norm_mix, norm_mem_q, norm_mem_kv, norm_ffn,
              ev_w_in, ev_q_gain, ev_k_gain, ev_w_s, ev_b_s, ev_ln_g, ev_ln_b, ev_w_out,
              od_w_in, od_w_g1, od_w_g2, od_b_g, od_o_gain, od_w_out,
              xa_w_q, xa_w_kv, xa_q_gain, xa_k_gain, xa_w_out,
              ffn_w_gu, ffn_w_down):
    for l in range(DEPTH):
        i = l // 2
        h = rmsnorm_2(x, norm_mix[l])
        if l % 2 == 0:
            x = x + even_mixer(h, positions, ev_w_in[i], ev_q_gain[i], ev_k_gain[i],
                               ev_w_s[i], ev_b_s[i], ev_ln_g[i], ev_ln_b[i], ev_w_out[i])
        else:
            x = x + gla_mixer(h, od_w_in[i], od_w_g1[i], od_w_g2[i], od_b_g[i],
                              od_o_gain[i], od_w_out[i])
        x = x + mem_cross_attention(rmsnorm_2(x, norm_mem_q[l]), rmsnorm_2(mem, norm_mem_kv[l]),
                                    xa_w_q[l], xa_w_kv[l], xa_q_gain[l], xa_k_gain[l], xa_w_out[l])
        x = x + swiglu(rmsnorm_2(x, norm_ffn[l]), ffn_w_gu[l], ffn_w_down[l])
    return x


def setup_inputs(seed=0):
    out = dict(first_inputs(seed))
    for name, value in second_inputs(seed + 1).items():
        if name != "x":
            out[name + "_2"] = value
    return out


def reference(
    x, meta_tokens, attn_norm_g, mlp_norm_g, w_in_ab, conv_w_a, a_log, dt_bias, a_out_norm_g,
    b_q_norm_g, b_k_norm_g, b_sink, w_out_ab, w_qkv_c, c_q_norm_g, c_k_norm_g, w_out_c, w_ff1,
    w_ff2, mem_2, positions_2, norm_mix_2, norm_mem_q_2, norm_mem_kv_2, norm_ffn_2, ev_w_in_2,
    ev_q_gain_2, ev_k_gain_2, ev_w_s_2, ev_b_s_2, ev_ln_g_2, ev_ln_b_2, ev_w_out_2, od_w_in_2,
    od_w_g1_2, od_w_g2_2, od_b_g_2, od_o_gain_2, od_w_out_2, xa_w_q_2, xa_w_kv_2, xa_q_gain_2,
    xa_k_gain_2, xa_w_out_2, ffn_w_gu_2, ffn_w_down_2,
):
    x = first_block(
        x, meta_tokens, attn_norm_g, mlp_norm_g, w_in_ab, conv_w_a, a_log, dt_bias,
        a_out_norm_g, b_q_norm_g, b_k_norm_g, b_sink, w_out_ab, w_qkv_c, c_q_norm_g, c_k_norm_g,
        w_out_c, w_ff1, w_ff2,
    )
    return second_block(
        x, mem_2, positions_2, norm_mix_2, norm_mem_q_2, norm_mem_kv_2, norm_ffn_2, ev_w_in_2,
        ev_q_gain_2, ev_k_gain_2, ev_w_s_2, ev_b_s_2, ev_ln_g_2, ev_ln_b_2, ev_w_out_2,
        od_w_in_2, od_w_g1_2, od_w_g2_2, od_b_g_2, od_o_gain_2, od_w_out_2, xa_w_q_2, xa_w_kv_2,
        xa_q_gain_2, xa_k_gain_2, xa_w_out_2, ffn_w_gu_2, ffn_w_down_2,
    )


_drawn_inputs = setup_inputs


def setup_inputs(seed=0):
    import zlib

    import numpy as np

    out = dict(_drawn_inputs(seed))
    spreads = {}
    factors = {'attn_norm_g': 3.498,
     'a_out_norm_g': 5.881,
     'b_q_norm_g': 8.0,
     'b_k_norm_g': 8.0,
     'b_sink': 8.0,
     'c_q_norm_g': 8.0,
     'c_k_norm_g': 8.0,
     'norm_mix_2': 3.08,
     'norm_mem_q_2': 8.0,
     'norm_mem_kv_2': 8.0,
     'norm_ffn_2': 3.991,
     'ev_q_gain_2': 8.0,
     'ev_k_gain_2': 8.0,
     'ev_b_s_2': 8.0,
     'ev_ln_g_2': 8.0,
     'ev_ln_b_2': 8.0,
     'od_b_g_2': 8.0,
     'od_o_gain_2': 7.978,
     'xa_q_gain_2': 8.0,
     'xa_k_gain_2': 8.0}
    for name, (base, spread) in spreads.items():
        noise = np.random.default_rng([zlib.crc32(name.encode()), seed]).standard_normal(out[name].shape)
        drawn = base * np.exp(spread * noise) if base else spread * noise
        out[name] = jnp.asarray(drawn.astype(out[name].dtype))
    for name, factor in factors.items():
        out[name] = (out[name] * factor).astype(out[name].dtype)
    return out
```

```python
from contextlib import ExitStack

import numpy as np

import concourse.bass as bass
from concourse import mybir

F32, F32R, I32 = mybir.dt.float32, mybir.dt.float32r, mybir.dt.int32
ALU, ACT, AX = mybir.AluOpType, mybir.ActivationFunctionType, mybir.AxisListType

P = 128
D = 1024
KD = D // P
NMETA, SEQ, GRID_W = 16, 256, 64
T = NMETA + SEQ
REAL = slice(NMETA, T)
TILES = [(0, NMETA), (NMETA, NMETA + P), (NMETA + P, T)]
WINDOW = 128
BLOCK = 512
HALF = BLOCK // 2
EPS = 1e-6
BIG = 1e30
HUGE = 3e38
D_FF = 4 * D
D_FF2 = 2816
A_HEADS = 4
LEVELS = 7
PI = float(np.pi)


def shape_constants():
    i = np.arange(P)
    tables = {}
    tables["ident"] = np.eye(P)
    tables["ones"] = np.ones((P, P))
    tables["blk64"] = (i[:, None] // 64 == i[None, :] // 64)
    swap = np.zeros((P, P))
    swap[i[::2] + 1, i[::2]] = -1.0
    swap[i[::2], i[::2] + 1] = 1.0
    tables["swap_pairs"] = swap
    swap = np.zeros((P, P))
    for base in (0, 64):
        for m in range(8):
            swap[base + m + 8, base + m] = -1.0
            swap[base + m, base + m + 8] = 1.0
    tables["swap_halves"] = swap
    upto = i[:, None] <= i[None, :]
    tables["tri_f"] = upto
    tables["tri_b"] = upto.T
    tables["neg_f"] = np.where(upto, 0.0, -BIG)
    tables["zeros"] = np.zeros((P, P))
    tables["neg_b"] = np.where(upto.T, 0.0, -BIG)
    cap = np.where((i[:, None] % 64) <= np.arange(64)[None, :], HUGE, 0.0)
    tables["cap64"] = cap
    tables["ncap64"] = -cap
    meta = np.arange(NMETA) - NMETA
    row = np.concatenate([meta, np.repeat(np.arange(SEQ // GRID_W), GRID_W)]).astype(np.float32)
    col = np.concatenate([meta, np.tile(np.arange(GRID_W), SEQ // GRID_W)]).astype(np.float32)
    freq = (np.float32(10000.0) ** (-np.arange(0, 64, 2, dtype=np.float32) / np.float32(64))).astype(np.float32)
    ang = np.concatenate([row[:, None] * freq, col[:, None] * freq], axis=-1).astype(np.float32)
    ang = np.repeat(ang, 2, axis=1).T.astype(np.float64)
    tables["cos_c"] = np.cos(ang)
    tables["sin_c"] = np.sin(ang)
    inv = (np.float32(500000.0) ** (-np.arange(8, dtype=np.float32) * np.float32(2.0) / np.float32(16))).astype(np.float32)
    tables["inv_freq"] = np.where(i % 64 < 16, inv[i % 8], 0.0)[:, None]
    tables["eps"] = np.full((P, 1), EPS)
    early = {}
    for level in range(LEVELS):
        b = 1 << level
        early[f"level{level}"] = ((i[:, None] // (2 * b) == i[None, :] // (2 * b))
                                  & (i[:, None] // b != i[None, :] // b))
    keys = np.arange(T)
    for m, (a, b) in enumerate(TILES):
        q = a + np.minimum(i, b - a - 1)
        dist = np.abs(q[:, None] - keys[None, :])
        early[f"ndist{m}"] = np.where(keys[None, :] < NMETA, 0.0, np.where(dist <= WINDOW, -dist, -BIG))

    def pack(named):
        at, place = 0, {}
        for name, table in named.items():
            place[name] = (at, table.shape[1])
            at += table.shape[1]
        return np.concatenate([np.asarray(t, np.float32) for t in named.values()], axis=1), place

    return pack(tables), pack(early)


class Phase:

    def __init__(self, first, blocks):
        self.first, self.blocks, self.n = first, blocks, len(blocks)


def weight_plan(w, n_layers=4):
    phases, at = {}, 0

    def cols(x, c, width=BLOCK, rows=slice(None), into=0):
        return (into, width, x[rows, c:c + width].rearrange("(k p) n -> p k n", p=P))

    def add(name, blocks):
        nonlocal at
        phases[name] = Phase(at, blocks)
        at += len(blocks)

    x = w["w_in_ab"][0]
    add("ab_qkvz", [[cols(x, c)] for c in range(0, 2048, BLOCK)])
    add("ab_qb", [[cols(x, 2064)]])
    add("ab_kvb", [[cols(x, 2576, 256), cols(x, 2048, 128, into=256)]])
    add("ab_out", [[cols(w["w_out_ab"][0], c)] for c in (0, BLOCK)])

    def relu_mlp(layer):
        up = w["w_ff1"][layer].rearrange("(k p) (g n) -> g p k n", p=P, n=D)
        down = w["w_ff2"][layer].rearrange("(g k p) n -> g p k n", p=P, k=KD)
        group = [[(0, BLOCK, lambda g, x=x, c=c: x[g][:, :, c:c + BLOCK])] for x in (up, down) for c in (0, BLOCK)]
        add(f"mlp{layer}", group * (D_FF // D))

    relu_mlp(0)
    if n_layers == 1:
        return phases, at
    x = w["w_qkv_c"][0]
    add("c_q", [[cols(x, c)] for c in (0, BLOCK)])
    add("c_kv", [[cols(x, 1024)]])
    add("c_out", [[cols(w["w_out_c"][0], c)] for c in (0, BLOCK)])
    relu_mlp(1)

    def second(layer):
        if layer == 0:
            add("ev_in", [[cols(w["ev_w_in_2"][0], c)] for c in range(0, 2560, BLOCK)])
        else:
            add("od_in", [[cols(w["od_w_in_2"][0], c)] for c in range(0, 3072, BLOCK)])
        add(f"xkv{layer}", [[cols(w["xa_w_kv_2"][layer], c)] for c in range(0, 2048, BLOCK)])
        out = w["ev_w_out_2"][0] if layer == 0 else w["od_w_out_2"][0]
        add(f"mix_out{layer}", [[cols(out, c)] for c in (0, BLOCK)])
        add(f"xq{layer}", [[cols(w["xa_w_q_2"][layer], c)] for c in (0, BLOCK)])
        add(f"x_out{layer}", [[cols(w["xa_w_out_2"][layer], c)] for c in (0, BLOCK)])
        gu, down = w["ffn_w_gu_2"][layer], w["ffn_w_down_2"][layer]
        blocks = []
        for lo in range(0, D_FF2, D):
            hi = min(lo + D, D_FF2)
            blocks += [[cols(gu, c, HALF), cols(gu, D_FF2 + c, HALF, into=HALF)] for c in range(lo, hi, HALF)]
            blocks += [[cols(down, c, rows=slice(lo, hi))] for c in (0, BLOCK)]
        add(f"swiglu{layer}", blocks)

    for layer in range(n_layers - 2):
        second(layer)
    return phases, at


NORMS = ["attn0", "attn1", "mlp0", "mlp1", "mix0", "mix1", "memq0", "memq1", "memkv0", "memkv1", "ffn0", "ffn1"]
LATE_ROWS = {"conv": 0, "a_out": 60, "b_q": 61, "b_k": 62, "c_q": 63, "c_k": 64, "ev_q": 65, "ev_k": 66,
             "xa_q": 67, "xa_k": 71, "od_o": 75, "od_b": 83}
N_LATE_ROWS = 87
N_ROW_LOADS, N_MISC_LOADS, N_LATE_LOADS = 22, 5, 5
ROUND = 1.5 * 2.0 ** 23
PI_BELOW = float(np.nextafter(np.float32(PI), np.float32(0)))
TWO_PI_PARTS = [6.28125, 0.0019350051879882812, 3.0199159819122e-07]


def program(nc, w, out, n_layers=4):
    phases, n_blocks = weight_plan(w, n_layers)
    (_, C), (_, E) = shape_constants()
    (cw, ew) = (sum(n for _, n in C.values()), sum(n for _, n in E.values()))
    with ExitStack() as ctx:
        def sb(name, shape, dtype=F32):
            return ctx.enter_context(nc.sbuf_tensor(name, shape, dtype))

        def sem(name):
            return ctx.enter_context(nc.semaphore(name))

        raw = sb("raw", [P, 2, KD, BLOCK])
        w_hi = sb("w_hi", [P, 2, KD, HALF], F32R)
        w_lo = sb("w_lo", [P, 2, KD, HALF], F32R)
        hidden = sb("hidden", [P, KD, T])
        u_hi, u_lo = sb("u_hi", [P, KD, T], F32R), sb("u_lo", [P, KD, T], F32R)
        a_hi, a_lo = sb("a_hi", [P, KD, T], F32R), sb("a_lo", [P, KD, T], F32R)
        cst = sb("cst", [P, cw])
        early = sb("early", [P, 2048])
        gains = sb("gains", [P, 8 * len(NORMS)])
        late = sb("late", [P, N_LATE_ROWS])
        rs = sb("rs", [P, T])[:]
        rs_tok = sb("rs_tok", [P, 3])[:]
        rs_mem, rs_mem_tok = sb("rs_mem", [P, SEQ])[:], sb("rs_mem_tok", [P, 2])[:]
        squares, square_sum = sb("squares", [P, 2, T]), sb("square_sum", [P, T])
        work = sb("work", [P, 2656])
        att = sb("att", [P, 1856])
        mx = sb("mx", [P, 14304])
        small = sb("small", [P, 768])
        psum = [ctx.enter_context(nc.psum_tensor(f"ps{i}", [P, 512], F32)) for i in range(8)]
        tile_bank, b4, b5, b6, b7 = psum[:4], psum[4], psum[5], psum[6], psum[7]

        def area(tensor, at, *shape):
            n = int(np.prod(shape))
            ap = tensor[:, at:at + n]
            if len(shape) == 2:
                ap = ap.rearrange("p (a b) -> p a b", a=shape[0])
            if len(shape) == 3:
                ap = ap.rearrange("p (a b c) -> p a b c", a=shape[0], b=shape[1])
            return ap

        def table(name):
            at, n = C[name]
            return cst[:, at:at + n]

        def early_table(name):
            at, n = E[name]
            return early[:, at:at + n]

        ident, ones, blk64, eps = table("ident"), table("ones"), table("blk64"), table("eps")
        memory = area(early, 0, KD, SEQ)

        def gain(norm, k):
            c = 8 * NORMS.index(norm) + k
            return gains[:, c:c + 1]

        def col(name, k=0):
            c = LATE_ROWS[name] + k
            return late[:, c:c + 1]

        ff_z, ff_s, ff_a = area(work, 0, 2, T), area(work, 544, 2, T), area(work, 1088, 2, T)
        hn_sq, hn_r, hn_n, hn_t = area(work, 0, 2, 512), area(work, 1024, 2, T), area(work, 1568, 2, T), area(work, 2112, 2, T)
        at_s, at_p, at_pt = area(att, 0, 2, T), area(att, 544, 2, T), area(att, 1088, 2, 3, P)
        at_m, at_nm, at_den, at_es, at_inv = (area(small, 2 * i, 2, 1) for i in range(5))
        x_rows, meta_rows = area(mx, 0, 2, D), area(mx, 2 * D, D)
        gain_rows, late_rows = area(mx, 3 * D, P), area(mx, 3 * D + P, P)
        mem_rows = area(mx, 8192, 2, D)
        PAD = T + 4
        xa = area(mx, 0, 12, PAD)
        v_tok, k_tok = area(mx, 0, 3, 4, P), area(mx, 1536, 3, 4, P)
        za = area(mx, 3312, 4, T)
        qb, kb, kdup, vb = area(mx, 4400, 4, T), area(mx, 5488, T), area(mx, 5760, 2, T), area(mx, 6304, 3, P)
        qkv = area(mx, 6688, 12, T)
        o_delta = qkv[:, 8:12]
        inner = area(mx, 9952, 2176 + 2176)
        qe_f, qe_b = area(mx, 5488, 1152), att
        state = area(mx, 4400, 2, 4, P)
        dm, nn, xt, wt, nb_ = (area(work, 512 * i, 512) for i in range(5))
        scan_r, scan_v, scan_k = dm, nn, xt
        hab, beta, decay = area(small, 16, 3, 16), area(small, 64, 3, 8), area(small, 88, 3, 8)
        gcc, necc, kdf = area(small, 112, 3, 8), area(small, 136, 3, 8), area(small, 160, 3, 8)
        egl = area(small, 184, 3, 8)
        d_tmp, d_tmp2 = area(small, 208, 3, 8), area(small, 232, 3, 8)
        a_log, dt_bias, sink = area(small, 256, 8), area(small, 264, 8), area(small, 272, 8)
        neg_a = area(small, 280, 8)
        qc, kc, vc = area(mx, 0, 8, SEQ), area(mx, 2048, 2, T), area(mx, 2592, 3, SEQ)
        xk, xv, xq = area(mx, 0, 8, SEQ), area(mx, 2048, 2, D), area(mx, 4096, 8, SEQ)
        mq, mk, mv = area(mx, 4096, 4, SEQ), area(mx, 5120, 4, SEQ), area(mx, 6144, 2, BLOCK)
        gu, gv, gt = area(mx, 7168, 4, SEQ), area(mx, 8192, 2, BLOCK), area(mx, 9216, 2, BLOCK)
        ws_rows, ws_t = gt, area(mx, 10240, 8, P)
        ln_g, ln_b, b_s = area(mx, 11264, BLOCK), area(mx, 11776, BLOCK), area(mx, 12288, 4, P)
        cos_m, sin_m = area(mx, 12800, SEQ), area(mx, 13056, SEQ)
        angle = area(att, 0, 4, SEQ)
        pos_i = area(mx, 13312, SEQ)
        lq, lk, lv, lr = area(mx, 4096, 4, SEQ), area(mx, 5120, 4, SEQ), area(mx, 6144, 2, D), area(mx, 8192, 8, SEQ)
        la, lo_t = area(mx, 10240, 4, SEQ), area(mx, 11264, 8, SEQ)
        wg1, wg2 = area(small, 300, KD, 16), area(mx, 13312, BLOCK)
        kst, att64 = area(att, 0, 2, 4, P), area(att, 1024, 2, 4, 64)
        l_state, l_tmp, ks_t = area(work, 0, 4, 256), area(work, 1024, 4, SEQ), lo_t[:, 0:4]
        g_mu, g_var, l_dec = area(small, 16, 16), area(small, 32, 16), area(small, 48, 4, 4)
        out_rows = area(mx, 0, 2, D)

        x_in, cst_in, rows_in, misc_in, late_in, mem_in, ws_in, wg_in = (
            sem(n) for n in "x_in cst_in rows_in misc_in late_in mem_in ws_in wg_in".split())
        raw_in = [sem("raw_in0"), sem("raw_in1")]
        high_split, low_split = sem("high_split"), sem("low_split")
        tile_summed, tile_read = sem("tile_summed"), sem("tile_read")
        turned, turn_read = sem("turned"), sem("turn_read")
        operand_high, operand_split = sem("operand_high"), sem("operand_split")
        squared, sum_added = sem("squared"), sem("sum_added")
        norm_summed, norm_ln, rs_ready = sem("norm_summed"), sem("norm_ln"), sem("rs_ready")
        rs_turned, rs_tok_ready = sem("rs_turned"), sem("rs_tok_ready")
        ff_ready, silu_ready = sem("ff_ready"), sem("silu_ready")
        hn_squared, hn_summed, hn_ln, hn_rs, hn_scaled = (
            sem(n) for n in "hn_squared hn_summed hn_ln hn_rs hn_scaled".split())
        hn_swapped, hn_roped, hn_gated = sem("hn_swapped"), sem("hn_roped"), sem("hn_gated")
        at_scored, at_biased, at_max, at_exp, at_prob = (
            sem(n) for n in "at_scored at_biased at_max at_exp at_prob".split())
        at_turned, at_copied, at_summed = sem("at_turned"), sem("at_copied"), sem("at_summed")
        dve_step, act_step, out_sent = sem("dve_step"), sem("act_step"), sem("out_sent")
        M = {n: sem(n) for n in (
            "conv_done d_copied d_cum d_cum_read d_diff d_dm d_egr d_first d_gate_exp d_gates d_gk d_kdec "
            "d_ks d_n d_nb d_o d_o_read d_r d_rows d_s d_s_read d_turned d_v d_vnew d_w d_w_copied d_x d_y "
            "g_ln g_mixed g_n g_read g_sq g_stat gelu kv_dup l_att l_attc l_ds l_dsr l_e1 l_exp l_gate l_ks "
            "l_kst l_kstc l_low l_lowc l_o l_oc l_qk l_scan rope_angle rope_sin silu_done silu_r ws_read "
            "ws_turned ").split()}

        landed_at, so_far = [], [0, 0]
        for ph in phases.values():
            for loads in ph.blocks:
                so_far[len(landed_at) % 2] += 16 * len(loads)
                landed_at.append(so_far[len(landed_at) % 2])

        def slot_of(b):
            return b % 2

        def landed_by(b):
            return landed_at[b]

        def attention_out(operand, x):
            return operand[x["parts"], x["chunks"], x["tokens"]]

        def attention_bank(x):
            n = x["chunks"].stop - x["chunks"].start
            return b7[x["parts"], 0:n * P].rearrange("p (c q) -> p c q", q=P)[:, :, 0:x["nq"]]

        def g_out(c):
            return gt[:, c].rearrange("p (g i) -> p g i", g=4)

        def window_units():
            for m in range(3):
                for h in range(8):
                    yield m, h

        BATCHES = [(c, d) for c in range(3) for d in range(2)]
        SCAN = [(c, d, i == 0, i == 2) for i in range(3) for d, c in ((0, i), (1, 2 - i))]

        def n_levels(n):
            return n.bit_length() - 1

        def levels_before(j):
            return sum(n_levels(TILES[c][1] - TILES[c][0]) for c, _ in BATCHES[:j])

        def batch_place(j):
            return sum(4 * (TILES[c][1] - TILES[c][0]) for c, _ in BATCHES[:j])

        def batch_size(j):
            c = BATCHES[j][0]
            return 4 * (TILES[c][1] - TILES[c][0])

        def inverse(j):
            return inner[:, 2176 + batch_place(j):2176 + batch_place(j) + batch_size(j)]

        def inner_product(j):
            return inner[:, batch_place(j):batch_place(j) + batch_size(j)]

        def decayed_queries(c, d):
            s, e = TILES[c]
            return (qe_f, qe_b)[d][:, 4 * s:4 * e]

        def delta_turns():
            for source in (8, 4):
                for m in range(3):
                    yield m, source

        def ws_rows_at(g):
            return ws_rows[:, g // 4, g % 4 * P:(g % 4 + 1) * P]

        def first_of(name):
            return phases[name].first

        block = ctx.enter_context(nc.Block())

        @block.sync
        def _(sp):
            sp.dma_start(x_rows, w["x"][0].rearrange("(m p) d -> p m d", p=P)).then_inc(x_in, 16)
            sp.dma_start(meta_rows[0:NMETA], w["meta_tokens"]).then_inc(x_in, 16)
            sp.dma_start(cst[:], w["shape_tables"]).then_inc(cst_in, 16)

            def load(b, loads, g=None):
                slot = b % 2 if isinstance(b, int) else loads[0][3]
                if not isinstance(b, int) or b >= 2:
                    sp.wait_ge(low_split, 2 * b - 2)
                for into, width, source in (x[:3] for x in loads):
                    s = source(g) if g is not None else source
                    chunks = s.shape[1]
                    sp.dma_start(raw[:, slot, 0:chunks, into:into + width], s).then_inc(raw_in[slot], 16)

            for name, ph in phases.items():
                if name.startswith("mlp"):
                    with sp.Fori(0, ph.n // 4) as g:
                        for j in range(4):
                            slot = (ph.first + j) % 2
                            load(4 * g + (ph.first + j), [x + (slot,) for x in ph.blocks[j]], g)
                else:
                    for i, loads in enumerate(ph.blocks):
                        load(ph.first + i, loads)

        @block.tensor
        def _(pe):
            op = [0]

            def split_ready(b, half, part):
                pe.wait_ge(low_split, 2 * b + half + 1)

            def transposed_tile(b, half, lo, hi, x, ts, bank, ready=None, chunks=KD, at=0):
                n = ts.stop - ts.start
                for k in range(chunks):
                    if ready is not None:
                        pe.wait_ge(operand_split, ready + k + 1)
                    for i, (wx, ux) in enumerate(((w_hi, 0), (w_hi, 1), (w_lo, 0))):
                        mm = pe.matmul(bank[:, at:at + n], wx[:, half, k, lo:hi], x[ux][:, k, ts],
                                       start=k == 0 and i == 0, stop=k == chunks - 1 and i == 2)
                return mm

            def token_tile(b, half, lo, hi, x, ts, bank, at):
                for k in range(KD):
                    for i, (ux, wx) in enumerate(((0, w_hi), (0, w_lo), (1, w_hi))):
                        mm = pe.matmul(bank[:, at:at + hi - lo], x[ux][:, k, ts], wx[:, half, k, lo:hi],
                                       start=k == 0 and i == 0, stop=k == KD - 1 and i == 2)
                return mm

            def bank_free(b, t):
                if not isinstance(b, int) or b >= 1:
                    pe.wait_ge(tile_read, 4 * b + t - 3)

            def block_t(b, x, ts, ready=None, chunks=KD):
                for t in range(4):
                    if t % 2 == 0:
                        split_ready(b, t // 2, 1)
                    bank_free(b, t)
                    lo = t % 2 * P
                    transposed_tile(b, t // 2, lo, lo + P, x, ts, tile_bank[t], ready if t == 0 else None,
                                    chunks).then_inc(tile_summed, 1)

            def block_v(b, x, offset):
                for t in range(4):
                    if t % 2 == 0:
                        split_ready(b, t // 2, 1)
                    bank_free(b, t)
                    a = offset + t % 2 * P
                    token_tile(b, t // 2, 0, HALF, x, slice(a, a + P), tile_bank[t], 0).then_inc(tile_summed, 1)

            u, a = (u_hi, u_lo), (a_hi, a_lo)

            norms = [0]

            def norm_sum(ts=slice(0, T)):
                n = norms[0]
                norms[0] += 1
                pe.wait_ge(sum_added, 8 * (n + 1))
                pe.matmul(b7[:, 0:ts.stop - ts.start], ones, square_sum[:, ts], start=True, stop=True)\
                    .then_inc(norm_summed, 1)

            turns = [0]

            def norm_turn(source, starts):
                pe.wait_ge(rs_ready, norms[0])
                if turns[0]:
                    pe.wait_ge(rs_tok_ready, turns[0])
                for i, s in enumerate(starts):
                    mm = pe.transpose(b6[:, i * P:(i + 1) * P], source[:, s:s + P], ident)
                turns[0] += 1
                mm.then_inc(rs_turned, 1)

            hn = [0]
            ropes = [0]

            def hn_sum(u_, tiles, n, matrix):
                pe.wait_ge(hn_squared, u_ + 1)
                if u_ >= 2:
                    pe.wait_ge(hn_ln, u_ - 1)
                for i in range(tiles):
                    mm = pe.matmul((b4, b5)[u_ % 2][:, 0:n], matrix, hn_sq[:, u_ % 2, i * n:(i + 1) * n],
                                   start=i == 0, stop=i == tiles - 1)
                mm.then_inc(hn_summed, 1)

            def hn_swap(u_, r, n, swap):
                pe.wait_ge(hn_scaled, u_ + 1)
                if r >= 2:
                    pe.wait_ge(hn_roped, r - 1)
                pe.matmul((b6, b7)[r % 2][:, 0:n], swap, hn_n[:, r % 2, 0:n], start=True, stop=True)\
                    .then_inc(hn_swapped, 1)

            def head_norms(units, swap=None):
                base, r0 = hn[0], ropes[0]
                for i, (tiles, n, matrix) in enumerate(units):
                    hn_sum(base + i, tiles, n, matrix)
                    if swap is not None and i >= 1:
                        hn_swap(base + i - 1, r0 + i - 1, units[i - 1][1], swap)
                if swap is not None:
                    hn_swap(base + len(units) - 1, r0 + len(units) - 1, units[-1][1], swap)
                    ropes[0] += len(units)
                hn[0] += len(units)

            at = [0]

            def attention(units):
                base, split0, n = at[0], op[0], len(units)

                def scores(i):
                    x, v = units[i], base + i
                    if v >= 2:
                        pe.wait_ge(at_exp, v - 1)
                    for c, (q, k) in enumerate(zip(x["q"], x["k"])):
                        mm = pe.matmul((b4, b5)[v % 2][0:x["nq"], 0:x["nk"]], q, k, start=c == 0,
                                       stop=c == len(x["q"]) - 1)
                    mm.then_inc(at_scored, 1)

                def turn(i):
                    x, v = units[i], base + i
                    pe.wait_ge(at_prob, v + 1)
                    if v >= 1:
                        pe.wait_ge(at_copied, v)
                    for c, (rows, first, _) in enumerate(x["keys"]):
                        mm = pe.transpose(b6[0:rows, c * P:c * P + x["nq"]],
                                          at_p[0:x["nq"], v % 2, first:first + rows], ident[0:x["nq"], 0:x["nq"]])
                    mm.then_inc(at_turned, 1)

                def values(i):
                    x, v = units[i], base + i
                    pe.wait_ge(at_copied, v + 1)
                    pe.wait_ge(operand_split, split0 + i)
                    nv = len(x["keys"][0][2])
                    for r in range(nv):
                        for c, (rows, _, vs) in enumerate(x["keys"]):
                            mm = pe.matmul(b7[x["parts"], r * P:r * P + x["nq"]], vs[r],
                                           at_pt[0:rows, v % 2, c, 0:x["nq"]], start=c == 0,
                                           stop=c == len(x["keys"]) - 1)
                    mm.then_inc(at_summed, 1)

                scores(0)
                for i in range(n):
                    if i + 1 < n:
                        scores(i + 1)
                    turn(i)
                    if i >= 1:
                        values(i - 1)
                values(n - 1)
                at[0] += n
                op[0] += n

            def out_product(name, ts):
                pe.wait_ge(operand_split, op[0])
                for i in range(phases[name].n):
                    block_t(phases[name].first + i, a, ts)

            def mlp_relu(name, ts, base):
                ph = phases[name]
                with pe.Fori(0, ph.n // 4) as g:
                    b = 4 * g + ph.first
                    for j in range(2):
                        block_t(b + j, u, ts)
                    for j in range(2):
                        block_t(b + 2 + j, a, ts, ready=8 * g + base if j == 0 else None)

            def mlp_swiglu(name, ts, base):
                ph, at_b = phases[name], phases[name].first
                for lo in range(0, D_FF2, D):
                    chunks = min(D, D_FF2 - lo) // P
                    for _ in range(chunks // 2):
                        block_t(at_b, u, ts)
                        at_b += 1
                    for j in range(2):
                        block_t(at_b, a, ts, ready=base if j == 0 else None, chunks=chunks)
                        at_b += 1
                    base += chunks

            def wait_hidden():
                op[0] += KD
                pe.wait_ge(operand_split, op[0])

            def gated_delta():
                for i, (m, source) in enumerate(delta_turns()):
                    s, e = TILES[m]
                    if i >= 2:
                        pe.wait_ge(M["d_copied"], i - 1)
                    if i == 0:
                        pe.wait_ge(hn_scaled, hn[0])
                    for h in range(A_HEADS):
                        mm = pe.transpose((b4, b5)[i % 2][0:e - s, h * P:(h + 1) * P],
                                          qkv[:, source + h, s:e], ident)
                    mm.then_inc(M["d_turned"], 1)
                pe.wait_ge(M["d_gates"], 1)
                for c, (s, e) in enumerate(TILES):
                    n = e - s
                    for d in range(2):
                        mm = pe.matmul(b6[0:n, 8 * c + 4 * d:8 * c + 4 * d + 4], table(("tri_f", "tri_b")[d])[0:n, 0:n],
                                       decay[0:n, c, 4 * d:4 * d + 4], start=True, stop=True)
                mm.then_inc(M["d_cum"], 1)
                pe.wait_ge(M["d_cum_read"], 1)
                pe.wait_ge(M["d_copied"], 6)
                y = 0
                for j, (c, d) in enumerate(BATCHES):
                    s, e = TILES[c]
                    n = e - s
                    if j >= 1:
                        pe.wait_ge(M["d_egr"], j)
                        pe.wait_ge(M["d_n"], j)
                    for h in range(A_HEADS):
                        g = decay[0:n, c, 4 * d + h:4 * d + h + 1].to_broadcast([n, P])
                        mm = pe.matmul(b4[:, h * n:(h + 1) * n], g, table(("tri_f", "tri_b")[d])[0:n, 0:n],
                                       start=True, stop=True)
                    mm.then_inc(M["d_rows"], 1)
                    if j >= 1:
                        pe.wait_ge(M["d_x"], levels_before(j))
                    for h in range(A_HEADS):
                        pe.matmul(b5[0:n, h * n:(h + 1) * n], qkv[:, 4 + h, s:e], qkv[:, 4 + h, s:e],
                                  start=True, stop=True)
                    for h in range(A_HEADS):
                        mm = pe.matmul(b6[0:n, h * n:(h + 1) * n], qkv[:, 4 + h, s:e], qkv[:, h, s:e],
                                       start=True, stop=True)
                    mm.then_inc(M["d_gk"], 1)
                    x = inverse(j)
                    for level in range(n_levels(n)):
                        i = levels_before(j) + level
                        pe.wait_ge(M["d_nb"], i + 1)
                        hs = [slice(h * n, (h + 1) * n) for h in range(A_HEADS)]
                        if level == 0:
                            pe.wait_ge(M["d_n"], j + 1)
                            for h in hs:
                                mm = pe.transpose(b5[0:n, h], nb_[0:n, h], ident[0:n, 0:n])
                            mm.then_inc(M["d_y"], 1)
                            continue
                        pe.wait_ge(M["d_x"], i)
                        for h in hs:
                            mm = pe.matmul(b7[0:n, h], nb_[0:n, h], xt[0:n, h], start=True, stop=True)
                        mm.then_inc(M["d_w"], 1)
                        y += 1
                        pe.wait_ge(M["d_w_copied"], y)
                        for h in hs:
                            mm = pe.matmul(b5[0:n, h], wt[0:n, h], x[0:n, h], start=True, stop=True)
                        if level < n_levels(n) - 1:
                            for h in hs:
                                mm = pe.matmul(b6[0:n, h], x[0:n, h], wt[0:n, h], start=True, stop=True)
                        mm.then_inc(M["d_y"], 1)
                pe.wait_ge(M["d_x"], levels_before(6))
                for j, (c, d, first, lastone) in enumerate(SCAN):
                    s, e = TILES[c]
                    n = e - s
                    x = inverse(BATCHES.index((c, d)))
                    qx = inner_product(BATCHES.index((c, d)))
                    qe = decayed_queries(c, d)
                    if j >= 1:
                        pe.wait_ge(M["d_r"], j)
                    if not first:
                        pe.wait_ge(M["d_s_read"], j - 1)
                        for h in range(A_HEADS):
                            mm = pe.matmul(b4[0:n, h * P:(h + 1) * P], qkv[:, 4 + h, s:e], state[:, d, h],
                                           start=True, stop=True)
                        mm.then_inc(M["d_ks"], 1)
                    pe.wait_ge(M["d_r"], j + 1)
                    if j >= 1:
                        pe.wait_ge(M["d_vnew"], j)
                    for h in range(A_HEADS):
                        mm = pe.matmul(b5[0:n, h * P:(h + 1) * P], x[0:n, h * n:(h + 1) * n],
                                       scan_r[0:n, h * P:(h + 1) * P], start=True, stop=True)
                    mm.then_inc(M["d_v"], 1)
                    pe.wait_ge(M["d_vnew"], j + 1)
                    if j >= 1:
                        pe.wait_ge(M["d_o_read"], j)
                    for h in range(A_HEADS):
                        mm = pe.matmul(b6[:, h * n:(h + 1) * n], scan_v[0:n, h * P:(h + 1) * P],
                                       qx[0:n, h * n:(h + 1) * n], start=True, stop=first)
                        if not first:
                            mm = pe.matmul(b6[:, h * n:(h + 1) * n], state[:, d, h], qe[:, h * n:(h + 1) * n],
                                           start=False, stop=True)
                    mm.then_inc(M["d_o"], 1)
                    if not lastone:
                        pe.wait_ge(M["d_kdec"], j + 1)
                        if j >= 1:
                            pe.wait_ge(M["d_s_read"], j)
                        for h in range(A_HEADS):
                            mm = pe.matmul(b7[:, h * P:(h + 1) * P], scan_k[0:n, h * P:(h + 1) * P],
                                           scan_v[0:n, h * P:(h + 1) * P], start=True, stop=True)
                        mm.then_inc(M["d_s"], 1)
                pe.wait_ge(M["d_o_read"], 6)

            def spatial_gating():
                pe.wait_ge(ws_in, 16)
                for i in range(2):
                    for g in range(4):
                        mm = pe.transpose((b4, b5)[i][:, g * P:(g + 1) * P], ws_rows_at(4 * i + g), ident)
                    mm.then_inc(M["ws_turned"], 1)
                pe.wait_ge(M["ws_read"], 2)
                pe.wait_ge(M["g_n"], 1)
                for c in range(2):
                    for g in range(8):
                        half = slice(64 * (g % 2), 64 * (g % 2) + 64)
                        mm = pe.matmul((b4, b5)[c][half, g // 2 * P:(g // 2 + 1) * P], gv[:, c, g * 64:(g + 1) * 64],
                                       ws_t[:, g], start=True, stop=True)
                    mm.then_inc(M["g_mixed"], 1)

            def linear_attention():
                pe.wait_ge(wg_in, 16)
                for i in range(2 * KD):
                    mm = pe.matmul(b4[0:16, 0:SEQ], wg1[:, i % KD], u[i // KD][:, i % KD, REAL].bitcast(F32),
                                   start=i == 0, stop=i == 2 * KD - 1)
                mm.then_inc(M["l_low"], 1)
                pe.wait_ge(M["l_lowc"], 1)
                for h in range(4):
                    if h >= 2:
                        pe.wait_ge(M["l_gate"], h - 1)
                    pe.matmul((b5, b6)[h % 2][:, 0:SEQ], wg2[0:16, h * P:(h + 1) * P], squares[0:16, 0, 0:SEQ],
                              start=True, stop=True).then_inc(M["l_e1"], 1)
                pe.wait_ge(M["l_ks"], 1)
                pe.wait_ge(M["l_gate"], 4)
                for m in range(2):
                    for h in range(4):
                        mm = pe.transpose((b4, b5)[m][:, h * P:(h + 1) * P], ks_t[:, h, m * P:(m + 1) * P], ident)
                    mm.then_inc(M["l_kst"], 1)
                pe.wait_ge(M["l_qk"], 1)
                for c in range(4):
                    half, cs = slice(64 * (c % 2), 64 * (c % 2) + 64), slice(64 * c, 64 * c + 64)
                    for h in range(4):
                        at_c = (c // 2 * 4 + h) * 64
                        mm = pe.matmul(b6[half, at_c:at_c + 64], lk[:, h, cs], lq[:, h, cs], start=True, stop=True)
                mm.then_inc(M["l_att"], 1)
                pe.wait_ge(M["l_attc"], 1)
                pe.wait_ge(M["l_kstc"], 2)
                for c in range(4):
                    half, cs = slice(64 * (c % 2), 64 * (c % 2) + 64), slice(64 * c, 64 * c + 64)
                    m = c // 2
                    if c >= 1:
                        pe.wait_ge(M["l_oc"], c)
                        pe.wait_ge(M["l_dsr"], c)
                    for h in range(4):
                        for r in range(2):
                            vs = slice((2 * h + r) * P, (2 * h + r + 1) * P)
                            o = b7[:, (2 * h + r) * 64:(2 * h + r + 1) * 64]
                            mm = pe.matmul(o, lv[half, m, vs], att64[half, m, h], start=True, stop=c == 0)
                            if c >= 1:
                                mm = pe.matmul(o, l_state[:, h, r * P:(r + 1) * P], lq[:, h, cs], start=False, stop=True)
                    mm.then_inc(M["l_o"], 1)
                    if c < 3:
                        for h in range(4):
                            mm = pe.matmul((b4, b5)[h // 2][:, h % 2 * 256:(h % 2 + 1) * 256], kst[half, m, h],
                                           lv[half, m, h * 256:(h + 1) * 256], start=True, stop=True)
                        mm.then_inc(M["l_ds"], 1)
                pe.wait_ge(M["l_oc"], 4)

            def closing(done):
                pe.wait_ge(tile_read, 4 * done)
                for m in range(2):
                    for k4 in range(2):
                        turn_rows([(k * P, P, hidden[:, 4 * k4 + k, NMETA + m * P:NMETA + (m + 1) * P]) for k in range(4)])

            pe.wait_ge(cst_in, 16)
            pe.wait_ge(rows_in, 16 * N_ROW_LOADS)
            n_turn = [0]

            def turn_rows(jobs):
                n = n_turn[0]
                if n >= 4:
                    pe.wait_ge(turn_read, n - 3)
                for lo, rows, source in jobs:
                    mm = pe.transpose(tile_bank[n % 4][:, lo:lo + rows], source, ident[0:rows, 0:rows])
                mm.then_inc(turned, 1)
                n_turn[0] += 1

            turn_rows([(0, 96, gain_rows[0:96]), (P, N_LATE_ROWS, late_rows[0:N_LATE_ROWS])])
            pe.wait_ge(x_in, 32)
            for k in range(KD):
                ks = slice(k * P, (k + 1) * P)
                turn_rows([(0, NMETA, meta_rows[0:NMETA, ks])]
                          + [(NMETA + m * P, P, x_rows[:, m, ks]) for m in range(2)])
            pe.wait_ge(turn_read, n_turn[0])

            norm_sum()
            wait_hidden()
            block_t(first_of("ab_qkvz"), u, slice(0, T))
            norm_turn(rs, [0, 16, 144])
            for i in range(1, 4):
                block_t(first_of("ab_qkvz") + i, u, slice(0, T))
            block_t(first_of("ab_qb"), u, slice(0, T))
            b = first_of("ab_kvb")
            split_ready(b, 0, 1)
            bank_free(b, 0)
            transposed_tile(b, 0, 0, P, u, slice(0, T), tile_bank[0]).then_inc(tile_summed, 1)
            bank_free(b, 1)
            for m, s in enumerate((0, 16, 144)):
                mm = token_tile(b, 0, P, 2 * P, u, slice(s, s + P), tile_bank[1], m * P)
            mm.then_inc(tile_summed, 1)
            split_ready(b, 1, 1)
            bank_free(b, 2)
            for m, s in enumerate((0, 16, 144)):
                mm = token_tile(b, 1, 0, 16, u, slice(s, s + P), tile_bank[2], m * 16)
            mm.then_inc(tile_summed, 2)

            head_norms([(1, T, blk64)] * 5)
            pe.wait_ge(hn_scaled, hn[0])
            pe.wait_ge(M["kv_dup"], 1)
            pe.wait_ge(tile_read, 4 * b + 4)
            units = []
            for m, h in window_units():
                lo, hi = TILES[m]
                half = slice(64 * (h % 2), 64 * (h % 2) + 64)
                g = h // 4
                units.append(dict(
                    q=[qb[half, h // 2, lo:hi]], k=[kdup[half, g]], nq=hi - lo, nk=T, parts=half,
                    keys=[(e - s, s, [vb[0:e - s, c, 64 * g:64 * g + 64]]) for c, (s, e) in enumerate(TILES)]))
            attention(units)

            pe.wait_ge(M["silu_done"], 12)
            head_norms([(1, T, ones)] * 8)
            gated_delta()
            head_norms([(1, T, ones)] * 4)
            op[0] += 4
            out_product("ab_out", slice(0, T))
            norm_sum()
            wait_hidden()
            mlp_relu("mlp0", slice(0, T), op[0])
            op[0] += D_FF // P
            if n_layers == 1:
                closing(n_blocks)
                return

            norm_sum()
            wait_hidden()
            for i in range(2):
                block_t(first_of("c_q") + i, u, REAL)
                if i == 0:
                    norm_turn(rs, [0, 16, 144])
            b = first_of("c_kv")
            split_ready(b, 0, 1)
            for t in range(2):
                bank_free(b, t)
                transposed_tile(b, 0, t * P, t * P + P, u, slice(0, T), tile_bank[t]).then_inc(tile_summed, 1)
            split_ready(b, 1, 1)
            bank_free(b, 2)
            for m, s in enumerate((16, 144)):
                mm = token_tile(b, 1, 0, HALF, u, slice(s, s + P), tile_bank[2], m * HALF)
            mm.then_inc(tile_summed, 1)
            bank_free(b, 3)
            token_tile(b, 1, 0, HALF, u, slice(0, P), tile_bank[3], 0).then_inc(tile_summed, 1)
            head_norms([(1, SEQ, ones)] * 8 + [(1, T, ones)] * 2, table("swap_pairs"))
            pe.wait_ge(hn_roped, ropes[0])
            pe.wait_ge(tile_read, 4 * b + 4)
            units = []
            for m in range(2):
                for h in range(8):
                    g = h // 4
                    units.append(dict(
                        q=[qc[:, h, m * P:m * P + P]], k=[kc[:, g]], nq=P, nk=T, parts=slice(0, P),
                        keys=[(e - s, s, [vc[0:e - s, c, g * P:g * P + P]]) for c, (s, e) in enumerate(TILES)]))
            attention(units)
            out_product("c_out", REAL)
            norm_sum(REAL)
            wait_hidden()
            mlp_relu("mlp1", REAL, op[0])
            op[0] += D_FF // P
            if n_layers == 2:
                closing(n_blocks)
                return

            pe.wait_ge(tile_read, 4 * first_of("ev_in"))
            pe.wait_ge(mem_in, 16)
            for k in range(KD):
                turn_rows([(m * P, P, mem_rows[:, m, k * P:k * P + P]) for m in range(2)])
            pe.wait_ge(turn_read, n_turn[0])
            norm_sum(REAL)
            norms_mem = norms[0]
            pe.wait_ge(norm_ln, norms_mem)
            norm_sum(slice(0, SEQ))
            norm_turn(rs_mem, [0, P])

            for layer in range(n_layers - 2):
                if layer == 1:
                    norm_sum(REAL)
                wait_hidden()
                name = ("ev_in", "od_in")[layer]
                b = first_of(name)
                if layer == 0:
                    block_t(b, u, REAL)
                    norm_turn(rs, [16, 144])
                    block_t(b + 1, u, REAL)
                    block_v(b + 2, u, NMETA)
                    block_t(b + 3, u, REAL)
                    block_v(b + 4, u, NMETA)
                else:
                    block_t(b, u, REAL)
                    norm_turn(rs, [16, 144])
                    block_t(b + 1, u, REAL)
                    block_v(b + 2, u, NMETA)
                    block_v(b + 3, u, NMETA)
                    block_t(b + 4, u, REAL)
                    block_t(b + 5, u, REAL)
                op[0] += KD
                pe.wait_ge(operand_split, op[0])
                b = first_of(f"xkv{layer}")
                for i in range(2):
                    block_t(b + i, a, slice(0, SEQ))
                for i in range(2):
                    block_v(b + 2 + i, a, 0)
                if layer == 0:
                    head_norms([(1, SEQ, blk64)] * 8, table("swap_halves"))
                    pe.wait_ge(hn_roped, ropes[0])
                    units = []
                    for m in range(2):
                        for h in range(8):
                            half = slice(64 * (h % 2), 64 * (h % 2) + 64)
                            units.append(dict(
                                q=[mq[half, h // 2, m * P:m * P + P]], k=[mk[half, h // 2, 0:(m + 1) * P]], nq=P,
                                nk=(m + 1) * P, parts=half,
                                keys=[(P, c * P, [mv[:, c, 64 * h:64 * h + 64]]) for c in range(m + 1)]))
                    attention(units)
                    spatial_gating()
                    op[0] += 2
                else:
                    linear_attention()
                    head_norms([(2, SEQ, ones)] * 4)
                    op[0] += 8
                out_product(f"mix_out{layer}", REAL)
                norm_sum(REAL)
                wait_hidden()
                b = first_of(f"xq{layer}")
                for i in range(2):
                    block_t(b + i, u, REAL)
                head_norms([(2, SEQ, ones)] * 8)
                pe.wait_ge(hn_scaled, hn[0])
                units = []
                for m in range(2):
                    for h in range(4):
                        units.append(dict(
                            q=[xq[:, 2 * h + c, m * P:m * P + P] for c in range(2)],
                            k=[xk[:, 2 * h + c] for c in range(2)], nq=P, nk=SEQ, parts=slice(0, P),
                            keys=[(P, c * P, [xv[:, c, (2 * h + r) * P:(2 * h + r + 1) * P] for r in range(2)])
                                  for c in range(2)]))
                attention(units)
                out_product(f"x_out{layer}", REAL)
                norm_sum(REAL)
                wait_hidden()
                mlp_swiglu(f"swiglu{layer}", REAL, op[0])
                op[0] += D_FF2 // P
                if layer == n_layers - 3:
                    closing(n_blocks)

        @block.scalar
        def _(act):
            op, fin, step = [0], [0], [0]

            def link(ins):
                step[0] += 1
                ins.then_inc(act_step, 1)
                act.wait_ge(act_step, step[0])

            def split_high(b, half):
                if isinstance(b, int) and b >= n_blocks:
                    return
                slot, landed = slot_of(b), landed_by(b)
                act.wait_ge(raw_in[slot], landed)
                if not isinstance(b, int) or b >= 1:
                    act.wait_ge(tile_summed, 4 * b - 2 + 2 * half)
                act.activation(w_hi[:, half], raw[:, slot, :, half * HALF:(half + 1) * HALF], ACT.Copy)\
                    .then_inc(high_split, 1)

            def stream(name, evac, start=0, n=None):
                ph = phases[name]
                for i in range(start, ph.n if n is None else start + n):
                    b = ph.first + i
                    for half in range(2):
                        evac(i, 2 * half)
                        split_high(b + 1, half)
                        evac(i, 2 * half + 1)

            def nothing(i, t):
                pass

            def finish_chunk(k, norm, ready, ts, source=None):
                f = fin[0]
                fin[0] += 1
                x = hidden[:, k, ts] if source is None else source
                act.wait_ge(*ready)
                act.activation(u_hi[:, k, ts], x, ACT.Copy, scale=gain(norm, k)).then_inc(operand_high, 1)
                op[0] += 1
                if f >= 2:
                    act.wait_ge(sum_added, f - 1)
                act.activation(squares[:, f % 2, ts], x, ACT.Square).then_inc(squared, 1)

            norms = [0]

            def norm_rs(target, n, scale=1.0 / D):
                norms[0] += 1
                act.wait_ge(norm_summed, norms[0])
                act.activation(target, b7[:, 0:n], ACT.Ln, bias=eps, scale=scale).then_inc(norm_ln, 1)
                act.wait_ge(norm_ln, norms[0])
                act.activation(target, target, ACT.Exp, scale=-0.5).then_inc(rs_ready, 1)

            hn = [0]

            def head_norms(units):
                base, n = hn[0], len(units)

                def square(i):
                    source, columns, _, tokens, wait = units[i]
                    v = base + i
                    act.wait_ge(*wait)
                    if v >= 2:
                        act.wait_ge(hn_summed, v - 1)
                    act.activation(hn_sq[:, v % 2, 0:columns], source, ACT.Square).then_inc(hn_squared, 1)

                def scale(i):
                    _, _, mean, tokens, _ = units[i]
                    v = base + i
                    act.wait_ge(hn_summed, v + 1)
                    if v >= 2:
                        act.wait_ge(hn_scaled, v - 1)
                    act.activation(hn_r[:, v % 2, 0:tokens], (b4, b5)[v % 2][:, 0:tokens], ACT.Ln, bias=eps,
                                   scale=mean).then_inc(hn_ln, 1)
                    act.wait_ge(hn_ln, v + 1)
                    act.activation(hn_r[:, v % 2, 0:tokens], hn_r[:, v % 2, 0:tokens], ACT.Exp, scale=-0.5)\
                        .then_inc(hn_rs, 1)

                square(0)
                for i in range(n):
                    if i + 1 < n:
                        square(i + 1)
                    scale(i)
                hn[0] += n

            at = [0]

            def attention(units):
                base, n = at[0], len(units)

                def exponent(i):
                    x, v = units[i], base + i
                    q, s = slice(0, x["nq"]), v % 2
                    act.wait_ge(at_max, v + 1)
                    if v >= 2:
                        act.wait_ge(at_turned, v - 1)
                        act.wait_ge(at_prob, v - 1)
                    logits = at_s[q, s, 0:x["nk"]] if x["kind"] else (b4, b5)[s][q, 0:x["nk"]]
                    if x["kind"] == "window":
                        act.activation(at_es[q, s], sink[q, x["head"]:x["head"] + 1], ACT.Exp, bias=at_nm[q, s])
                    act.activation(at_p[q, s, 0:x["nk"]], logits, ACT.Exp, bias=at_nm[q, s], accum_out=at_den[q, s])\
                        .then_inc(at_exp, 1)

                def copy(i):
                    x, v = units[i], base + i
                    act.wait_ge(at_turned, v + 1)
                    if v >= 2:
                        act.wait_ge(at_summed, v - 1)
                    rows = x["rows"]
                    c = 0
                    while c < len(rows):
                        e = c
                        while e < len(rows) and rows[e] == rows[c]:
                            e += 1
                        ins = act.activation(at_pt[0:rows[c], v % 2, c:e, 0:x["nq"]],
                                             b6[0:rows[c], c * P:e * P].rearrange("p (c q) -> p c q", q=P)[:, :, 0:x["nq"]],
                                             ACT.Copy)
                        c = e
                    ins.then_inc(at_copied, 1)

                def result(i):
                    x, v = units[i], base + i
                    act.wait_ge(at_summed, v + 1)
                    act.activation(attention_out(a_hi, x), attention_bank(x), ACT.Copy).then_inc(operand_high, 1)
                    op[0] += 1

                exponent(0)
                for i in range(n):
                    if i + 1 < n:
                        exponent(i + 1)
                    copy(i)
                    if i >= 1:
                        result(i - 1)
                result(n - 1)
                at[0] += n

            def residual(name, norm, ts):
                def evac(i, t):
                    gt = 4 * (phases[name].first + i) + t
                    if norm is not None:
                        finish_chunk(4 * i + t, norm, (tile_read, gt + 1), ts)
                stream(name, evac)

            def mlp_relu(name, norm, ts, base, last):
                first = phases[name].first

                def group(g, closing):
                    b = 4 * g + first
                    for j in range(2):
                        for half in range(2):
                            for t in (2 * half, 2 * half + 1):
                                i = 4 * j + t
                                act.wait_ge(ff_ready, 8 * g + (ff[0] + i + 1))
                                act.activation(a_hi[:, i, ts], ff_a[:, i % 2, ts], ACT.Copy).then_inc(operand_high, 1)
                                if t % 2 == 0:
                                    split_at(g, b + j, first + j, half)
                    for j in range(2):
                        for half in range(2):
                            for t in (2 * half, 2 * half + 1):
                                if closing and norm is not None:
                                    op[0] = base + 32 + 4 * j + t
                                    finish_chunk(4 * j + t, norm, (tile_read, 4 * (b + 2 + j) + t + 1), ts)
                                if t % 2 == 0 and not (closing and last and j == 1):
                                    split_at(g, b + 2 + j, first + 2 + j, half)

                def split_at(g, b, like, half):
                    slot = (like + 1) % 2
                    if isinstance(b, int):
                        split_high(b + 1, half)
                        return
                    act.wait_ge(raw_in[slot], 32 * g + landed_by(like + 1))
                    act.wait_ge(tile_summed, 4 * b + (2 + 2 * half))
                    act.activation(w_hi[:, half], raw[:, slot, :, half * HALF:(half + 1) * HALF], ACT.Copy)\
                        .then_inc(high_split, 1)

                with act.Fori(0, D_FF // D - 1) as g:
                    group(g, False)
                group(D_FF // D - 1, True)
                ff[0] += D_FF // P
                op[0] = base + 32 + (8 if norm is not None else 0)

            ff, si = [0], [0]

            def mlp_swiglu(name, norm, ts):
                ph = phases[name]
                i, n = 0, ts.stop - ts.start
                for lo in range(0, D_FF2, D):
                    chunks = min(D, D_FF2 - lo) // P

                    def gate_up(i, t):
                        if t < 2:
                            act.wait_ge(tile_read, 4 * (ph.first + i) + t + 1)
                            act.activation(ff_s[:, t, 0:n], ff_z[:, t, 0:n], ACT.Silu).then_inc(silu_ready, 1)
                        else:
                            ff[0] += 1
                            act.wait_ge(ff_ready, ff[0])
                            act.activation(a_hi[:, (2 * (i - start) + t - 2), ts], ff_a[:, t - 2, 0:n], ACT.Copy)\
                                .then_inc(operand_high, 1)
                            op[0] += 1

                    def down(i, t):
                        if lo + D >= D_FF2 and norm is not None:
                            finish_chunk(4 * (i - start) + t, norm, (tile_read, 4 * (ph.first + i) + t + 1), ts)

                    start = i
                    stream(name, gate_up, i, chunks // 2)
                    i += chunks // 2
                    start = i
                    stream(name, down, i, 2)
                    i += 2

            split_high(0, 0)
            split_high(0, 1)
            act.wait_ge(cst_in, 16)
            for k in range(KD):
                finish_chunk(k, "attn0", (turn_read, k + 2), slice(0, T))
            norm_rs(rs, T)

            first = phases["ab_qkvz"].first

            def conv(i, t):
                c = 4 * i + t
                if c < 12:
                    act.wait_ge(M["conv_done"], c + 1)
                    act.activation(qkv[:, c], qkv[:, c], ACT.Silu).then_inc(M["silu_done"], 1)

            stream("ab_qkvz", conv)
            stream("ab_qb", nothing)
            stream("ab_kvb", nothing)
            b = 4 * phases["ab_qb"].first
            head_norms([(qb[:, i], T, 1.0 / 64, T, (tile_read, b + i + 1)) for i in range(4)]
                       + [(kb, T, 1.0 / 64, T, (tile_read, b + 5))])
            act.wait_ge(hn_scaled, hn[0])
            for g in range(2):
                for half in range(2):
                    ins = act.activation(kdup[64 * half:64 * half + 64, g], kb[64 * g:64 * g + 64], ACT.Copy)
            ins.then_inc(M["kv_dup"], 1)
            act.wait_ge(misc_in, 16 * N_MISC_LOADS)
            attention([dict(nq=TILES[m][1] - TILES[m][0], nk=T, kind="window", head=h, rows=[16, P, P],
                            parts=slice(64 * (h % 2), 64 * (h % 2) + 64), chunks=slice(4 + h // 2, 5 + h // 2),
                            tokens=slice(*TILES[m])) for m, h in window_units()])
            act.wait_ge(M["silu_done"], 12)
            head_norms([(qkv[:, i], T, 1.0, T, (M["silu_done"], 12)) for i in range(8)])

            act.activation(neg_a, a_log, ACT.Exp)
            act.activation(beta, hab[:, :, 0:8], ACT.Exp, scale=-1.0)
            act.wait_ge(M["d_first"], 1)
            link(act.activation(d_tmp2, d_tmp, ACT.Abs))
            link(act.activation(d_tmp2, d_tmp2, ACT.Exp, scale=-1.0))
            act.activation(d_tmp2, d_tmp2, ACT.Ln, bias=ones[:, 0:1]).then_inc(M["d_gate_exp"], 1)
            for i, (m, source) in enumerate(delta_turns()):
                n = TILES[m][1] - TILES[m][0]
                act.wait_ge(M["d_turned"], i + 1)
                act.activation((v_tok if source == 8 else k_tok)[0:n, m], (b4, b5)[i % 2][0:n, 0:4 * P].rearrange(
                    "p (h d) -> p h d", h=4), ACT.Copy).then_inc(M["d_copied"], 1)
            act.wait_ge(M["d_cum_read"], 1)
            act.activation(necc[0:NMETA, 0], gcc[0:NMETA, 0], ACT.Exp)
            act.activation(necc[:, 1:3], gcc[:, 1:3], ACT.Exp).then_inc(M["d_gate_exp"], 1)
            y = 0
            for j, (c, d) in enumerate(BATCHES):
                n = TILES[c][1] - TILES[c][0]
                act.wait_ge(M["d_diff"], j + 1)
                act.activation(decayed_queries(c, d), b4[:, 0:4 * n], ACT.Exp).then_inc(M["d_egr"], 1)
                act.activation(kdf[0:n, c, 4 * d:4 * d + 4], d_tmp[0:n, c, 4 * d:4 * d + 4], ACT.Exp)
                act.activation(dm[0:n, 0:4 * n], dm[0:n, 0:4 * n], ACT.Exp).then_inc(M["d_dm"], 1)
                for level in range(1, n_levels(n)):
                    y += 1
                    act.wait_ge(M["d_w"], y)
                    act.activation(wt[0:n, 0:4 * n], b7[0:n, 0:4 * n], ACT.Copy).then_inc(M["d_w_copied"], 1)
            act.wait_ge(tile_read, 4 * first + 16)
            act.activation(za, za, ACT.Silu).then_inc(M["silu_r"], 1)

            def gated_norms(units, chunk_of):
                head_norms(units)
                for c in chunk_of:
                    gated[0] += 1
                    act.wait_ge(hn_gated, gated[0])
                    act.activation(a_hi[:, c, gts], hn_t[:, (gated[0] - 1) % 2, 0:gts.stop - gts.start], ACT.Copy)\
                        .then_inc(operand_high, 1)
                    op[0] += 1

            gated, gts = [0], slice(0, T)
            gated_norms([(o_delta[:, h], T, 1.0 / P, T, (M["d_o_read"], 6)) for h in range(4)], range(4))
            residual("ab_out", "mlp0", slice(0, T))
            norm_rs(rs, T)
            mlp_relu("mlp0", "attn1" if n_layers > 1 else None, slice(0, T), op[0], n_layers == 1)
            if n_layers == 1:
                return

            norm_rs(rs, T)
            stream("c_q", nothing)
            stream("c_kv", nothing)
            b = 4 * phases["c_q"].first
            head_norms([(qc[:, i], SEQ, 1.0 / P, SEQ, (tile_read, b + i + 1)) for i in range(8)]
                       + [(kc[:, i], T, 1.0 / P, T, (tile_read, b + 9 + i)) for i in range(2)])
            attention([dict(nq=P, nk=T, kind=None, rows=[16, P, P], parts=slice(0, P), chunks=slice(h, h + 1),
                            tokens=slice(16 + m * P, 16 + (m + 1) * P)) for m in range(2) for h in range(8)])
            residual("c_out", "mlp1", REAL)
            norm_rs(rs[:, REAL], SEQ)
            mlp_relu("mlp1", "mix0" if n_layers > 2 else None, REAL, op[0], n_layers == 2)
            if n_layers == 2:
                return

            norm_rs(rs[:, REAL], SEQ)
            for k in range(KD):
                f = fin[0]
                fin[0] += 1
                act.wait_ge(turn_read, 10 + k)
                if f >= 2:
                    act.wait_ge(sum_added, f - 1)
                act.activation(squares[:, f % 2, 0:SEQ], memory[:, k], ACT.Square).then_inc(squared, 1)
            norm_rs(rs_mem, SEQ)

            for layer in range(n_layers - 2):
                def memory_operand():
                    for k in range(KD):
                        act.activation(a_hi[:, k, 0:SEQ], memory[:, k], ACT.Copy, scale=gain(f"memkv{layer}", k))\
                            .then_inc(operand_high, 1)
                        op[0] += 1

                if layer == 1:
                    norm_rs(rs[:, REAL], SEQ)
                memory_operand()
                if layer == 0:
                    first = 4 * phases["ev_in"].first

                    def gelu(i, t):
                        if i == 3:
                            act.wait_ge(tile_read, first + 4 * i + t + 1)
                            act.activation(gu[:, t], gu[:, t], ACT.Gelu).then_inc(M["gelu"], 1)
                        if i == 4:
                            act.wait_ge(tile_read, first + 4 * i + t + 1)
                            part = gv[:, t % 2, t // 2 * HALF:(t // 2 + 1) * HALF]
                            act.activation(part, part, ACT.Gelu).then_inc(M["gelu"], 1)

                    stream("ev_in", gelu)
                    stream("xkv0", nothing)
                    act.wait_ge(M["rope_angle"], 1)
                    act.activation(sin_m, angle[:, 0], ACT.Sin)
                    act.activation(cos_m, angle[:, 1], ACT.Sin).then_inc(M["rope_sin"], 1)
                    head_norms([(x[:, i], SEQ, 1.0 / 64, SEQ, (tile_read, first + 4 * j + i + 1))
                                for j, x in enumerate((mq, mk)) for i in range(4)])
                    attention([dict(nq=P, nk=(m + 1) * P, kind="causal", rows=[P] * (m + 1),
                                    parts=slice(64 * (h % 2), 64 * (h % 2) + 64), chunks=slice(h // 2, h // 2 + 1),
                                    tokens=slice(16 + m * P, 16 + (m + 1) * P)) for m in range(2) for h in range(8)])
                    act.wait_ge(M["g_stat"], 1)
                    act.wait_ge(M["ws_turned"], 2)
                    act.activation(gt, gv, ACT.Square).then_inc(M["g_sq"], 1)
                    act.wait_ge(M["g_stat"], 2)
                    link(act.activation(g_var, g_var, ACT.Ln, bias=eps, scale=1.0 / 64))
                    act.activation(g_var, g_var, ACT.Exp, scale=-0.5).then_inc(M["g_ln"], 1)
                    for c in range(2):
                        act.wait_ge(M["g_read"], c + 1)
                        act.activation(a_hi[:, 4:8, 16 + c * P:16 + (c + 1) * P], g_out(c), ACT.Copy)\
                            .then_inc(operand_high, 1)
                        op[0] += 1
                else:
                    first = 4 * phases["od_in"].first
                    stream("od_in", nothing)
                    stream("xkv1", nothing)
                    act.wait_ge(tile_read, first + 24)
                    act.activation(lr, lr, ACT.Silu).then_inc(M["silu_r"], 1)
                    for h in range(4):
                        act.wait_ge(M["l_gate"], h + 1)
                        link(act.activation(l_tmp[:, h], la[:, h], ACT.Abs))
                        link(act.activation(l_tmp[:, h], l_tmp[:, h], ACT.Exp, scale=-1.0))
                        act.activation(l_tmp[:, h], l_tmp[:, h], ACT.Ln, bias=ones[:, 0:1]).then_inc(M["l_exp"], 1)
                    act.wait_ge(M["l_scan"], 1)
                    act.activation(l_tmp, la, ACT.Exp).then_inc(M["l_exp"], 1)
                    for h in range(4):
                        for c in range(4):
                            cs = slice(64 * c, 64 * c + 64)
                            ins = act.activation(ks_t[:, h, cs], la[:, h, cs], ACT.Exp, scale=-1.0,
                                                 bias=la[:, h, 64 * c + 63:64 * c + 64])
                    ins.then_inc(M["l_exp"], 1)
                    act.activation(l_dec, la.rearrange("p h (c t) -> p h c t", t=64)[:, :, :, 63], ACT.Exp)
                    act.activation(lo_t[:, 4:8], la, ACT.Exp, scale=-1.0).then_inc(M["l_exp"], 1)
                    for m in range(2):
                        act.wait_ge(M["l_kst"], m + 1)
                        act.activation(kst[:, m], (b4, b5)[m][:, 0:4 * P].rearrange("p (h d) -> p h d", h=4), ACT.Copy)\
                            .then_inc(M["l_kstc"], 1)
                    gts = REAL
                    gated_norms([(lo_t[:, 2 * h:2 * h + 2].rearrange("p a t -> p (a t)"), 2 * SEQ, 1.0 / 256, SEQ,
                                  (M["l_oc"], 4)) for h in range(4)], range(8))
                residual(f"mix_out{layer}", f"memq{layer}", REAL)
                norm_rs(rs[:, REAL], SEQ)
                stream(f"xq{layer}", nothing)
                b, bk = 4 * phases[f"xq{layer}"].first, 4 * phases[f"xkv{layer}"].first
                head_norms([(x[:, 2 * h:2 * h + 2].rearrange("p a t -> p (a t)"), 2 * SEQ, 1.0 / 256, SEQ,
                             (tile_read, at_ + 2 * h + 2)) for x, at_ in ((xk, bk), (xq, b)) for h in range(4)])
                attention([dict(nq=P, nk=SEQ, kind=None, rows=[P, P], parts=slice(0, P), chunks=slice(2 * h, 2 * h + 2),
                                tokens=slice(16 + m * P, 16 + (m + 1) * P)) for m in range(2) for h in range(4)])
                residual(f"x_out{layer}", f"ffn{layer}", REAL)
                norm_rs(rs[:, REAL], SEQ)
                mlp_swiglu(f"swiglu{layer}", "mix1" if layer == 0 and n_layers == 4 else None, REAL)

        @block.vector
        def _(dve):
            op, fin, step = [0], [0], [0]

            def link(ins):
                step[0] += 1
                ins.then_inc(dve_step, 1)
                dve.wait_ge(dve_step, step[0])

            def split_low(b, half, slot=None):
                if isinstance(b, int) and b >= n_blocks:
                    return
                slot = slot_of(b) if slot is None else slot
                dve.wait_ge(high_split, 2 * b + (half + 1))
                dve.tensor_tensor(w_lo[:, half], raw[:, slot, :, half * HALF:(half + 1) * HALF],
                                  w_hi[:, half].bitcast(F32), ALU.subtract).then_inc(low_split, 1)

            def stream(name, evac, start=0, n=None, close=None):
                ph = phases[name]
                for i in range(start, ph.n if n is None else start + n):
                    b = ph.first + i
                    for half in range(2):
                        evac(i, 2 * half, 4 * b + 2 * half)
                        split_low(b + 1, half)
                        evac(i, 2 * half + 1, 4 * b + 2 * half + 1)
                    if close is not None:
                        close(i)

            def low_part(target, source, high):
                op[0] += 1
                dve.wait_ge(operand_high, op[0])
                dve.tensor_tensor(target, source, high.bitcast(F32), ALU.subtract).then_inc(operand_split, 1)

            def finish_low(k, norm, ts, source=None):
                op[0] += 1
                dve.wait_ge(operand_high, op[0])
                dve.scalar_tensor_tensor(u_lo[:, k, ts], hidden[:, k, ts], gain(norm, k),
                                         u_hi[:, k, ts].bitcast(F32), ALU.mult, ALU.subtract).then_inc(operand_split, 1)

            norms, turns = [0], [0]

            def rms_ready():
                norms[0] += 1
                dve.wait_ge(rs_ready, norms[0])

            def turn_rs(target, n):
                turns[0] += 1
                dve.wait_ge(rs_turned, turns[0])
                dve.tensor_copy(target, b6[:, 0:n * P].rearrange("p (m c) -> p m c", c=P)[:, :, 0]).then_inc(rs_tok_ready, 1)
                dve.wait_ge(rs_tok_ready, turns[0])

            def scaled(target, t, gt, ts, scale=None):
                dve.wait_ge(tile_summed, gt + 1)
                n = ts.stop - ts.start
                dve.tensor_tensor(target, tile_bank[t][:, 0:n], rs[:, ts] if scale is None else scale, ALU.mult)\
                    .then_inc(tile_read, 1)

            def scaled_tokens(target, t, gt, column):
                dve.wait_ge(tile_summed, gt + 1)
                dve.tensor_scalar(target, tile_bank[t][:, 0:HALF], column, None, ALU.mult).then_inc(tile_read, 1)

            def add_tile(k, t, gt, ts, first=False):
                dve.wait_ge(tile_summed, gt + 1)
                dve.wait_ge(tile_read, gt)
                dve.tensor_tensor(hidden[:, k, ts], tile_bank[t][:, 0:ts.stop - ts.start], hidden[:, k, ts], ALU.add)\
                    .then_inc(tile_read, 1)

            hn, ropes, gated = [0], [0], [0]

            def head_norms(units, rope=None, gate=None, ts=slice(0, T)):
                base, r0, n = hn[0], ropes[0], len(units)
                chunk = [0]

                def scale(i):
                    sources, gains_, targets = units[i]
                    v = base + i
                    dve.wait_ge(hn_rs, v + 1)
                    if rope is not None and r0 + i >= 2:
                        dve.wait_ge(hn_swapped, r0 + i - 1)
                    for source, g, target in zip(sources, gains_, targets):
                        w_ = source.shape[1]
                        if rope is not None:
                            target = hn_n[:, (r0 + i) % 2, 0:w_]
                        ins = dve.scalar_tensor_tensor(target, source, g, hn_r[:, v % 2, 0:w_], ALU.mult, ALU.mult)
                    ins.then_inc(hn_scaled, 1)

                def rotate(i):
                    r, target = r0 + i, units[i][2][0]
                    w_ = target.shape[1]
                    cos, sin = rope[i]
                    dve.wait_ge(hn_scaled, base + i + 1)
                    dve.tensor_tensor(target, hn_n[:, r % 2, 0:w_], cos, ALU.mult)
                    dve.wait_ge(hn_swapped, r + 1)
                    link(dve.tensor_tensor(hn_t[:, r % 2, 0:w_], (b6, b7)[r % 2][:, 0:w_], sin, ALU.mult))
                    dve.tensor_tensor(target, target, hn_t[:, r % 2, 0:w_], ALU.add).then_inc(hn_roped, 1)

                def gates(i):
                    dve.wait_ge(hn_scaled, base + i + 1)
                    for target in units[i][2]:
                        c = gated[0]
                        if chunk[0] >= 2:
                            dve.wait_ge(operand_split, op[0])
                        w_ = target.shape[1]
                        dve.tensor_tensor(hn_t[:, c % 2, 0:w_], target, gate[chunk[0]], ALU.mult).then_inc(hn_gated, 1)
                        gated[0] += 1
                        chunk[0] += 1
                        if chunk[0] >= 2:
                            low(chunk[0] - 2, c - 1)

                def low(k, c):
                    low_part(a_lo[:, k, ts], hn_t[:, c % 2, 0:ts.stop - ts.start], a_hi[:, k, ts])

                for i in range(n):
                    scale(i)
                    if rope is not None and i >= 1:
                        rotate(i - 1)
                if rope is not None:
                    rotate(n - 1)
                    ropes[0] += n
                if gate is not None:
                    for i in range(n):
                        gates(i)
                    low(chunk[0] - 1, gated[0] - 1)
                hn[0] += n

            at = [0]
            biased = [0]

            def attention(units):
                base, n = at[0], len(units)

                def maximum(i):
                    x, v = units[i], base + i
                    q, s, nk = slice(0, x["nq"]), v % 2, x["nk"]
                    dve.wait_ge(at_scored, v + 1)
                    logits = (b4, b5)[s][q, 0:nk]
                    if x["kind"]:
                        if v >= 2:
                            dve.wait_ge(at_exp, v - 1)
                        if x["kind"] == "window":
                            ins = dve.scalar_tensor_tensor(at_s[q, s, 0:nk], x["bias"][q], x["slope"], logits,
                                                           ALU.mult, ALU.add)
                        else:
                            ins = dve.tensor_tensor(at_s[q, s, 0:nk], logits, x["bias"], ALU.add)
                        link(ins)
                        logits = at_s[q, s, 0:nk]
                    if x["kind"] == "window":
                        link(dve.tensor_reduce(at_m[q, s], logits, AX.X, ALU.max))
                        dve.tensor_scalar(at_nm[q, s], at_m[q, s], sink[q, x["head"]:x["head"] + 1], -1.0, ALU.max,
                                          ALU.mult).then_inc(at_max, 1)
                    else:
                        dve.tensor_reduce(at_nm[q, s], logits, AX.X, ALU.max, negate=True).then_inc(at_max, 1)

                def normalise(i):
                    x, v = units[i], base + i
                    q, s = slice(0, x["nq"]), v % 2
                    dve.wait_ge(at_exp, v + 1)
                    if x["kind"] == "window":
                        link(dve.tensor_tensor(at_den[q, s], at_den[q, s], at_es[q, s], ALU.add))
                    link(dve.reciprocal(at_inv[q, s], at_den[q, s]))
                    dve.tensor_scalar(at_p[q, s, 0:x["nk"]], at_p[q, s, 0:x["nk"]], at_inv[q, s], None, ALU.mult)\
                        .then_inc(at_prob, 1)

                def result(i):
                    x = units[i]
                    low_part(attention_out(a_lo, x), attention_bank(x), attention_out(a_hi, x))

                maximum(0)
                for i in range(n):
                    if i + 1 < n:
                        maximum(i + 1)
                    normalise(i)
                    if i >= 1:
                        result(i - 1)
                result(n - 1)
                at[0] += n

            def residual(name, norm, ts):
                def evac(i, t, gt):
                    add_tile(4 * i + t, t, gt, ts)
                    if norm is not None and 4 * i + t >= 1:
                        finish_low(4 * i + t - 1, norm, ts)
                stream(name, evac)
                if norm is not None:
                    finish_low(KD - 1, norm, ts)

            ff = [0]

            def mlp_relu(name, norm, ts, last):
                first = phases[name].first
                n, base, f0 = ts.stop - ts.start, op[0], ff[0]

                def group(g, closing):
                    b = 4 * g + first

                    def low(i):
                        dve.wait_ge(operand_high, 8 * g + (base + i + 1))
                        dve.tensor_tensor(a_lo[:, i, ts], ff_a[:, i % 2, ts], a_hi[:, i, ts].bitcast(F32), ALU.subtract)\
                            .then_inc(operand_split, 1)

                    for j in range(2):
                        for t in range(4):
                            i, gt = 4 * j + t, 4 * b + (4 * j + t)
                            if f0 + i >= 2:
                                dve.wait_ge(ff_ready, 8 * g + (f0 + i - 1))
                            scaled(ff_z[:, i % 2, ts], t, gt, ts)
                            if i >= 2:
                                low(i - 2)
                            dve.wait_ge(operand_split, 8 * g + (base + i - 1))
                            dve.wait_ge(tile_read, gt + 1)
                            dve.scalar_tensor_tensor(ff_a[:, i % 2, ts], ff_z[:, i % 2, ts], 0.0, ff_z[:, i % 2, ts],
                                                     ALU.max, ALU.mult).then_inc(ff_ready, 1)
                            if t % 2 == 0:
                                split_low(b + j + 1, t // 2, slot_of(first + j + 1))
                    low(6)
                    low(7)
                    for j in range(2):
                        for t in range(4):
                            i, gt = 4 * j + t, 4 * b + (8 + 4 * j + t)
                            add_tile(i, t, gt, ts)
                            if closing and norm is not None and i >= 1:
                                finish_low(i - 1, norm, ts)
                            if t % 2 == 0 and not (closing and last and j == 1):
                                split_low(b + j + 3, t // 2, slot_of(first + j + 3))

                with dve.Fori(0, D_FF // D - 1) as g:
                    group(g, False)
                op[0] = base + D_FF // P
                group(D_FF // D - 1, True)
                if norm is not None:
                    finish_low(KD - 1, norm, ts)
                ff[0] += D_FF // P

            ff_relu = 2 * D_FF // P

            def mlp_swiglu(name, norm, ts):
                i, n = 0, ts.stop - ts.start
                for lo in range(0, D_FF2, D):
                    chunks = min(D, D_FF2 - lo) // P
                    begin = i
                    closing = lo + D >= D_FF2 and norm is not None

                    def gate_up(i, t, gt):
                        if t < 2:
                            dve.wait_ge(ff_ready, ff[0])
                        else:
                            dve.wait_ge(silu_ready, ff[0] - ff_relu + 1)
                        scaled(ff_z[:, t % 2, 0:n], t, gt, ts)
                        if t >= 2:
                            ff[0] += 1
                            dve.wait_ge(operand_split, op[0])
                            dve.wait_ge(tile_read, gt + 1)
                            dve.tensor_tensor(ff_a[:, t - 2, 0:n], ff_z[:, t - 2, 0:n], ff_s[:, t - 2, 0:n], ALU.mult)\
                                .then_inc(ff_ready, 1)

                    def lows(i):
                        for t in range(2):
                            k = 2 * (i - begin) + t
                            low_part(a_lo[:, k, ts], ff_a[:, t, 0:n], a_hi[:, k, ts])

                    def down(i, t, gt):
                        k = 4 * (i - begin) + t
                        add_tile(k, t, gt, ts)
                        if closing and k >= 1:
                            finish_low(k - 1, norm, ts)

                    stream(name, gate_up, i, chunks // 2, close=lows)
                    i += chunks // 2
                    begin = i
                    stream(name, down, i, 2)
                    i += 2
                if norm is not None:
                    finish_low(KD - 1, norm, ts)

            split_low(0, 0)
            split_low(0, 1)
            dve.wait_ge(turned, 1)
            dve.tensor_copy(gains[:], tile_bank[0][:, 0:96])
            link(dve.tensor_copy(late[:], tile_bank[0][:, P:P + N_LATE_ROWS]))
            dve.tensor_scalar(col("b_q"), col("b_q"), 64.0 ** -0.5, None, ALU.mult)
            dve.tensor_scalar(col("c_q"), col("c_q"), 128.0 ** -0.5, None, ALU.mult)
            dve.tensor_scalar(col("ev_q"), col("ev_q"), 64.0 ** -0.5, None, ALU.mult)
            dve.tensor_scalar(late[:, LATE_ROWS["xa_q"]:LATE_ROWS["xa_q"] + 4],
                              late[:, LATE_ROWS["xa_q"]:LATE_ROWS["xa_q"] + 4], 256.0 ** -0.5, None,
                              ALU.mult).then_inc(turn_read, 1)
            for k in range(KD):
                dve.wait_ge(turned, k + 2)
                dve.tensor_copy(hidden[:, k], tile_bank[(k + 1) % 4][:, 0:T]).then_inc(turn_read, 1)
                finish_low(k, "attn0", slice(0, T))

            full = slice(0, T)
            dve.memset(xa[:, :, 0:2], 0.0)
            dve.memset(xa[:, :, PAD - 2:PAD], 0.0)
            rms_ready()

            def project_ab(i, t, gt):
                c = 4 * i + t
                if c >= 12:
                    scaled(za[:, c - 12], t, gt, full)
                    if c == 12:
                        turn_rs(rs_tok, 3)
                    return
                scaled(xa[:, c, 2:2 + T], t, gt, full)
                dve.wait_ge(tile_read, gt + 1)
                link(dve.tensor_scalar(qkv[:, c], xa[:, c, 0:T], col("conv", c), None, ALU.mult))
                for j in range(1, 5):
                    ins = dve.scalar_tensor_tensor(qkv[:, c], xa[:, c, j:j + T], col("conv", 12 * j + c), qkv[:, c],
                                                   ALU.mult, ALU.add)
                    if j < 4:
                        link(ins)
                ins.then_inc(M["conv_done"], 1)

            stream("ab_qkvz", project_ab)
            stream("ab_qb", lambda i, t, gt: scaled(qb[:, t], t, gt, full))

            def project_kvb(i, t, gt):
                if t == 0:
                    scaled(kb, t, gt, full)
                if t == 1:
                    dve.wait_ge(tile_summed, gt + 1)
                    dve.tensor_tensor(vb, tile_bank[1][:, 0:3 * P].rearrange("p (m d) -> p m d", m=3),
                                      rs_tok.unsqueeze(2).to_broadcast([P, 3, P]), ALU.mult).then_inc(tile_read, 1)
                if t == 2:
                    dve.wait_ge(tile_summed, gt + 1)
                    dve.tensor_tensor(hab, tile_bank[2][:, 0:48].rearrange("p (m d) -> p m d", m=3),
                                      rs_tok.unsqueeze(2).to_broadcast([P, 3, 16]), ALU.mult).then_inc(tile_read, 2)

            stream("ab_kvb", project_kvb)
            head_norms([([qb[:, i]], [col("b_q")], [qb[:, i]]) for i in range(4)] + [([kb], [col("b_k")], [kb])])
            dve.wait_ge(misc_in, 16 * N_MISC_LOADS)
            attention([dict(nq=TILES[m][1] - TILES[m][0], nk=T, kind="window", head=h, bias=early_table(f"ndist{m}"),
                            slope=2.0 ** (-(h + 1)), parts=slice(64 * (h % 2), 64 * (h % 2) + 64),
                            chunks=slice(4 + h // 2, 5 + h // 2), tokens=slice(*TILES[m])) for m, h in window_units()])
            head_norms([([qkv[:, i]], [P ** -0.5 if i < 4 else 1.0], [qkv[:, i]]) for i in range(8)])

            dve.tensor_tensor(d_tmp, hab[:, :, 8:16], dt_bias.unsqueeze(1).to_broadcast([P, 3, 8]), ALU.add)\
                .then_inc(M["d_first"], 1)
            dve.wait_ge(M["d_gate_exp"], 1)
            link(dve.tensor_scalar(beta, beta, 1.0, None, ALU.add))
            dve.reciprocal(beta, beta)
            dve.wait_ge(M["d_first"], 1)
            link(dve.scalar_tensor_tensor(d_tmp2, d_tmp, 0.0, d_tmp2, ALU.max, ALU.add))
            link(dve.tensor_scalar(d_tmp2, d_tmp2, -1.0, None, ALU.mult))
            dve.tensor_tensor(decay, d_tmp2, neg_a.unsqueeze(1).to_broadcast([P, 3, 8]), ALU.mult)\
                .then_inc(M["d_gates"], 1)
            dve.wait_ge(M["d_cum"], 1)
            dve.tensor_copy(gcc[0:NMETA, 0], b6[0:NMETA, 0:8])
            dve.tensor_copy(gcc[:, 1:3], b6[:, 8:24].rearrange("p (c h) -> p c h", c=2)).then_inc(M["d_cum_read"], 1)
            dve.wait_ge(M["d_cum_read"], 1)
            for j, (c, d) in enumerate(BATCHES):
                s, e = TILES[c]
                n, dh = e - s, slice(4 * d, 4 * d + 4)

                def heads(ap):
                    return ap.rearrange("p (h i) -> p h i", h=4)

                x, last_row = inverse(j), (n - 1) * (1 - d)
                dmn = heads(dm[0:n, 0:4 * n])
                dve.wait_ge(M["d_rows"], j + 1)
                rows = heads(b4[:, 0:4 * n])
                dve.tensor_tensor(d_tmp[0:n, c, dh], rows[0:n, :, last_row], gcc[0:n, c, dh], ALU.subtract)
                link(dve.tensor_tensor(dmn, rows[0:n], gcc[0:n, c, dh].unsqueeze(2).to_broadcast([n, 4, n]), ALU.subtract))
                neg = table(("neg_f", "neg_b")[d])[0:n, 0:n].unsqueeze(1).to_broadcast([n, 4, n])
                dve.tensor_tensor(dmn, dmn, neg, ALU.add).then_inc(M["d_diff"], 1)
                dve.wait_ge(M["d_egr"], j + 1)
                qd = heads(decayed_queries(c, d))
                link(dve.tensor_copy(egl[:, c, dh], qd[:, :, last_row]))
                dve.tensor_tensor(qd, qd, qkv[:, 0:4, s:e], ALU.mult)
                dve.wait_ge(M["d_gk"], j + 1)
                nnn = heads(nn[0:n, 0:4 * n])
                link(dve.tensor_tensor(nnn, heads(b5[0:n, 0:4 * n]),
                                       beta[0:n, c, dh].unsqueeze(2).to_broadcast([n, 4, n]), ALU.mult))
                dve.wait_ge(M["d_dm"], j + 1)
                dve.tensor_tensor(nnn, nnn, dmn, ALU.mult)
                dve.tensor_tensor(heads(inner_product(j)[0:n]), heads(b6[0:n, 0:4 * n]), dmn, ALU.mult)\
                    .then_inc(M["d_n"], 1)
                eye = ident[0:n, 0:n].unsqueeze(1).to_broadcast([n, 4, n])
                for level in range(n_levels(n)):
                    i = levels_before(j) + level
                    dve.wait_ge(M["d_y"], i + 1)
                    if level == 0:
                        dve.wait_ge(M["d_nb"], i + 1)
                        dve.tensor_tensor(heads(x[0:n]), eye, heads(nb_[0:n, 0:4 * n]), ALU.subtract)
                        dve.tensor_tensor(heads(xt[0:n, 0:4 * n]), eye, heads(b5[0:n, 0:4 * n]), ALU.subtract)\
                            .then_inc(M["d_x"], 1)
                        continue
                    dve.wait_ge(M["d_x"], i)
                    if level < n_levels(n) - 1:
                        dve.tensor_tensor(xt[0:n, 0:4 * n], xt[0:n, 0:4 * n], b6[0:n, 0:4 * n], ALU.subtract)
                    dve.tensor_tensor(x[0:n], x[0:n], b5[0:n, 0:4 * n], ALU.subtract).then_inc(M["d_x"], 1)
            dve.wait_ge(M["d_gate_exp"], 2)
            dve.wait_ge(M["d_copied"], 6)
            seen = set()
            for j, (c, d, first, lastone) in enumerate(SCAN):
                s, e = TILES[c]
                n, dh = e - s, slice(4 * d, 4 * d + 4)

                def by_head(ap):
                    return ap.rearrange("p (h i) -> p h i", h=4)

                r, vn, kd = (by_head(x[0:n]) for x in (scan_r, scan_v, scan_k))
                if j >= 1:
                    dve.wait_ge(M["d_v"], j)
                if first:
                    dve.tensor_copy(r, v_tok[0:n, c]).then_inc(M["d_r"], 1)
                else:
                    dve.wait_ge(M["d_ks"], j - 1)
                    link(dve.tensor_tensor(r, by_head(b4[0:n]), necc[0:n, c, dh].unsqueeze(2).to_broadcast([n, 4, P]),
                                           ALU.mult))
                    dve.tensor_tensor(r, v_tok[0:n, c], r, ALU.subtract).then_inc(M["d_r"], 1)
                if not lastone:
                    if j >= 1:
                        dve.wait_ge(M["d_s"], j)
                    dve.tensor_tensor(kd, k_tok[0:n, c], kdf[0:n, c, dh].unsqueeze(2).to_broadcast([n, 4, P]),
                                      ALU.mult).then_inc(M["d_kdec"], 1)
                dve.wait_ge(M["d_v"], j + 1)
                if j >= 1:
                    dve.wait_ge(M["d_o"], j)
                dve.tensor_tensor(vn, by_head(b5[0:n]), beta[0:n, c, dh].unsqueeze(2).to_broadcast([n, 4, P]), ALU.mult)\
                    .then_inc(M["d_vnew"], 1)
                dve.wait_ge(M["d_o"], j + 1)
                o = by_head(b6[:, 0:4 * n])
                if c in seen:
                    dve.wait_ge(M["d_o_read"], j)
                    dve.tensor_tensor(o_delta[:, :, s:e], o, o_delta[:, :, s:e], ALU.add).then_inc(M["d_o_read"], 1)
                else:
                    dve.tensor_copy(o_delta[:, :, s:e], o).then_inc(M["d_o_read"], 1)
                seen.add(c)
                if not lastone:
                    dve.wait_ge(M["d_s"], j + 1)
                    if first:
                        dve.tensor_copy(state[:, d], by_head(b7[:])).then_inc(M["d_s_read"], 1)
                    else:
                        dve.wait_ge(M["d_s_read"], j - 1)
                        link(dve.tensor_tensor(state[:, d], state[:, d],
                                               egl[:, c, dh].unsqueeze(2).to_broadcast([P, 4, P]), ALU.mult))
                        dve.tensor_tensor(state[:, d], state[:, d], by_head(b7[:]), ALU.add).then_inc(M["d_s_read"], 1)
            dve.wait_ge(M["silu_r"], 1)
            head_norms([([o_delta[:, h]], [col("a_out")], [o_delta[:, h]]) for h in range(4)],
                       gate=[za[:, h] for h in range(4)], ts=full)
            residual("ab_out", "mlp0", full)
            rms_ready()
            mlp_relu("mlp0", "attn1" if n_layers > 1 else None, full, n_layers == 1)

            def closing(first_turn):
                for i in range(4):
                    dve.wait_ge(turned, first_turn + i + 1)
                    dve.tensor_copy(out_rows[:, i // 2, i % 2 * BLOCK:(i % 2 + 1) * BLOCK],
                                    tile_bank[(first_turn + i) % 4][:]).then_inc(turn_read, 1)

            if n_layers == 1:
                closing(9)
                return

            rms_ready()

            def project_c(i, t, gt):
                scaled(qc[:, 4 * i + t], t, gt, REAL)
                if i == 1 and t == 0:
                    turn_rs(rs_tok, 3)

            stream("c_q", project_c)

            def project_ckv(i, t, gt):
                if t < 2:
                    scaled(kc[:, t], t, gt, full)
                    return
                dve.wait_ge(tile_summed, gt + 1)
                if t == 2:
                    dve.tensor_tensor(vc[:, 1:3], tile_bank[2][:].rearrange("p (m d) -> p m d", m=2),
                                      rs_tok[:, 1:3].unsqueeze(2).to_broadcast([P, 2, HALF]), ALU.mult).then_inc(tile_read, 1)
                else:
                    dve.tensor_scalar(vc[:, 0], tile_bank[3][:, 0:HALF], rs_tok[:, 0:1], None, ALU.mult)\
                        .then_inc(tile_read, 1)

            stream("c_kv", project_ckv)
            cos, sin = table("cos_c"), table("sin_c")
            head_norms([([qc[:, i]], [col("c_q")], [qc[:, i]]) for i in range(8)]
                       + [([kc[:, i]], [col("c_k")], [kc[:, i]]) for i in range(2)],
                       rope=[(cos[:, REAL], sin[:, REAL])] * 8 + [(cos, sin)] * 2)
            attention([dict(nq=P, nk=T, kind=None, parts=slice(0, P), chunks=slice(h, h + 1),
                            tokens=slice(16 + m * P, 16 + (m + 1) * P)) for m in range(2) for h in range(8)])
            residual("c_out", "mlp1", REAL)
            rms_ready()
            mlp_relu("mlp1", "mix0" if n_layers > 2 else None, REAL, n_layers == 2)
            if n_layers == 2:
                closing(9)
                return

            for k in range(KD):
                dve.wait_ge(turned, 10 + k)
                dve.tensor_copy(memory[:, k], tile_bank[(9 + k) % 4][:, 0:SEQ]).then_inc(turn_read, 1)
            rms_ready()
            rms_ready()
            turn_rs(rs_mem_tok, 2)

            for layer in range(n_layers - 2):
                if layer == 1:
                    rms_ready()
                for k in range(KD):
                    op[0] += 1
                    dve.wait_ge(operand_high, op[0])
                    dve.scalar_tensor_tensor(a_lo[:, k, 0:SEQ], memory[:, k], gain(f"memkv{layer}", k),
                                             a_hi[:, k, 0:SEQ].bitcast(F32), ALU.mult, ALU.subtract)\
                        .then_inc(operand_split, 1)

                def project_memory(i, t, gt):
                    if i < 2:
                        scaled(xk[:, 4 * i + t], t, gt, slice(0, SEQ), rs_mem)
                    else:
                        at_ = (i - 2) * BLOCK + t // 2 * HALF
                        scaled_tokens(xv[:, t % 2, at_:at_ + HALF], t, gt, rs_mem_tok[:, t % 2:t % 2 + 1])

                if layer == 0:
                    def project_ev(i, t, gt):
                        if i == 1 and t == 0:
                            turn_rs(rs_tok[:, 0:2], 2)
                        if i in (2, 4):
                            part = (mv, gv)[i // 4][:, t % 2, t // 2 * HALF:(t // 2 + 1) * HALF]
                            scaled_tokens(part, t, gt, rs_tok[:, t % 2:t % 2 + 1])
                        else:
                            scaled((mq, mk, None, gu)[i][:, t], t, gt, REAL)

                    stream("ev_in", project_ev)
                    stream("xkv0", project_memory)
                    dve.wait_ge(late_in, 16 * N_LATE_LOADS)
                    ang, tmp, cosa = angle[:, 0], angle[:, 2], angle[:, 1]
                    link(dve.tensor_copy(tmp, pos_i.bitcast(I32)))
                    link(dve.tensor_scalar(ang, tmp, table("inv_freq"), None, ALU.mult))
                    link(dve.tensor_scalar(tmp, ang, 1.0 / (2.0 * PI), ROUND, ALU.mult, ALU.add))
                    link(dve.tensor_scalar(tmp, tmp, -ROUND, None, ALU.add))
                    for part in TWO_PI_PARTS:
                        link(dve.scalar_tensor_tensor(ang, tmp, -part, ang, ALU.mult, ALU.add))
                    link(dve.tensor_scalar(cosa, ang, PI / 2, None, ALU.add))
                    link(dve.tensor_scalar(tmp, cosa, PI, -2.0 * PI, ALU.is_gt, ALU.mult))
                    link(dve.tensor_tensor(cosa, cosa, tmp, ALU.add))
                    link(dve.tensor_scalar(ang, ang, PI_BELOW, -PI_BELOW, ALU.min, ALU.max))
                    dve.tensor_scalar(cosa, cosa, PI_BELOW, -PI_BELOW, ALU.min, ALU.max).then_inc(M["rope_angle"], 1)
                    dve.wait_ge(M["rope_sin"], 1)
                    head_norms([([x[:, i]], [col(g)], [x[:, i]]) for x, g in ((mq, "ev_q"), (mk, "ev_k")) for i in range(4)],
                               rope=[(cos_m, sin_m)] * 8)
                    zeros_at = C["zeros"][0]
                    causal = cst[:, zeros_at:zeros_at + 2 * P]
                    attention([dict(nq=P, nk=(m + 1) * P, kind="causal", bias=causal[:, (1 - m) * P:2 * P],
                                    parts=slice(64 * (h % 2), 64 * (h % 2) + 64), chunks=slice(h // 2, h // 2 + 1),
                                    tokens=slice(16 + m * P, 16 + (m + 1) * P)) for m in range(2) for h in range(8)])
                    for i in range(2):
                        dve.wait_ge(M["ws_turned"], i + 1)
                        dve.tensor_tensor(ws_t[:, 4 * i:4 * i + 4], (b4, b5)[i][:].rearrange("p (g i) -> p g i", g=4),
                                          table("tri_f").unsqueeze(1).to_broadcast([P, 4, P]), ALU.mult)\
                            .then_inc(M["ws_read"], 1)
                    dve.wait_ge(M["gelu"], 8)
                    groups = gv.rearrange("p m (g d) -> p (m g) d", d=64)
                    wide = [P, 16, 64]
                    link(dve.tensor_reduce(g_mu, groups, AX.X, ALU.add))
                    link(dve.tensor_scalar(g_mu, g_mu, 1.0 / 64, None, ALU.mult))
                    dve.tensor_tensor(groups, groups, g_mu.unsqueeze(2).to_broadcast(wide), ALU.subtract)\
                        .then_inc(M["g_stat"], 1)
                    dve.wait_ge(M["g_sq"], 1)
                    dve.tensor_reduce(g_var, gt.rearrange("p m (g d) -> p (m g) d", d=64), AX.X, ALU.add)\
                        .then_inc(M["g_stat"], 1)
                    dve.wait_ge(M["g_ln"], 1)
                    link(dve.tensor_tensor(groups, groups, g_var.unsqueeze(2).to_broadcast(wide), ALU.mult))
                    link(dve.tensor_tensor(gv, gv, ln_g.unsqueeze(1).to_broadcast([P, 2, BLOCK]), ALU.mult))
                    dve.tensor_tensor(gv, gv, ln_b.unsqueeze(1).to_broadcast([P, 2, BLOCK]), ALU.add).then_inc(M["g_n"], 1)
                    for c in range(2):
                        dve.wait_ge(M["g_mixed"], c + 1)
                        link(dve.tensor_tensor(g_out(c), (b4, b5)[c][:].rearrange("p (g i) -> p g i", g=4), b_s, ALU.add))
                        dve.tensor_tensor(g_out(c), g_out(c), gu[:, :, c * P:(c + 1) * P], ALU.mult).then_inc(M["g_read"], 1)
                    for c in range(2):
                        ts = slice(16 + c * P, 16 + (c + 1) * P)
                        dve.wait_ge(M["g_read"], c + 1)
                        low_part(a_lo[:, 4:8, ts], g_out(c), a_hi[:, 4:8, ts])
                else:
                    def project_od(i, t, gt):
                        if i == 1 and t == 0:
                            turn_rs(rs_tok[:, 0:2], 2)
                        if i in (2, 3):
                            at_ = (i - 2) * BLOCK + t // 2 * HALF
                            scaled_tokens(lv[:, t % 2, at_:at_ + HALF], t, gt, rs_tok[:, t % 2:t % 2 + 1])
                        elif i < 2:
                            scaled((lq, lk)[i][:, t], t, gt, REAL)
                        else:
                            scaled(lr[:, 4 * (i - 4) + t], t, gt, REAL)

                    stream("od_in", project_od)
                    stream("xkv1", project_memory)
                    dve.wait_ge(M["l_low"], 1)
                    dve.tensor_tensor(squares[0:16, 0, 0:SEQ], b4[0:16, 0:SEQ], rs[0:16, REAL], ALU.mult)\
                        .then_inc(M["l_lowc"], 1)
                    for h in range(4):
                        dve.wait_ge(M["l_e1"], h + 1)
                        dve.tensor_scalar(la[:, h], (b5, b6)[h % 2][:, 0:SEQ], col("od_b", h), None, ALU.add)\
                            .then_inc(M["l_gate"], 1)
                    for h in range(4):
                        dve.wait_ge(M["l_exp"], h + 1)
                        link(dve.scalar_tensor_tensor(la[:, h], la[:, h], 0.0, l_tmp[:, h], ALU.min, ALU.subtract))
                    link(dve.tensor_scalar(la, la, 1.0 / 16, None, ALU.mult))
                    for h in range(4):
                        for c in range(4):
                            cs = slice(64 * c, 64 * c + 64)
                            ins = dve.tensor_tensor_scan(la[:, h, cs], ones[:, 0:64], la[:, h, cs], 0.0, ALU.mult, ALU.add)
                    ins.then_inc(M["l_scan"], 1)
                    dve.wait_ge(M["l_exp"], 5)
                    dve.scalar_tensor_tensor(lq.rearrange("p h t -> p (h t)"), lq.rearrange("p h t -> p (h t)"), 128.0 ** -0.5,
                                             l_tmp.rearrange("p h t -> p (h t)"), ALU.mult, ALU.mult)
                    dve.wait_ge(M["l_exp"], 6)
                    dve.tensor_tensor(ks_t, ks_t, lk, ALU.mult).then_inc(M["l_ks"], 1)
                    dve.wait_ge(M["l_exp"], 7)
                    dve.tensor_tensor(lk, lk, lo_t[:, 4:8], ALU.mult).then_inc(M["l_qk"], 1)
                    dve.wait_ge(M["l_att"], 1)
                    mats = att64.rearrange("p m h t -> p (m h) t")
                    cap = table("cap64").unsqueeze(1).to_broadcast([P, 8, 64])
                    ncap = table("ncap64").unsqueeze(1).to_broadcast([P, 8, 64])
                    link(dve.tensor_tensor(mats, b6[:].rearrange("p (m t) -> p m t", t=64), cap, ALU.min))
                    dve.tensor_tensor(mats, mats, ncap, ALU.max).then_inc(M["l_attc"], 1)
                    for c in range(4):
                        cs = slice(64 * c, 64 * c + 64)
                        dve.wait_ge(M["l_o"], c + 1)
                        dve.tensor_copy(lo_t[:, :, cs], b7[:].rearrange("p (r t) -> p r t", t=64)).then_inc(M["l_oc"], 1)
                        if c < 3:
                            dve.wait_ge(M["l_ds"], c + 1)
                            for half in range(2):
                                new = (b4, b5)[half][:].rearrange("p (h v) -> p h v", h=2)
                                part = l_state[:, 2 * half:2 * half + 2]
                                if c == 0:
                                    ins = dve.tensor_copy(part, new)
                                else:
                                    if half == 0:
                                        dve.wait_ge(M["l_dsr"], c)
                                    f = l_dec[:, 2 * half:2 * half + 2, c].unsqueeze(2).to_broadcast([P, 2, 256])
                                    link(dve.tensor_tensor(part, part, f, ALU.mult))
                                    ins = dve.tensor_tensor(part, part, new, ALU.add)
                            ins.then_inc(M["l_dsr"], 1)
                    dve.wait_ge(M["l_oc"], 4)
                    dve.wait_ge(M["silu_r"], 2)
                    head_norms([([lo_t[:, 2 * h + r] for r in range(2)], [col("od_o", 2 * h + r) for r in range(2)],
                                 [lo_t[:, 2 * h + r] for r in range(2)]) for h in range(4)],
                               gate=[lr[:, c] for c in range(8)], ts=REAL)
                residual(f"mix_out{layer}", f"memq{layer}", REAL)
                rms_ready()
                stream(f"xq{layer}", lambda i, t, gt: scaled(xq[:, 4 * i + t], t, gt, REAL))
                head_norms([([x[:, 2 * h + r] for r in range(2)], [col(g, 2 * layer + r) for r in range(2)],
                             [x[:, 2 * h + r] for r in range(2)]) for x, g in ((xk, "xa_k"), (xq, "xa_q")) for h in range(4)])
                attention([dict(nq=P, nk=SEQ, kind=None, parts=slice(0, P), chunks=slice(2 * h, 2 * h + 2),
                                tokens=slice(16 + m * P, 16 + (m + 1) * P)) for m in range(2) for h in range(4)])
                residual(f"x_out{layer}", f"ffn{layer}", REAL)
                rms_ready()
                mlp_swiglu(f"swiglu{layer}", "mix1" if layer == 0 and n_layers == 4 else None, REAL)
            closing(17)

        @block.gpsimd
        def _(pool):
            fin = [0]

            def rows(target, at, n, source):
                pool.dma_start(target[at:at + n], source).then_inc(rows_in, 16)

            for i, name in enumerate(("attn_norm_g", "mlp_norm_g", "norm_mix_2", "norm_mem_q_2", "norm_mem_kv_2", "norm_ffn_2")):
                rows(gain_rows, 16 * i, 16, w[name].rearrange("l (k p) -> (l k) p", p=P))
            R = LATE_ROWS
            rows(late_rows, R["conv"], 60, w["conv_w_a"].rearrange("o j (t p) -> (o j t) p", p=P))
            for name, key in (("a_out", "a_out_norm_g"), ("c_q", "c_q_norm_g"), ("c_k", "c_k_norm_g")):
                rows(late_rows, R[name], 1, w[key])
            for name, key in (("b_q", "b_q_norm_g"), ("b_k", "b_k_norm_g"), ("ev_q", "ev_q_gain_2"), ("ev_k", "ev_k_gain_2")):
                for half in range(2):
                    rows(late_rows[:, 64 * half:64 * half + 64], R[name], 1, w[key])
            for name, key in (("xa_q", "xa_q_gain_2"), ("xa_k", "xa_k_gain_2")):
                rows(late_rows, R[name], 4, w[key].rearrange("l (r p) -> (l r) p", p=P))
            rows(late_rows, R["od_o"], 8, w["od_o_gain_2"].rearrange("o h (r p) -> (o h r) p", p=P))
            rows(late_rows, R["od_b"], 4, w["od_b_g_2"].rearrange("o (r p) -> (o r) p", p=P))

            def misc(target, source):
                pool.dma_start(target, source).then_inc(misc_in, 16)

            misc(early[:, 0:ew], w["early_tables"])
            misc(a_log, w["a_log"].rearrange("o d h -> (o d h)").partition_broadcast(P))
            misc(dt_bias, w["dt_bias"].rearrange("o d h -> (o d h)").partition_broadcast(P))
            misc(sink, w["b_sink"].rearrange("o h -> (o h)").partition_broadcast(P))
            misc(wg1, w["od_w_g1_2"][0].rearrange("(k p) r -> p k r", p=P))

            def add_squares(ts=slice(0, T)):
                n = fin[0] // KD
                if n >= 1:
                    pool.wait_ge(norm_summed, n)
                for k in range(KD):
                    f = fin[0]
                    fin[0] += 1
                    pool.wait_ge(squared, f + 1)
                    if k == 0:
                        pool.tensor_copy(square_sum[:, ts], squares[:, f % 2, ts]).then_inc(sum_added, 1)
                    else:
                        pool.wait_ge(sum_added, f)
                        pool.tensor_tensor(square_sum[:, ts], square_sum[:, ts], squares[:, f % 2, ts], ALU.add)\
                            .then_inc(sum_added, 1)

            add_squares()
            y = 0
            for j, (c, d) in enumerate(BATCHES):
                n = TILES[c][1] - TILES[c][0]
                pool.wait_ge(M["d_n"], j + 1)
                for level in range(n_levels(n)):
                    i = levels_before(j) + level
                    if i >= 1:
                        if level == 1:
                            pool.wait_ge(M["d_x"], i)
                        else:
                            pool.wait_ge(M["d_w"], y)
                    mask = early_table(f"level{level}")[0:n, 0:n].unsqueeze(1).to_broadcast([n, 4, n])
                    pool.tensor_tensor(nb_[0:n, 0:4 * n].rearrange("p (h i) -> p h i", h=4),
                                       nn[0:n, 0:4 * n].rearrange("p (h i) -> p h i", h=4), mask, ALU.mult)\
                        .then_inc(M["d_nb"], 1)
                    if level >= 1:
                        y += 1
            add_squares()
            if n_layers > 1:
                add_squares()
                add_squares(REAL)
            if n_layers > 2:
                pool.dma_start(mem_rows, w["mem_2"][0].rearrange("(m p) d -> p m d", p=P)).then_inc(mem_in, 16)

                def later(target, source):
                    pool.dma_start(target, source).then_inc(late_in, 16)

                later(ln_g, w["ev_ln_g_2"].rearrange("o g d -> (o g d)").partition_broadcast(P))
                later(ln_b, w["ev_ln_b_2"].rearrange("o g d -> (o g d)").partition_broadcast(P))
                for half in range(2):
                    later(b_s[64 * half:64 * half + 64],
                          w["ev_b_s_2"][0].rearrange("(t two) i -> two t i", two=2)[half].partition_broadcast(64))
                later(pos_i.bitcast(I32), w["positions_2"].rearrange("o t -> (o t)").partition_broadcast(P))
                add_squares(REAL)
                add_squares(slice(0, SEQ))
                pool.wait_ge(turn_read, 17)
                pool.dma_start(ws_rows.rearrange("p a (b j) -> p (a b) j", j=P), w["ev_w_s_2"][0].rearrange("g i j -> i g j"))\
                    .then_inc(ws_in, 16)
                add_squares(REAL)
                pool.dma_start(wg2[0:16], w["od_w_g2_2"][0]).then_inc(wg_in, 16)
                add_squares(REAL)
            if n_layers > 3:
                for _ in range(3):
                    add_squares(REAL)
            turns = {1: 9, 2: 9, 3: 17, 4: 17}[n_layers]
            pool.wait_ge(turn_read, turns + 4)
            pool.dma_start(out[0].rearrange("(m p) d -> p m d", p=P), out_rows).then_inc(out_sent, 16)
            pool.wait_ge(out_sent, 16)


_INS = """x meta_tokens attn_norm_g mlp_norm_g w_in_ab conv_w_a a_log dt_bias a_out_norm_g b_q_norm_g b_k_norm_g b_sink
w_out_ab w_qkv_c c_q_norm_g c_k_norm_g w_out_c w_ff1 w_ff2 mem_2 positions_2 norm_mix_2 norm_mem_q_2 norm_mem_kv_2
norm_ffn_2 ev_w_in_2 ev_q_gain_2 ev_k_gain_2 ev_w_s_2 ev_b_s_2 ev_ln_g_2 ev_ln_b_2 ev_w_out_2 od_w_in_2 od_w_g1_2
od_w_g2_2 od_b_g_2 od_o_gain_2 od_w_out_2 xa_w_q_2 xa_w_kv_2 xa_q_gain_2 xa_k_gain_2 xa_w_out_2 ffn_w_gu_2
ffn_w_down_2""".split()


def kernel(**inputs):
    import concourse.bacc as _bacc
    from concourse.bass_utils import run_bass_kernel_spmd as _run

    nc = _bacc.Bacc("TRN2", target_bir_lowering=False, num_devices=1)
    arrays, w = {}, {}
    (tables, _), (early, _) = shape_constants()
    for name, a in [(n, inputs[n]) for n in _INS] + [("shape_tables", tables), ("early_tables", early)]:
        a = np.ascontiguousarray(a)
        arrays[f"in_{name}_dram"] = a
        w[name] = nc.dram_tensor(f"in_{name}_dram", a.shape, mybir.dt.from_np(a.dtype), kind="ExternalInput").ap()
    out = nc.dram_tensor("out_dram", (1, SEQ, D), F32, kind="ExternalOutput").ap()
    program(nc, w, out)
    return _run(nc, [arrays], core_ids=[0]).results[0]["out_dram"]
```

```python
from contextlib import ExitStack

import numpy as np

import concourse.bass as bass
from concourse import mybir

F32, F32R, I32 = mybir.dt.float32, mybir.dt.float32r, mybir.dt.int32
ALU, ACT, AX = mybir.AluOpType, mybir.ActivationFunctionType, mybir.AxisListType

P = 128
D = 1024
KD = D // P
NMETA, SEQ, GRID_W = 16, 256, 64
T = NMETA + SEQ
REAL = slice(NMETA, T)
TILES = [(0, NMETA), (NMETA, NMETA + P), (NMETA + P, T)]
WINDOW = 128
BLOCK = 512
HALF = BLOCK // 2
EPS = 1e-6
BIG = 1e30
HUGE = 3e38
D_FF = 4 * D
D_FF2 = 2816
UNIT = BLOCK
N_UNITS = D_FF // UNIT
A_HEADS = 4
LEVELS = 7
PI = float(np.pi)


def shape_constants():
    i = np.arange(P)
    tables = {}
    tables["ident"] = np.eye(P)
    tables["ones"] = np.ones((P, P))
    tables["blk64"] = (i[:, None] // 64 == i[None, :] // 64)
    swap = np.zeros((P, P))
    swap[i[::2] + 1, i[::2]] = -1.0
    swap[i[::2], i[::2] + 1] = 1.0
    tables["swap_pairs"] = swap
    swap = np.zeros((P, P))
    for base in (0, 64):
        for m in range(8):
            swap[base + m + 8, base + m] = -1.0
            swap[base + m, base + m + 8] = 1.0
    tables["swap_halves"] = swap
    upto = i[:, None] <= i[None, :]
    tables["tri_f"] = upto
    tables["tri_b"] = upto.T
    tables["neg_f"] = np.where(upto, 0.0, -BIG)
    tables["zeros"] = np.zeros((P, P))
    tables["neg_b"] = np.where(upto.T, 0.0, -BIG)
    cap = np.where((i[:, None] % 64) <= np.arange(64)[None, :], HUGE, 0.0)
    tables["cap64"] = cap
    tables["ncap64"] = -cap
    meta = np.arange(NMETA) - NMETA
    row = np.concatenate([meta, np.repeat(np.arange(SEQ // GRID_W), GRID_W)]).astype(np.float32)
    col = np.concatenate([meta, np.tile(np.arange(GRID_W), SEQ // GRID_W)]).astype(np.float32)
    freq = (np.float32(10000.0) ** (-np.arange(0, 64, 2, dtype=np.float32) / np.float32(64))).astype(np.float32)
    ang = np.concatenate([row[:, None] * freq, col[:, None] * freq], axis=-1).astype(np.float32)
    ang = np.repeat(ang, 2, axis=1).T.astype(np.float64)
    tables["cos_c"] = np.cos(ang)
    tables["sin_c"] = np.sin(ang)
    inv = (np.float32(500000.0) ** (-np.arange(8, dtype=np.float32) * np.float32(2.0) / np.float32(16))).astype(np.float32)
    tables["inv_freq"] = np.where(i % 64 < 16, inv[i % 8], 0.0)[:, None]
    tables["eps"] = np.full((P, 1), EPS)
    early = {}
    for level in range(LEVELS):
        b = 1 << level
        early[f"level{level}"] = ((i[:, None] // (2 * b) == i[None, :] // (2 * b))
                                  & (i[:, None] // b != i[None, :] // b))
    keys = np.arange(T)
    for m, (a, b) in enumerate(TILES):
        q = a + np.minimum(i, b - a - 1)
        dist = np.abs(q[:, None] - keys[None, :])
        early[f"ndist{m}"] = np.where(keys[None, :] < NMETA, 0.0, np.where(dist <= WINDOW, -dist, -BIG))

    def pack(named):
        at, place = 0, {}
        for name, table in named.items():
            place[name] = (at, table.shape[1])
            at += table.shape[1]
        return np.concatenate([np.asarray(t, np.float32) for t in named.values()], axis=1), place

    return pack(tables), pack(early)


class Phase:

    def __init__(self, first, blocks, up=None, down=None, token_blocks=(), done=None):
        self.first, self.blocks, self.n, self.up, self.down = first, blocks, len(blocks), up, down
        self.token_blocks, self.done = token_blocks, done


def weight_plan(w):
    phases, at = {}, 0

    def cols(x, c, width=BLOCK, rows=slice(None), into=0):
        return (into, width, x[rows, c:c + width].rearrange("(k p) n -> p k n", p=P))

    def add(name, blocks, **more):
        nonlocal at
        phases[name] = Phase(at, blocks, **more)
        at += len(blocks)

    x = w["w_in_ab"][0]
    add("ab_qkvz", [[cols(x, c)] for c in range(0, 2048, BLOCK)])
    add("ab_qb", [[cols(x, 2064)]])
    add("ab_kvb", [[cols(x, 2576, 256), cols(x, 2048, 128, into=256)]])
    add("ab_out", [[cols(w["w_out_ab"][0], c)] for c in (0, BLOCK)])

    def relu_mlp(layer):
        up = w["w_ff1"][layer].rearrange("(k p) (g n) -> g p k n", p=P, n=UNIT)
        down = w["w_ff2"][layer].rearrange("(g k p) n -> g p k n", p=P, k=UNIT // P)
        blocks = [[(0, BLOCK, up[0])]]
        for i in range(N_UNITS):
            if i + 1 < N_UNITS:
                blocks.append([(0, BLOCK, up[i + 1])])
            blocks.append([(None, 0, down[i])])
        add(f"mlp{layer}", blocks, up=up, down=down)

    relu_mlp(0)
    x = w["w_qkv_c"][0]
    add("c_q", [[cols(x, c)] for c in (0, BLOCK)])
    add("c_kv", [[cols(x, 1024)]], done=(1, 2, 4, 4))
    add("c_out", [[cols(w["w_out_c"][0], c)] for c in (0, BLOCK)])
    relu_mlp(1)

    def second(layer):
        if layer == 0:
            add("ev_in", [[cols(w["ev_w_in_2"][0], c)] for c in range(0, 2560, BLOCK)], token_blocks=(2, 4))
        else:
            add("od_in", [[cols(w["od_w_in_2"][0], c)] for c in range(0, 3072, BLOCK)], token_blocks=(2, 3))
        add(f"xkv{layer}", [[cols(w["xa_w_kv_2"][layer], c)] for c in range(0, 2048, BLOCK)], token_blocks=(2, 3))
        out = w["ev_w_out_2"][0] if layer == 0 else w["od_w_out_2"][0]
        add(f"mix_out{layer}", [[cols(out, c)] for c in (0, BLOCK)])
        add(f"xq{layer}", [[cols(w["xa_w_q_2"][layer], c)] for c in (0, BLOCK)])
        add(f"x_out{layer}", [[cols(w["xa_w_out_2"][layer], c)] for c in (0, BLOCK)])
        gu, down = w["ffn_w_gu_2"][layer], w["ffn_w_down_2"][layer]
        blocks = []
        for c in range(0, D_FF2, HALF):
            blocks.append([cols(gu, c, HALF), cols(gu, D_FF2 + c, HALF, into=HALF)])
            if c % UNIT == 0 and c >= UNIT:
                blocks.append([(None, 0, down[c - UNIT:c].rearrange("(k p) n -> p k n", p=P))])
        blocks.append([(None, 0, down[D_FF2 // UNIT * UNIT:].rearrange("(k p) n -> p k n", p=P))])
        add(f"swiglu{layer}", blocks)

    for layer in range(2):
        second(layer)
    return phases, at


NORMS = ["attn0", "attn1", "mlp0", "mlp1", "mix0", "mix1", "memq0", "memq1", "memkv0", "memkv1", "ffn0", "ffn1"]
LATE_ROWS = {"conv": 0, "a_out": 60, "b_q": 61, "b_k": 62, "c_q": 63, "c_k": 64, "ev_q": 65, "ev_k": 66,
             "xa_q": 67, "xa_k": 71, "od_o": 75, "od_b": 83}
N_LATE_ROWS = 87
N_ROW_LOADS, N_MISC_LOADS, N_LATE_LOADS = 22, 5, 5
ROUND = 1.5 * 2.0 ** 23
PI_BELOW = float(np.nextafter(np.float32(PI), np.float32(0)))
TWO_PI_PARTS = [6.28125, 0.0019350051879882812, 3.0199159819122e-07]


def program(nc, w, out):
    phases, n_blocks = weight_plan(w)
    (_, C), (_, E) = shape_constants()
    (cw, ew) = (sum(n for _, n in C.values()), sum(n for _, n in E.values()))
    with ExitStack() as ctx:
        def sb(name, shape, dtype=F32):
            return ctx.enter_context(nc.sbuf_tensor(name, shape, dtype))

        def sem(name):
            return ctx.enter_context(nc.semaphore(name))

        raw = sb("raw", [P, 2, KD, BLOCK])
        w_hi = sb("w_hi", [P, 4, KD * P], F32R)
        w_lo = sb("w_lo", [P, 4, KD * P], F32R)
        hidden = sb("hidden", [P, KD, T])
        u_hi, u_lo = sb("u_hi", [P, KD, T], F32R), sb("u_lo", [P, KD, T], F32R)
        a_hi, a_lo = sb("a_hi", [P, KD, T], F32R), sb("a_lo", [P, KD, T], F32R)
        cst = sb("cst", [P, cw])
        early = sb("early", [P, 2048])
        gains = sb("gains", [P, 8 * len(NORMS)])
        late = sb("late", [P, N_LATE_ROWS])
        rs = sb("rs", [P, T])[:]
        rs_tok = sb("rs_tok", [P, 3])[:]
        rs_mem, rs_mem_tok = sb("rs_mem", [P, SEQ])[:], sb("rs_mem_tok", [P, 2])[:]
        squares, square_sum = sb("squares", [P, 2, T]), sb("square_sum", [P, T])
        work = sb("work", [P, 2656])
        att = sb("att", [P, 1856])
        mx = sb("mx", [P, 14304])
        small = sb("small", [P, 768])
        psum = [ctx.enter_context(nc.psum_tensor(f"ps{i}", [P, 512], F32)) for i in range(8)]
        tile_bank, b4, b5, b6, b7 = psum[:4], psum[4], psum[5], psum[6], psum[7]

        def area(tensor, at, *shape):
            n = int(np.prod(shape))
            ap = tensor[:, at:at + n]
            if len(shape) == 2:
                ap = ap.rearrange("p (a b) -> p a b", a=shape[0])
            if len(shape) == 3:
                ap = ap.rearrange("p (a b c) -> p a b c", a=shape[0], b=shape[1])
            return ap

        def table(name):
            at, n = C[name]
            return cst[:, at:at + n]

        def early_table(name):
            at, n = E[name]
            return early[:, at:at + n]

        ident, ones, blk64, eps = table("ident"), table("ones"), table("blk64"), table("eps")
        memory = area(early, 0, KD, SEQ)

        def gain(norm, k):
            c = 8 * NORMS.index(norm) + k
            return gains[:, c:c + 1]

        def col(name, k=0):
            c = LATE_ROWS[name] + k
            return late[:, c:c + 1]

        ff_z, ff_s, ff_a = area(work, 0, 2, T), area(work, 544, 2, T), area(work, 1088, 2, T)
        hn_sq, hn_r, hn_n, hn_t = area(work, 0, 2, 512), area(work, 1024, 2, T), area(work, 1568, 2, T), area(work, 2112, 2, T)
        at_s, at_p, at_pt = area(att, 0, 2, T), area(att, 544, 2, T), area(att, 1088, 2, 3, P)
        at_m, at_nm, at_den, at_es, at_inv = (area(small, 2 * i, 2, 1) for i in range(5))
        x_rows, meta_rows = area(mx, 0, 2, D), area(mx, 2 * D, D)
        gain_rows, late_rows = area(mx, 3 * D, P), area(mx, 3 * D + P, P)
        mem_rows = area(mx, 8192, 2, D)
        PAD = T + 4
        xa = area(mx, 0, 12, PAD)
        v_tok, k_tok = area(mx, 0, 3, 4, P), area(mx, 1536, 3, 4, P)
        za = area(mx, 3312, 4, T)
        qb, kb, kdup, vb = area(mx, 4400, 4, T), area(mx, 5488, T), area(mx, 5760, 2, T), area(mx, 6304, 3, P)
        qkv = area(mx, 6688, 12, T)
        o_delta = qkv[:, 8:12]
        inner = area(mx, 9952, 2176 + 2176)
        qe_f, qe_b = area(mx, 5488, 1152), att
        state = area(mx, 4400, 2, 4, P)
        dm, nn, xt, wt, nb_ = (area(work, 512 * i, 512) for i in range(5))
        scan_r, scan_v, scan_k = dm, nn, xt
        hab, beta, decay = area(small, 16, 3, 16), area(small, 64, 3, 8), area(small, 88, 3, 8)
        gcc, necc, kdf = area(small, 112, 3, 8), area(small, 136, 3, 8), area(small, 160, 3, 8)
        egl = area(small, 184, 3, 8)
        d_tmp, d_tmp2 = area(small, 208, 3, 8), area(small, 232, 3, 8)
        a_log, dt_bias, sink = area(small, 256, 8), area(small, 264, 8), area(small, 272, 8)
        neg_a = area(small, 280, 8)
        qc, kc, vc = area(mx, 0, 8, SEQ), area(mx, 2048, 2, T), area(mx, 2592, 3, SEQ)
        xk, xv, xq = area(mx, 0, 8, SEQ), area(mx, 2048, 2, D), area(mx, 4096, 8, SEQ)
        mq, mk, mv = area(mx, 4096, 4, SEQ), area(mx, 5120, 4, SEQ), area(mx, 6144, 2, BLOCK)
        gu, gv, gt = area(mx, 7168, 4, SEQ), area(mx, 8192, 2, BLOCK), area(mx, 9216, 2, BLOCK)
        ws_rows, ws_t = gt, area(mx, 10240, 8, P)
        ln_g, ln_b, b_s = area(mx, 11264, BLOCK), area(mx, 11776, BLOCK), area(mx, 12288, 4, P)
        cos_m, sin_m = area(mx, 12800, SEQ), area(mx, 13056, SEQ)
        angle = area(att, 0, 4, SEQ)
        pos_i = area(mx, 13312, SEQ)
        lq, lk, lv, lr = area(mx, 4096, 4, SEQ), area(mx, 5120, 4, SEQ), area(mx, 6144, 2, D), area(mx, 8192, 8, SEQ)
        la, lo_t = area(mx, 10240, 4, SEQ), area(mx, 11264, 8, SEQ)
        wg1, wg2 = area(small, 300, KD, 16), area(mx, 13312, BLOCK)
        kst, att64 = area(att, 0, 2, 4, P), area(att, 1024, 2, 4, 64)
        l_state, l_tmp, ks_t = area(work, 0, 4, 256), area(work, 1024, 4, SEQ), lo_t[:, 0:4]
        g_mu, g_var, l_dec = area(small, 16, 16), area(small, 32, 16), area(small, 48, 4, 4)
        out_rows = area(mx, 0, 2, D)

        x_in, cst_in, rows_in, misc_in, late_in, mem_in, ws_in, wg_in = (
            sem(n) for n in "x_in cst_in rows_in misc_in late_in mem_in ws_in wg_in".split())
        raw_in = [sem("raw_in0"), sem("raw_in1")]
        high_split, low_split = sem("high_split"), sem("low_split")
        tile_summed, tile_read = sem("tile_summed"), sem("tile_read")
        turned, turn_read = sem("turned"), sem("turn_read")
        operand_high, operand_split = sem("operand_high"), sem("operand_split")
        squared, sum_added = sem("squared"), sem("sum_added")
        norm_summed, norm_ln, rs_ready = sem("norm_summed"), sem("norm_ln"), sem("rs_ready")
        rs_turned, rs_tok_ready = sem("rs_turned"), sem("rs_tok_ready")
        ff_ready, silu_ready = sem("ff_ready"), sem("silu_ready")
        hn_squared, hn_summed, hn_ln, hn_rs, hn_scaled = (
            sem(n) for n in "hn_squared hn_summed hn_ln hn_rs hn_scaled".split())
        hn_swapped, hn_roped, hn_gated = sem("hn_swapped"), sem("hn_roped"), sem("hn_gated")
        at_scored, at_biased, at_max, at_exp, at_prob = (
            sem(n) for n in "at_scored at_biased at_max at_exp at_prob".split())
        at_turned, at_copied, at_summed = sem("at_turned"), sem("at_copied"), sem("at_summed")
        dve_step, act_step, out_sent = sem("dve_step"), sem("act_step"), sem("out_sent")
        M = {n: sem(n) for n in (
            "conv_done d_copied d_cum d_cum_read d_diff d_dm d_egr d_first d_gate_exp d_gates d_gk d_kdec "
            "d_ks d_n d_nb d_o d_o_read d_r d_rows d_s d_s_read d_turned d_v d_vnew d_w d_w_copied d_x d_y "
            "g_ln g_mixed g_n g_read g_sq g_stat gelu kv_dup l_att l_attc l_ds l_dsr l_e1 l_exp l_gate l_ks "
            "l_kst l_kstc l_low l_lowc l_o l_oc l_qk l_scan rope_angle rope_sin silu_done silu_r ws_read "
            "ws_turned ").split()}

        landed_at, tile_at, wide, quarter_done, so_far = [], [0], [], [], [0, 0]
        for ph in phases.values():
            for i, loads in enumerate(ph.blocks):
                so_far[len(landed_at) % 2] += 16 * len(loads)
                landed_at.append(so_far[len(landed_at) % 2])
                wide.append(loads[0][0] is None)
                done = ph.done or ((2, 4, 6, 8) if wide[-1] else (2, 2, 4, 4) if i in ph.token_blocks else (1, 2, 3, 4))
                quarter_done.append([tile_at[-1] + n for n in done])
                tile_at.append(tile_at[-1] + (8 if wide[-1] else 4))
        LOOP_BLOCKS, LOOP_TILES, LOOP_LANDED, LOOP_UNITS = 4, 24, 32, 2

        def looped(count, per_iteration, g):
            return count if g is None else per_iteration * g + count

        def raw_quarter(b, q):
            slot = raw[:, b % 2]
            if wide[b]:
                slot = slot.rearrange("p (k two) n -> p k (two n)", two=2)
            n = (2 if wide[b] else 1) * P
            return slot[:, :, q * n:(q + 1) * n]

        def quarter(part, b, q):
            return part[:, q].rearrange("p (k n) -> p k n", n=(2 if wide[b] else 1) * P)

        def attention_out(operand, x):
            return operand[x["parts"], x["chunks"], x["tokens"]]

        def attention_bank(x):
            n = x["chunks"].stop - x["chunks"].start
            return b7[x["parts"], 0:n * P].rearrange("p (c q) -> p c q", q=P)[:, :, 0:x["nq"]]

        def g_out(c):
            return gt[:, c].rearrange("p (g i) -> p g i", g=4)

        def window_units():
            for m in range(3):
                for h in range(8):
                    yield m, h

        BATCHES = [(c, d) for c in range(3) for d in range(2)]
        SCAN = [(c, d, i == 0, i == 2) for i in range(3) for d, c in ((0, i), (1, 2 - i))]

        def n_levels(n):
            return n.bit_length() - 1

        def levels_before(j):
            return sum(n_levels(TILES[c][1] - TILES[c][0]) for c, _ in BATCHES[:j])

        def batch_place(j):
            return sum(4 * (TILES[c][1] - TILES[c][0]) for c, _ in BATCHES[:j])

        def batch_size(j):
            c = BATCHES[j][0]
            return 4 * (TILES[c][1] - TILES[c][0])

        def inverse(j):
            return inner[:, 2176 + batch_place(j):2176 + batch_place(j) + batch_size(j)]

        def inner_product(j):
            return inner[:, batch_place(j):batch_place(j) + batch_size(j)]

        def decayed_queries(c, d):
            s, e = TILES[c]
            return (qe_f, qe_b)[d][:, 4 * s:4 * e]

        def delta_turns():
            for source in (8, 4):
                for m in range(3):
                    yield m, source

        def ws_rows_at(g):
            return ws_rows[:, g // 4, g % 4 * P:(g % 4 + 1) * P]

        def first_of(name):
            return phases[name].first

        block = ctx.enter_context(nc.Block())

        @block.sync
        def _(sp):
            sp.dma_start(x_rows, w["x"][0].rearrange("(m p) d -> p m d", p=P)).then_inc(x_in, 16)
            sp.dma_start(meta_rows[0:NMETA], w["meta_tokens"]).then_inc(x_in, 16)
            sp.dma_start(cst[:], w["shape_tables"]).then_inc(cst_in, 16)

            def load(b, loads, g=None):
                if b >= 2:
                    sp.wait_ge(low_split, looped(4 * (b - 1), 4 * LOOP_BLOCKS, g))
                for into, width, source in loads:
                    chunks = source.shape[1]
                    slot = raw[:, b % 2]
                    if wide[b]:
                        target = slot.rearrange("p (k two) n -> p k (two n)", two=2)[:, 0:chunks]
                    else:
                        target = slot[:, 0:chunks, into:into + width]
                    sp.dma_start(target, source).then_inc(raw_in[b % 2], 16)

            for name, ph in phases.items():
                if ph.up is not None:
                    load(ph.first, ph.blocks[0])
                    with sp.Fori(0, (N_UNITS - 2) // LOOP_UNITS) as g:
                        load(ph.first + 1, [(0, BLOCK, ph.up[2 * g + 1])], g)
                        load(ph.first + 2, [(None, 0, ph.down[2 * g])], g)
                        load(ph.first + 3, [(0, BLOCK, ph.up[2 * g + 2])], g)
                        load(ph.first + 4, [(None, 0, ph.down[2 * g + 1])], g)
                    for i in range(ph.n - 3, ph.n):
                        load(ph.first + i, ph.blocks[i])
                else:
                    for i, loads in enumerate(ph.blocks):
                        load(ph.first + i, loads)

        @block.tensor
        def _(pe):
            op = [0]

            def split_ready(b, q, g=None):
                pe.wait_ge(low_split, looped(4 * b + q + 1, 4 * LOOP_BLOCKS, g))

            def transposed_tile(q, x, ts, bank, ready=None):
                n = ts.stop - ts.start
                for k in range(KD):
                    if ready is not None:
                        pe.wait_ge(operand_split, ready + k + 1)
                    for i, (wx, ux) in enumerate(((w_hi, 0), (w_hi, 1), (w_lo, 0))):
                        mm = pe.matmul(bank[:, 0:n], wx[:, q, k * P:(k + 1) * P], x[ux][:, k, ts],
                                       start=k == 0 and i == 0, stop=k == KD - 1 and i == 2)
                return mm

            def token_tile(q, n_quarters, n, x, ts, bank, at):
                for k in range(KD):
                    for i, (ux, wx) in enumerate(((0, w_hi), (0, w_lo), (1, w_hi))):
                        mm = pe.matmul(bank[:, at:at + n_quarters * n].rearrange("p (q n) -> p q n", n=n), x[ux][:, k, ts],
                                       wx[:, q:q + n_quarters, k * P:k * P + n],
                                       start=k == 0 and i == 0, stop=k == KD - 1 and i == 2)
                return mm

            def bank_free(b, t, g=None):
                if tile_at[b] + t >= 4:
                    pe.wait_ge(tile_read, looped(tile_at[b] + t - 3, LOOP_TILES, g))

            def block_t(b, x, ts, ready=None, norm=None, g=None):
                for t in range(4):
                    if t == 2 and norm is not None:
                        norm_sum(norm)
                    split_ready(b, t, g)
                    bank_free(b, t, g)
                    transposed_tile(t, x, ts, tile_bank[t], ready if t == 0 else None)\
                        .then_inc(tile_summed, 1)

            def block_wide(b, unit, chunks, ts, ready, g=None):
                n = ts.stop - ts.start
                for t in range(8):
                    if t % 2 == 0:
                        split_ready(b, t // 2, g)
                    bank_free(b, t, g)
                    cols = slice(t % 2 * P, (t % 2 + 1) * P)
                    hi, lo = quarter(w_hi, b, t // 2), quarter(w_lo, b, t // 2)
                    for k in range(chunks):
                        if t == 0:
                            pe.wait_ge(operand_split, looped(ready + k + 1, 4 * LOOP_UNITS, g))
                        at_k = 4 * (unit % 2) + k
                        pe.matmul(tile_bank[t % 4][:, 0:n], hi[:, k, cols], a_hi[:, at_k, ts], start=k == 0, stop=False)
                        pe.matmul(tile_bank[t % 4][:, 0:n], hi[:, k, cols], a_lo[:, at_k, ts], start=False, stop=False)
                        mm = pe.matmul(tile_bank[t % 4][:, 0:n], lo[:, k, cols], a_hi[:, at_k, ts], start=False,
                                       stop=k == chunks - 1)
                    mm.then_inc(tile_summed, 1)

            def block_v(b, x, offset):
                for t in range(4):
                    if t % 2 == 0:
                        split_ready(b, t + 1)
                    bank_free(b, t)
                    a = offset + t % 2 * P
                    token_tile(t // 2 * 2, 2, P, x, slice(a, a + P), tile_bank[t], 0).then_inc(tile_summed, 1)

            u, a = (u_hi, u_lo), (a_hi, a_lo)

            norms = [0]

            def norm_sum(ts=slice(0, T)):
                n = norms[0]
                norms[0] += 1
                pe.wait_ge(sum_added, 8 * (n + 1))
                pe.matmul(b7[:, 0:ts.stop - ts.start], ones, square_sum[:, ts], start=True, stop=True)\
                    .then_inc(norm_summed, 1)

            turns = [0]

            def norm_turn(source, starts):
                pe.wait_ge(rs_ready, norms[0])
                if turns[0]:
                    pe.wait_ge(rs_tok_ready, turns[0])
                for i, s in enumerate(starts):
                    mm = pe.transpose(b6[:, i * P:(i + 1) * P], source[:, s:s + P], ident)
                turns[0] += 1
                mm.then_inc(rs_turned, 1)

            hn = [0]
            ropes = [0]

            def hn_sum(u_, tiles, n, matrix):
                pe.wait_ge(hn_squared, u_ + 1)
                if u_ >= 2:
                    pe.wait_ge(hn_ln, u_ - 1)
                for i in range(tiles):
                    mm = pe.matmul((b4, b5)[u_ % 2][:, 0:n], matrix, hn_sq[:, u_ % 2, i * n:(i + 1) * n],
                                   start=i == 0, stop=i == tiles - 1)
                mm.then_inc(hn_summed, 1)

            def hn_swap(u_, r, n, swap):
                pe.wait_ge(hn_scaled, u_ + 1)
                if r >= 2:
                    pe.wait_ge(hn_roped, r - 1)
                pe.matmul((b6, b7)[r % 2][:, 0:n], swap, hn_n[:, r % 2, 0:n], start=True, stop=True)\
                    .then_inc(hn_swapped, 1)

            def head_norms(units, swap=None):
                base, r0 = hn[0], ropes[0]
                for i, (tiles, n, matrix) in enumerate(units):
                    hn_sum(base + i, tiles, n, matrix)
                    if swap is not None and i >= 1:
                        hn_swap(base + i - 1, r0 + i - 1, units[i - 1][1], swap)
                if swap is not None:
                    hn_swap(base + len(units) - 1, r0 + len(units) - 1, units[-1][1], swap)
                    ropes[0] += len(units)
                hn[0] += len(units)

            at = [0]

            def attention(units):
                base, split0, n = at[0], op[0], len(units)

                def scores(i):
                    x, v = units[i], base + i
                    if v >= 2:
                        pe.wait_ge(at_exp, v - 1)
                    for c, (q, k) in enumerate(zip(x["q"], x["k"])):
                        mm = pe.matmul((b4, b5)[v % 2][0:x["nq"], 0:x["nk"]], q, k, start=c == 0,
                                       stop=c == len(x["q"]) - 1)
                    mm.then_inc(at_scored, 1)

                def turn(i):
                    x, v = units[i], base + i
                    pe.wait_ge(at_prob, v + 1)
                    if v >= 1:
                        pe.wait_ge(at_copied, v)
                    for c, (rows, first, _) in enumerate(x["keys"]):
                        mm = pe.transpose(b6[0:rows, c * P:c * P + x["nq"]],
                                          at_p[0:x["nq"], v % 2, first:first + rows], ident[0:x["nq"], 0:x["nq"]])
                    mm.then_inc(at_turned, 1)

                def values(i):
                    x, v = units[i], base + i
                    pe.wait_ge(at_copied, v + 1)
                    pe.wait_ge(operand_split, split0 + i)
                    nv = len(x["keys"][0][2])
                    for r in range(nv):
                        for c, (rows, _, vs) in enumerate(x["keys"]):
                            mm = pe.matmul(b7[x["parts"], r * P:r * P + x["nq"]], vs[r],
                                           at_pt[0:rows, v % 2, c, 0:x["nq"]], start=c == 0,
                                           stop=c == len(x["keys"]) - 1)
                    mm.then_inc(at_summed, 1)

                scores(0)
                for i in range(n):
                    if i + 1 < n:
                        scores(i + 1)
                    turn(i)
                    if i >= 1:
                        values(i - 1)
                values(n - 1)
                at[0] += n
                op[0] += n

            def out_product(name, ts):
                pe.wait_ge(operand_split, op[0])
                for i in range(phases[name].n):
                    block_t(phases[name].first + i, a, ts)

            def mlp_relu(name, ts):
                first, ready = phases[name].first, hidden_ready()
                base = op[0]
                block_t(first, u, ts, ready=ready, norm=ts)
                with pe.Fori(0, (N_UNITS - 2) // LOOP_UNITS) as g:
                    block_t(first + 1, u, ts, g=g)
                    block_wide(first + 2, 0, 4, ts, base, g)
                    block_t(first + 3, u, ts, g=g)
                    block_wide(first + 4, 1, 4, ts, base + 4, g)
                last = first + phases[name].n - 3
                block_t(last, u, ts)
                for i in (N_UNITS - 2, N_UNITS - 1):
                    block_wide(last + i - N_UNITS + 3, i, 4, ts, base + 4 * i)
                op[0] += D_FF // P

            def mlp_swiglu(name, ts):
                b, ready = phases[name].first, hidden_ready()
                base = op[0]
                for i in range(D_FF2 // HALF):
                    block_t(b, u, ts, ready=ready if i == 0 else None, norm=ts if i == 0 else None)
                    b += 1
                    if i % 2 == 0 and i >= 2:
                        block_wide(b, i // 2 - 1, 4, ts, base + 2 * i - 4)
                        b += 1
                block_wide(b, D_FF2 // UNIT, D_FF2 % UNIT // P, ts, base + D_FF2 // UNIT * 4)
                op[0] += D_FF2 // P

            def hidden_ready():
                op[0] += KD
                return op[0] - KD

            def gated_delta():
                for i, (m, source) in enumerate(delta_turns()):
                    s, e = TILES[m]
                    if i >= 2:
                        pe.wait_ge(M["d_copied"], i - 1)
                    if i == 0:
                        pe.wait_ge(hn_scaled, hn[0])
                    for h in range(A_HEADS):
                        mm = pe.transpose((b4, b5)[i % 2][0:e - s, h * P:(h + 1) * P],
                                          qkv[:, source + h, s:e], ident)
                    mm.then_inc(M["d_turned"], 1)
                pe.wait_ge(M["d_gates"], 1)
                for c, (s, e) in enumerate(TILES):
                    n = e - s
                    for d in range(2):
                        mm = pe.matmul(b6[0:n, 8 * c + 4 * d:8 * c + 4 * d + 4], table(("tri_f", "tri_b")[d])[0:n, 0:n],
                                       decay[0:n, c, 4 * d:4 * d + 4], start=True, stop=True)
                mm.then_inc(M["d_cum"], 1)
                pe.wait_ge(M["d_cum_read"], 1)
                pe.wait_ge(M["d_copied"], 6)
                y = 0
                for j, (c, d) in enumerate(BATCHES):
                    s, e = TILES[c]
                    n = e - s
                    if j >= 1:
                        pe.wait_ge(M["d_egr"], j)
                        pe.wait_ge(M["d_n"], j)
                    for h in range(A_HEADS):
                        g = decay[0:n, c, 4 * d + h:4 * d + h + 1].to_broadcast([n, P])
                        mm = pe.matmul(b4[:, h * n:(h + 1) * n], g, table(("tri_f", "tri_b")[d])[0:n, 0:n],
                                       start=True, stop=True)
                    mm.then_inc(M["d_rows"], 1)
                    if j >= 1:
                        pe.wait_ge(M["d_x"], levels_before(j))
                    for h in range(A_HEADS):
                        pe.matmul(b5[0:n, h * n:(h + 1) * n], qkv[:, 4 + h, s:e], qkv[:, 4 + h, s:e],
                                  start=True, stop=True)
                    for h in range(A_HEADS):
                        mm = pe.matmul(b6[0:n, h * n:(h + 1) * n], qkv[:, 4 + h, s:e], qkv[:, h, s:e],
                                       start=True, stop=True)
                    mm.then_inc(M["d_gk"], 1)
                    x = inverse(j)
                    for level in range(n_levels(n)):
                        i = levels_before(j) + level
                        pe.wait_ge(M["d_nb"], i + 1)
                        hs = [slice(h * n, (h + 1) * n) for h in range(A_HEADS)]
                        if level == 0:
                            pe.wait_ge(M["d_n"], j + 1)
                            for h in hs:
                                mm = pe.transpose(b5[0:n, h], nb_[0:n, h], ident[0:n, 0:n])
                            mm.then_inc(M["d_y"], 1)
                            continue
                        pe.wait_ge(M["d_x"], i)
                        for h in hs:
                            mm = pe.matmul(b7[0:n, h], nb_[0:n, h], xt[0:n, h], start=True, stop=True)
                        mm.then_inc(M["d_w"], 1)
                        y += 1
                        pe.wait_ge(M["d_w_copied"], y)
                        for h in hs:
                            mm = pe.matmul(b5[0:n, h], wt[0:n, h], x[0:n, h], start=True, stop=True)
                        if level < n_levels(n) - 1:
                            for h in hs:
                                mm = pe.matmul(b6[0:n, h], x[0:n, h], wt[0:n, h], start=True, stop=True)
                        mm.then_inc(M["d_y"], 1)
                pe.wait_ge(M["d_x"], levels_before(6))
                for j, (c, d, first, lastone) in enumerate(SCAN):
                    s, e = TILES[c]
                    n = e - s
                    x = inverse(BATCHES.index((c, d)))
                    qx = inner_product(BATCHES.index((c, d)))
                    qe = decayed_queries(c, d)
                    if j >= 1:
                        pe.wait_ge(M["d_r"], j)
                    if not first:
                        pe.wait_ge(M["d_s_read"], j - 1)
                        for h in range(A_HEADS):
                            mm = pe.matmul(b4[0:n, h * P:(h + 1) * P], qkv[:, 4 + h, s:e], state[:, d, h],
                                           start=True, stop=True)
                        mm.then_inc(M["d_ks"], 1)
                    pe.wait_ge(M["d_r"], j + 1)
                    if j >= 1:
                        pe.wait_ge(M["d_vnew"], j)
                    for h in range(A_HEADS):
                        mm = pe.matmul(b5[0:n, h * P:(h + 1) * P], x[0:n, h * n:(h + 1) * n],
                                       scan_r[0:n, h * P:(h + 1) * P], start=True, stop=True)
                    mm.then_inc(M["d_v"], 1)
                    pe.wait_ge(M["d_vnew"], j + 1)
                    if j >= 1:
                        pe.wait_ge(M["d_o_read"], j)
                    for h in range(A_HEADS):
                        mm = pe.matmul(b6[:, h * n:(h + 1) * n], scan_v[0:n, h * P:(h + 1) * P],
                                       qx[0:n, h * n:(h + 1) * n], start=True, stop=first)
                        if not first:
                            mm = pe.matmul(b6[:, h * n:(h + 1) * n], state[:, d, h], qe[:, h * n:(h + 1) * n],
                                           start=False, stop=True)
                    mm.then_inc(M["d_o"], 1)
                    if not lastone:
                        pe.wait_ge(M["d_kdec"], j + 1)
                        if j >= 1:
                            pe.wait_ge(M["d_s_read"], j)
                        for h in range(A_HEADS):
                            mm = pe.matmul(b7[:, h * P:(h + 1) * P], scan_k[0:n, h * P:(h + 1) * P],
                                           scan_v[0:n, h * P:(h + 1) * P], start=True, stop=True)
                        mm.then_inc(M["d_s"], 1)
                pe.wait_ge(M["d_o_read"], 6)

            def spatial_gating():
                pe.wait_ge(ws_in, 16)
                for i in range(2):
                    for g in range(4):
                        mm = pe.transpose((b4, b5)[i][:, g * P:(g + 1) * P], ws_rows_at(4 * i + g), ident)
                    mm.then_inc(M["ws_turned"], 1)
                pe.wait_ge(M["ws_read"], 2)
                pe.wait_ge(M["g_n"], 1)
                for c in range(2):
                    for g in range(8):
                        half = slice(64 * (g % 2), 64 * (g % 2) + 64)
                        mm = pe.matmul((b4, b5)[c][half, g // 2 * P:(g // 2 + 1) * P], gv[:, c, g * 64:(g + 1) * 64],
                                       ws_t[:, g], start=True, stop=True)
                    mm.then_inc(M["g_mixed"], 1)

            def linear_attention():
                pe.wait_ge(wg_in, 16)
                for i in range(2 * KD):
                    mm = pe.matmul(b4[0:16, 0:SEQ], wg1[:, i % KD], u[i // KD][:, i % KD, REAL].bitcast(F32),
                                   start=i == 0, stop=i == 2 * KD - 1)
                mm.then_inc(M["l_low"], 1)
                pe.wait_ge(M["l_lowc"], 1)
                for h in range(4):
                    if h >= 2:
                        pe.wait_ge(M["l_gate"], h - 1)
                    pe.matmul((b5, b6)[h % 2][:, 0:SEQ], wg2[0:16, h * P:(h + 1) * P], squares[0:16, 0, 0:SEQ],
                              start=True, stop=True).then_inc(M["l_e1"], 1)
                pe.wait_ge(M["l_ks"], 1)
                pe.wait_ge(M["l_gate"], 4)
                for m in range(2):
                    for h in range(4):
                        mm = pe.transpose((b4, b5)[m][:, h * P:(h + 1) * P], ks_t[:, h, m * P:(m + 1) * P], ident)
                    mm.then_inc(M["l_kst"], 1)
                pe.wait_ge(M["l_qk"], 1)
                for c in range(4):
                    half, cs = slice(64 * (c % 2), 64 * (c % 2) + 64), slice(64 * c, 64 * c + 64)
                    for h in range(4):
                        at_c = (c // 2 * 4 + h) * 64
                        mm = pe.matmul(b6[half, at_c:at_c + 64], lk[:, h, cs], lq[:, h, cs], start=True, stop=True)
                mm.then_inc(M["l_att"], 1)
                pe.wait_ge(M["l_attc"], 1)
                pe.wait_ge(M["l_kstc"], 2)
                for c in range(4):
                    half, cs = slice(64 * (c % 2), 64 * (c % 2) + 64), slice(64 * c, 64 * c + 64)
                    m = c // 2
                    if c >= 1:
                        pe.wait_ge(M["l_oc"], c)
                        pe.wait_ge(M["l_dsr"], c)
                    for h in range(4):
                        for r in range(2):
                            vs = slice((2 * h + r) * P, (2 * h + r + 1) * P)
                            o = b7[:, (2 * h + r) * 64:(2 * h + r + 1) * 64]
                            mm = pe.matmul(o, lv[half, m, vs], att64[half, m, h], start=True, stop=c == 0)
                            if c >= 1:
                                mm = pe.matmul(o, l_state[:, h, r * P:(r + 1) * P], lq[:, h, cs], start=False, stop=True)
                    mm.then_inc(M["l_o"], 1)
                    if c < 3:
                        for h in range(4):
                            mm = pe.matmul((b4, b5)[h // 2][:, h % 2 * 256:(h % 2 + 1) * 256], kst[half, m, h],
                                           lv[half, m, h * 256:(h + 1) * 256], start=True, stop=True)
                        mm.then_inc(M["l_ds"], 1)
                pe.wait_ge(M["l_oc"], 4)

            def closing():
                pe.wait_ge(tile_read, tile_at[n_blocks])
                for m in range(2):
                    for k4 in range(2):
                        turn_rows(tile_bank, [(k * P, P, hidden[:, 4 * k4 + k, NMETA + m * P:NMETA + (m + 1) * P]) for k in range(4)])

            pe.wait_ge(cst_in, 16)
            pe.wait_ge(rows_in, 16 * N_ROW_LOADS)
            n_turn = [0]

            def turn_rows(banks, jobs):
                n = n_turn[0]
                if n >= len(banks):
                    pe.wait_ge(turn_read, n - len(banks) + 1)
                for lo, rows, source in jobs:
                    mm = pe.transpose(banks[n % len(banks)][:, lo:lo + rows], source, ident[0:rows, 0:rows])
                mm.then_inc(turned, 1)
                n_turn[0] += 1

            turn_rows(tile_bank, [(0, 96, gain_rows[0:96]), (P, N_LATE_ROWS, late_rows[0:N_LATE_ROWS])])
            pe.wait_ge(x_in, 32)
            for k in range(KD):
                ks = slice(k * P, (k + 1) * P)
                turn_rows(tile_bank, [(0, NMETA, meta_rows[0:NMETA, ks])]
                          + [(NMETA + m * P, P, x_rows[:, m, ks]) for m in range(2)])
            pe.wait_ge(turn_read, n_turn[0])

            full = slice(0, T)
            block_t(first_of("ab_qkvz"), u, full, ready=hidden_ready(), norm=full)
            norm_turn(rs, [0, 16, 144])
            for i in range(1, 4):
                block_t(first_of("ab_qkvz") + i, u, slice(0, T))
            block_t(first_of("ab_qb"), u, slice(0, T))
            b = first_of("ab_kvb")
            split_ready(b, 0)
            bank_free(b, 0)
            transposed_tile(0, u, slice(0, T), tile_bank[0]).then_inc(tile_summed, 1)
            split_ready(b, 1)
            bank_free(b, 1)
            for m, s in enumerate((0, 16, 144)):
                mm = token_tile(1, 1, P, u, slice(s, s + P), tile_bank[1], m * P)
            mm.then_inc(tile_summed, 1)
            split_ready(b, 3)
            bank_free(b, 2)
            for m, s in enumerate((0, 16, 144)):
                mm = token_tile(2, 1, 16, u, slice(s, s + P), tile_bank[2], m * 16)
            mm.then_inc(tile_summed, 2)

            head_norms([(1, T, blk64)] * 5)
            pe.wait_ge(hn_scaled, hn[0])
            pe.wait_ge(M["kv_dup"], 1)
            pe.wait_ge(tile_read, tile_at[b + 1])
            units = []
            for m, h in window_units():
                lo, hi = TILES[m]
                half = slice(64 * (h % 2), 64 * (h % 2) + 64)
                g = h // 4
                units.append(dict(
                    q=[qb[half, h // 2, lo:hi]], k=[kdup[half, g]], nq=hi - lo, nk=T, parts=half,
                    keys=[(e - s, s, [vb[0:e - s, c, 64 * g:64 * g + 64]]) for c, (s, e) in enumerate(TILES)]))
            attention(units)

            pe.wait_ge(M["silu_done"], 12)
            head_norms([(1, T, ones)] * 8)
            gated_delta()
            head_norms([(1, T, ones)] * 4)
            op[0] += 4
            out_product("ab_out", slice(0, T))
            mlp_relu("mlp0", full)

            ready = hidden_ready()
            for i in range(2):
                block_t(first_of("c_q") + i, u, REAL, ready=ready if i == 0 else None, norm=full if i == 0 else None)
                if i == 0:
                    norm_turn(rs, [0, 16, 144])
            pe.wait_ge(mem_in, 16)
            for k in range(KD):
                turn_rows((b4, b5), [(m * P, P, mem_rows[:, m, k * P:k * P + P]) for m in range(2)])
            b = first_of("c_kv")
            for t in range(2):
                split_ready(b, t)
                bank_free(b, t)
                transposed_tile(t, u, slice(0, T), tile_bank[t]).then_inc(tile_summed, 1)
            split_ready(b, 3)
            bank_free(b, 2)
            for m, s in enumerate((16, 144)):
                mm = token_tile(2, 2, P, u, slice(s, s + P), tile_bank[2], m * HALF)
            mm.then_inc(tile_summed, 1)
            bank_free(b, 3)
            token_tile(2, 2, P, u, slice(0, P), tile_bank[3], 0).then_inc(tile_summed, 1)
            norm_sum(slice(0, SEQ))
            norm_turn(rs_mem, [0, P])
            pe.wait_ge(turn_read, n_turn[0])
            pe.wait_ge(rs_tok_ready, turns[0])
            head_norms([(1, SEQ, ones)] * 8 + [(1, T, ones)] * 2, table("swap_pairs"))
            pe.wait_ge(hn_roped, ropes[0])
            pe.wait_ge(tile_read, tile_at[b + 1])
            units = []
            for m in range(2):
                for h in range(8):
                    g = h // 4
                    units.append(dict(
                        q=[qc[:, h, m * P:m * P + P]], k=[kc[:, g]], nq=P, nk=T, parts=slice(0, P),
                        keys=[(e - s, s, [vc[0:e - s, c, g * P:g * P + P]]) for c, (s, e) in enumerate(TILES)]))
            attention(units)
            out_product("c_out", REAL)
            mlp_relu("mlp1", REAL)

            for layer in range(2):
                ready = hidden_ready()
                name = ("ev_in", "od_in")[layer]
                b = first_of(name)
                if layer == 0:
                    block_t(b, u, REAL, ready=ready, norm=REAL)
                    norm_turn(rs, [16, 144])
                    block_t(b + 1, u, REAL)
                    block_v(b + 2, u, NMETA)
                    block_t(b + 3, u, REAL)
                    block_v(b + 4, u, NMETA)
                else:
                    block_t(b, u, REAL, ready=ready, norm=REAL)
                    norm_turn(rs, [16, 144])
                    block_t(b + 1, u, REAL)
                    block_v(b + 2, u, NMETA)
                    block_v(b + 3, u, NMETA)
                    block_t(b + 4, u, REAL)
                    block_t(b + 5, u, REAL)
                op[0] += KD
                pe.wait_ge(operand_split, op[0])
                b = first_of(f"xkv{layer}")
                for i in range(2):
                    block_t(b + i, a, slice(0, SEQ))
                for i in range(2):
                    block_v(b + 2 + i, a, 0)
                if layer == 0:
                    head_norms([(1, SEQ, blk64)] * 8, table("swap_halves"))
                    pe.wait_ge(hn_roped, ropes[0])
                    units = []
                    for m in range(2):
                        for h in range(8):
                            half = slice(64 * (h % 2), 64 * (h % 2) + 64)
                            units.append(dict(
                                q=[mq[half, h // 2, m * P:m * P + P]], k=[mk[half, h // 2, 0:(m + 1) * P]], nq=P,
                                nk=(m + 1) * P, parts=half,
                                keys=[(P, c * P, [mv[:, c, 64 * h:64 * h + 64]]) for c in range(m + 1)]))
                    attention(units)
                    spatial_gating()
                    op[0] += 2
                else:
                    linear_attention()
                    head_norms([(2, SEQ, ones)] * 4)
                    op[0] += 8
                out_product(f"mix_out{layer}", REAL)
                b = first_of(f"xq{layer}")
                block_t(b, u, REAL, ready=hidden_ready(), norm=REAL)
                block_t(b + 1, u, REAL)
                head_norms([(2, SEQ, ones)] * 8)
                pe.wait_ge(hn_scaled, hn[0])
                units = []
                for m in range(2):
                    for h in range(4):
                        units.append(dict(
                            q=[xq[:, 2 * h + c, m * P:m * P + P] for c in range(2)],
                            k=[xk[:, 2 * h + c] for c in range(2)], nq=P, nk=SEQ, parts=slice(0, P),
                            keys=[(P, c * P, [xv[:, c, (2 * h + r) * P:(2 * h + r + 1) * P] for r in range(2)])
                                  for c in range(2)]))
                attention(units)
                out_product(f"x_out{layer}", REAL)
                mlp_swiglu(f"swiglu{layer}", REAL)
            closing()

        @block.scalar
        def _(act):
            op, fin, step = [0], [0], [0]

            def link(ins):
                step[0] += 1
                ins.then_inc(act_step, 1)
                act.wait_ge(act_step, step[0])

            def split_high(b, q, g=None):
                if b >= n_blocks:
                    return
                if q == 0:
                    act.wait_ge(raw_in[b % 2], looped(landed_at[b], LOOP_LANDED, g))
                if b >= 1:
                    act.wait_ge(tile_summed, looped(quarter_done[b - 1][q], LOOP_TILES, g))
                act.activation(quarter(w_hi, b, q), raw_quarter(b, q), ACT.Copy).then_inc(high_split, 1)

            def stream(name, evac, start=0, n=None):
                ph = phases[name]
                for i in range(start, ph.n if n is None else start + n):
                    for t in range(4):
                        evac(i, t)
                        split_high(ph.first + i + 1, t)

            def nothing(i, t):
                pass

            def finish_chunk(k, norm, ready, ts, source=None):
                f = fin[0]
                fin[0] += 1
                x = hidden[:, k, ts] if source is None else source
                act.wait_ge(*ready)
                act.activation(u_hi[:, k, ts], x, ACT.Copy, scale=gain(norm, k)).then_inc(operand_high, 1)
                op[0] += 1
                if f >= 2:
                    act.wait_ge(sum_added, f - 1)
                act.activation(squares[:, f % 2, ts], x, ACT.Square).then_inc(squared, 1)

            norms = [0]

            def norm_rs(target, n, scale=1.0 / D):
                norms[0] += 1
                act.wait_ge(norm_summed, norms[0])
                act.activation(target, b7[:, 0:n], ACT.Ln, bias=eps, scale=scale).then_inc(norm_ln, 1)
                act.wait_ge(norm_ln, norms[0])
                act.activation(target, target, ACT.Exp, scale=-0.5).then_inc(rs_ready, 1)

            hn = [0]

            def head_norms(units):
                base, n = hn[0], len(units)

                def square(i):
                    source, columns, _, tokens, wait = units[i]
                    v = base + i
                    act.wait_ge(*wait)
                    if v >= 2:
                        act.wait_ge(hn_summed, v - 1)
                    act.activation(hn_sq[:, v % 2, 0:columns], source, ACT.Square).then_inc(hn_squared, 1)

                def scale(i):
                    _, _, mean, tokens, _ = units[i]
                    v = base + i
                    act.wait_ge(hn_summed, v + 1)
                    if v >= 2:
                        act.wait_ge(hn_scaled, v - 1)
                    act.activation(hn_r[:, v % 2, 0:tokens], (b4, b5)[v % 2][:, 0:tokens], ACT.Ln, bias=eps,
                                   scale=mean).then_inc(hn_ln, 1)
                    act.wait_ge(hn_ln, v + 1)
                    act.activation(hn_r[:, v % 2, 0:tokens], hn_r[:, v % 2, 0:tokens], ACT.Exp, scale=-0.5)\
                        .then_inc(hn_rs, 1)

                square(0)
                for i in range(n):
                    if i + 1 < n:
                        square(i + 1)
                    scale(i)
                hn[0] += n

            at = [0]

            def attention(units):
                base, n = at[0], len(units)

                def exponent(i):
                    x, v = units[i], base + i
                    q, s = slice(0, x["nq"]), v % 2
                    act.wait_ge(at_max, v + 1)
                    if v >= 2:
                        act.wait_ge(at_turned, v - 1)
                        act.wait_ge(at_prob, v - 1)
                    logits = at_s[q, s, 0:x["nk"]] if x["kind"] else (b4, b5)[s][q, 0:x["nk"]]
                    if x["kind"] == "window":
                        act.activation(at_es[q, s], sink[q, x["head"]:x["head"] + 1], ACT.Exp, bias=at_nm[q, s])
                    act.activation(at_p[q, s, 0:x["nk"]], logits, ACT.Exp, bias=at_nm[q, s], accum_out=at_den[q, s])\
                        .then_inc(at_exp, 1)

                def copy(i):
                    x, v = units[i], base + i
                    act.wait_ge(at_turned, v + 1)
                    if v >= 2:
                        act.wait_ge(at_summed, v - 1)
                    rows = x["rows"]
                    c = 0
                    while c < len(rows):
                        e = c
                        while e < len(rows) and rows[e] == rows[c]:
                            e += 1
                        ins = act.activation(at_pt[0:rows[c], v % 2, c:e, 0:x["nq"]],
                                             b6[0:rows[c], c * P:e * P].rearrange("p (c q) -> p c q", q=P)[:, :, 0:x["nq"]],
                                             ACT.Copy)
                        c = e
                    ins.then_inc(at_copied, 1)

                def result(i):
                    x, v = units[i], base + i
                    act.wait_ge(at_summed, v + 1)
                    act.activation(attention_out(a_hi, x), attention_bank(x), ACT.Copy).then_inc(operand_high, 1)
                    op[0] += 1

                exponent(0)
                for i in range(n):
                    if i + 1 < n:
                        exponent(i + 1)
                    copy(i)
                    if i >= 1:
                        result(i - 1)
                result(n - 1)
                at[0] += n

            def residual(name, norm, ts):
                def evac(i, t):
                    finish_chunk(4 * i + t, norm, (tile_read, tile_at[phases[name].first + i] + t + 1), ts)
                stream(name, evac)

            ff = [0]

            def mlp_relu(name, norm, ts):
                first, base, f0 = phases[name].first, op[0], ff[0]

                def up(b, unit, g=None):
                    for t in range(4):
                        act.wait_ge(ff_ready, looped(f0 + 4 * unit + t + 1, 4 * LOOP_UNITS, g))
                        act.activation(a_hi[:, 4 * (unit % 2) + t, ts], ff_a[:, t % 2, ts], ACT.Copy).then_inc(operand_high, 1)
                        split_high(b + 1, t, g)

                def down(b, g=None):
                    for q in range(4):
                        split_high(b + 1, q, g)

                up(first, 0)
                with act.Fori(0, (N_UNITS - 2) // LOOP_UNITS) as g:
                    up(first + 1, 1, g)
                    down(first + 2, g)
                    up(first + 3, 2, g)
                    down(first + 4, g)
                last = first + phases[name].n - 3
                up(last, N_UNITS - 1)
                down(last + 1)
                op[0] = base + D_FF // P
                ff[0] += D_FF // P
                closing_down(last + 2, norm, ts)

            def closing_down(b, norm, ts):
                for k in range(KD):
                    if norm is not None:
                        finish_chunk(k, norm, (tile_read, tile_at[b] + k + 1), ts)
                    if k % 2 == 1:
                        split_high(b + 1, k // 2)

            def mlp_swiglu(name, norm, ts):
                b, n = phases[name].first, ts.stop - ts.start
                for i in range(D_FF2 // HALF):
                    for t in range(4):
                        if t < 2:
                            act.wait_ge(tile_read, tile_at[b] + t + 1)
                            act.activation(ff_s[:, t, 0:n], ff_z[:, t, 0:n], ACT.Silu).then_inc(silu_ready, 1)
                        else:
                            ff[0] += 1
                            act.wait_ge(ff_ready, ff[0])
                            act.activation(a_hi[:, 2 * (i % 4) + t - 2, ts], ff_a[:, t - 2, 0:n], ACT.Copy)\
                                .then_inc(operand_high, 1)
                            op[0] += 1
                        split_high(b + 1, t)
                    b += 1
                    if i % 2 == 0 and i >= 2:
                        for q in range(4):
                            split_high(b + 1, q)
                        b += 1
                log_and_exp()
                closing_down(b, norm, ts)

            def log_and_exp():
                nc.scalar.preload_act_table_set("natural_log_exp_and_others")

            log_and_exp()
            for q in range(4):
                split_high(0, q)
            act.wait_ge(cst_in, 16)
            for k in range(KD):
                finish_chunk(k, "attn0", (turn_read, k + 2), slice(0, T))
            norm_rs(rs, T)

            def conv(i, t):
                c = 4 * i + t
                if c < 12:
                    act.wait_ge(M["conv_done"], c + 1)
                    act.activation(qkv[:, c], qkv[:, c], ACT.Silu).then_inc(M["silu_done"], 1)

            stream("ab_qkvz", conv)
            log_and_exp()
            stream("ab_qb", nothing)
            stream("ab_kvb", nothing)
            b = tile_at[phases["ab_qb"].first]
            head_norms([(qb[:, i], T, 1.0 / 64, T, (tile_read, b + i + 1)) for i in range(4)]
                       + [(kb, T, 1.0 / 64, T, (tile_read, b + 5))])
            act.wait_ge(hn_scaled, hn[0])
            for g in range(2):
                for half in range(2):
                    ins = act.activation(kdup[64 * half:64 * half + 64, g], kb[64 * g:64 * g + 64], ACT.Copy)
            ins.then_inc(M["kv_dup"], 1)
            act.wait_ge(misc_in, 16 * N_MISC_LOADS)
            attention([dict(nq=TILES[m][1] - TILES[m][0], nk=T, kind="window", head=h, rows=[16, P, P],
                            parts=slice(64 * (h % 2), 64 * (h % 2) + 64), chunks=slice(4 + h // 2, 5 + h // 2),
                            tokens=slice(*TILES[m])) for m, h in window_units()])
            act.wait_ge(M["silu_done"], 12)
            head_norms([(qkv[:, i], T, 1.0, T, (M["silu_done"], 12)) for i in range(8)])

            act.activation(neg_a, a_log, ACT.Exp)
            act.activation(beta, hab[:, :, 0:8], ACT.Exp, scale=-1.0)
            act.wait_ge(M["d_first"], 1)
            link(act.activation(d_tmp2, d_tmp, ACT.Abs))
            link(act.activation(d_tmp2, d_tmp2, ACT.Exp, scale=-1.0))
            act.activation(d_tmp2, d_tmp2, ACT.Ln, bias=ones[:, 0:1]).then_inc(M["d_gate_exp"], 1)
            for i, (m, source) in enumerate(delta_turns()):
                n = TILES[m][1] - TILES[m][0]
                act.wait_ge(M["d_turned"], i + 1)
                act.activation((v_tok if source == 8 else k_tok)[0:n, m], (b4, b5)[i % 2][0:n, 0:4 * P].rearrange(
                    "p (h d) -> p h d", h=4), ACT.Copy).then_inc(M["d_copied"], 1)
            act.wait_ge(M["d_cum_read"], 1)
            act.activation(necc[0:NMETA, 0], gcc[0:NMETA, 0], ACT.Exp)
            act.activation(necc[:, 1:3], gcc[:, 1:3], ACT.Exp).then_inc(M["d_gate_exp"], 1)
            y = 0
            for j, (c, d) in enumerate(BATCHES):
                n = TILES[c][1] - TILES[c][0]
                act.wait_ge(M["d_diff"], j + 1)
                act.activation(decayed_queries(c, d), b4[:, 0:4 * n], ACT.Exp).then_inc(M["d_egr"], 1)
                act.activation(kdf[0:n, c, 4 * d:4 * d + 4], d_tmp[0:n, c, 4 * d:4 * d + 4], ACT.Exp)
                act.activation(dm[0:n, 0:4 * n], dm[0:n, 0:4 * n], ACT.Exp).then_inc(M["d_dm"], 1)
                for level in range(1, n_levels(n)):
                    y += 1
                    act.wait_ge(M["d_w"], y)
                    act.activation(wt[0:n, 0:4 * n], b7[0:n, 0:4 * n], ACT.Copy).then_inc(M["d_w_copied"], 1)
            act.wait_ge(tile_read, tile_at[phases["ab_qkvz"].first] + 16)
            act.activation(za, za, ACT.Silu).then_inc(M["silu_r"], 1)
            log_and_exp()

            def gated_norms(units, chunk_of):
                head_norms(units)
                for c in chunk_of:
                    gated[0] += 1
                    act.wait_ge(hn_gated, gated[0])
                    act.activation(a_hi[:, c, gts], hn_t[:, (gated[0] - 1) % 2, 0:gts.stop - gts.start], ACT.Copy)\
                        .then_inc(operand_high, 1)
                    op[0] += 1

            gated, gts = [0], slice(0, T)
            gated_norms([(o_delta[:, h], T, 1.0 / P, T, (M["d_o_read"], 6)) for h in range(4)], range(4))
            residual("ab_out", "mlp0", slice(0, T))
            norm_rs(rs, T)
            mlp_relu("mlp0", "attn1", slice(0, T))

            norm_rs(rs, T)
            stream("c_q", nothing)
            for k in range(KD):
                f = fin[0]
                fin[0] += 1
                act.wait_ge(turn_read, 10 + k)
                act.wait_ge(sum_added, f - 1)
                act.activation(squares[:, f % 2, 0:SEQ], memory[:, k], ACT.Square).then_inc(squared, 1)
            stream("c_kv", nothing)
            norm_rs(rs_mem, SEQ)
            b = tile_at[phases["c_q"].first]
            head_norms([(qc[:, i], SEQ, 1.0 / P, SEQ, (tile_read, b + i + 1)) for i in range(8)]
                       + [(kc[:, i], T, 1.0 / P, T, (tile_read, b + 9 + i)) for i in range(2)])
            attention([dict(nq=P, nk=T, kind=None, rows=[16, P, P], parts=slice(0, P), chunks=slice(h, h + 1),
                            tokens=slice(16 + m * P, 16 + (m + 1) * P)) for m in range(2) for h in range(8)])
            residual("c_out", "mlp1", REAL)
            norm_rs(rs[:, REAL], SEQ)
            mlp_relu("mlp1", "mix0", REAL)

            for layer in range(2):
                def memory_operand():
                    for k in range(KD):
                        act.activation(a_hi[:, k, 0:SEQ], memory[:, k], ACT.Copy, scale=gain(f"memkv{layer}", k))\
                            .then_inc(operand_high, 1)
                        op[0] += 1

                norm_rs(rs[:, REAL], SEQ)
                if layer == 0:
                    first = tile_at[phases["ev_in"].first]

                    def gelu(i, t):
                        if i == 3:
                            act.wait_ge(tile_read, first + 4 * i + t + 1)
                            act.activation(gu[:, t], gu[:, t], ACT.Gelu).then_inc(M["gelu"], 1)
                        if i == 4:
                            act.wait_ge(tile_read, first + 4 * i + t + 1)
                            part = gv[:, t % 2, t // 2 * HALF:(t // 2 + 1) * HALF]
                            act.activation(part, part, ACT.Gelu).then_inc(M["gelu"], 1)

                    stream("ev_in", gelu, 0, 2)
                    memory_operand()
                    stream("ev_in", gelu, 2)
                    stream("xkv0", nothing)
                    act.wait_ge(M["rope_angle"], 1)
                    act.activation(sin_m, angle[:, 0], ACT.Sin)
                    act.activation(cos_m, angle[:, 1], ACT.Sin).then_inc(M["rope_sin"], 1)
                    log_and_exp()
                    head_norms([(x[:, i], SEQ, 1.0 / 64, SEQ, (tile_read, first + 4 * j + i + 1))
                                for j, x in enumerate((mq, mk)) for i in range(4)])
                    attention([dict(nq=P, nk=(m + 1) * P, kind="causal", rows=[P] * (m + 1),
                                    parts=slice(64 * (h % 2), 64 * (h % 2) + 64), chunks=slice(h // 2, h // 2 + 1),
                                    tokens=slice(16 + m * P, 16 + (m + 1) * P)) for m in range(2) for h in range(8)])
                    act.wait_ge(M["g_stat"], 1)
                    act.wait_ge(M["ws_turned"], 2)
                    act.activation(gt, gv, ACT.Square).then_inc(M["g_sq"], 1)
                    act.wait_ge(M["g_stat"], 2)
                    link(act.activation(g_var, g_var, ACT.Ln, bias=eps, scale=1.0 / 64))
                    act.activation(g_var, g_var, ACT.Exp, scale=-0.5).then_inc(M["g_ln"], 1)
                    for c in range(2):
                        act.wait_ge(M["g_read"], c + 1)
                        act.activation(a_hi[:, 4:8, 16 + c * P:16 + (c + 1) * P], g_out(c), ACT.Copy)\
                            .then_inc(operand_high, 1)
                        op[0] += 1
                else:
                    first = tile_at[phases["od_in"].first]
                    stream("od_in", nothing, 0, 2)
                    memory_operand()
                    stream("od_in", nothing, 2)
                    stream("xkv1", nothing)
                    act.wait_ge(tile_read, first + 24)
                    act.activation(lr, lr, ACT.Silu).then_inc(M["silu_r"], 1)
                    log_and_exp()
                    for h in range(4):
                        act.wait_ge(M["l_gate"], h + 1)
                        link(act.activation(l_tmp[:, h], la[:, h], ACT.Abs))
                        link(act.activation(l_tmp[:, h], l_tmp[:, h], ACT.Exp, scale=-1.0))
                        act.activation(l_tmp[:, h], l_tmp[:, h], ACT.Ln, bias=ones[:, 0:1]).then_inc(M["l_exp"], 1)
                    act.wait_ge(M["l_scan"], 1)
                    act.activation(l_tmp, la, ACT.Exp).then_inc(M["l_exp"], 1)
                    for h in range(4):
                        for c in range(4):
                            cs = slice(64 * c, 64 * c + 64)
                            ins = act.activation(ks_t[:, h, cs], la[:, h, cs], ACT.Exp, scale=-1.0,
                                                 bias=la[:, h, 64 * c + 63:64 * c + 64])
                    ins.then_inc(M["l_exp"], 1)
                    act.activation(l_dec, la.rearrange("p h (c t) -> p h c t", t=64)[:, :, :, 63], ACT.Exp)
                    act.activation(lo_t[:, 4:8], la, ACT.Exp, scale=-1.0).then_inc(M["l_exp"], 1)
                    for m in range(2):
                        act.wait_ge(M["l_kst"], m + 1)
                        act.activation(kst[:, m], (b4, b5)[m][:, 0:4 * P].rearrange("p (h d) -> p h d", h=4), ACT.Copy)\
                            .then_inc(M["l_kstc"], 1)
                    gts = REAL
                    gated_norms([(lo_t[:, 2 * h:2 * h + 2].rearrange("p a t -> p (a t)"), 2 * SEQ, 1.0 / 256, SEQ,
                                  (M["l_oc"], 4)) for h in range(4)], range(8))
                residual(f"mix_out{layer}", f"memq{layer}", REAL)
                norm_rs(rs[:, REAL], SEQ)
                stream(f"xq{layer}", nothing)
                b, bk = tile_at[phases[f"xq{layer}"].first], tile_at[phases[f"xkv{layer}"].first]
                head_norms([(x[:, 2 * h:2 * h + 2].rearrange("p a t -> p (a t)"), 2 * SEQ, 1.0 / 256, SEQ,
                             (tile_read, at_ + 2 * h + 2)) for x, at_ in ((xk, bk), (xq, b)) for h in range(4)])
                attention([dict(nq=P, nk=SEQ, kind=None, rows=[P, P], parts=slice(0, P), chunks=slice(2 * h, 2 * h + 2),
                                tokens=slice(16 + m * P, 16 + (m + 1) * P)) for m in range(2) for h in range(4)])
                residual(f"x_out{layer}", f"ffn{layer}", REAL)
                norm_rs(rs[:, REAL], SEQ)
                mlp_swiglu(f"swiglu{layer}", "mix1" if layer == 0 else None, REAL)

        @block.vector
        def _(dve):
            op, fin, step = [0], [0], [0]

            def link(ins):
                step[0] += 1
                ins.then_inc(dve_step, 1)
                dve.wait_ge(dve_step, step[0])

            def split_low(b, q, g=None):
                b, q = (b, q) if q >= 0 else (b - 1, 3)
                if b >= n_blocks:
                    return
                dve.wait_ge(high_split, looped(4 * b + q + 1, 4 * LOOP_BLOCKS, g))
                dve.tensor_tensor(quarter(w_lo, b, q), raw_quarter(b, q), quarter(w_hi, b, q).bitcast(F32), ALU.subtract)\
                    .then_inc(low_split, 1)

            def stream(name, evac, start=0, n=None):
                ph = phases[name]
                for i in range(start, ph.n if n is None else start + n):
                    b = ph.first + i
                    for t in range(4):
                        evac(i, t, tile_at[b] + t)
                        split_low(b + 1, t - 1)

            def low_part(target, source, high):
                op[0] += 1
                dve.wait_ge(operand_high, op[0])
                dve.tensor_tensor(target, source, high.bitcast(F32), ALU.subtract).then_inc(operand_split, 1)

            def finish_low(k, norm, ts, source=None):
                op[0] += 1
                dve.wait_ge(operand_high, op[0])
                dve.scalar_tensor_tensor(u_lo[:, k, ts], hidden[:, k, ts], gain(norm, k),
                                         u_hi[:, k, ts].bitcast(F32), ALU.mult, ALU.subtract).then_inc(operand_split, 1)

            norms, turns = [0], [0]

            def rms_ready():
                norms[0] += 1
                dve.wait_ge(rs_ready, norms[0])

            def turn_rs(target, n):
                turns[0] += 1
                dve.wait_ge(rs_turned, turns[0])
                dve.tensor_copy(target, b6[:, 0:n * P].rearrange("p (m c) -> p m c", c=P)[:, :, 0]).then_inc(rs_tok_ready, 1)
                dve.wait_ge(rs_tok_ready, turns[0])

            def scaled(target, t, gt, ts, scale=None):
                dve.wait_ge(tile_summed, gt + 1)
                n = ts.stop - ts.start
                dve.tensor_tensor(target, tile_bank[t][:, 0:n], rs[:, ts] if scale is None else scale, ALU.mult)\
                    .then_inc(tile_read, 1)

            def scaled_tokens(target, t, gt, column):
                dve.wait_ge(tile_summed, gt + 1)
                dve.tensor_scalar(target, tile_bank[t][:, 0:HALF], column, None, ALU.mult).then_inc(tile_read, 1)

            def add_tile(k, t, gt, ts, first=False):
                dve.wait_ge(tile_summed, gt + 1)
                dve.wait_ge(tile_read, gt)
                dve.tensor_tensor(hidden[:, k, ts], tile_bank[t][:, 0:ts.stop - ts.start], hidden[:, k, ts], ALU.add)\
                    .then_inc(tile_read, 1)

            hn, ropes, gated = [0], [0], [0]

            def head_norms(units, rope=None, gate=None, ts=slice(0, T)):
                base, r0, n = hn[0], ropes[0], len(units)
                chunk = [0]

                def scale(i):
                    sources, gains_, targets = units[i]
                    v = base + i
                    dve.wait_ge(hn_rs, v + 1)
                    if rope is not None and r0 + i >= 2:
                        dve.wait_ge(hn_swapped, r0 + i - 1)
                    for source, g, target in zip(sources, gains_, targets):
                        w_ = source.shape[1]
                        if rope is not None:
                            target = hn_n[:, (r0 + i) % 2, 0:w_]
                        ins = dve.scalar_tensor_tensor(target, source, g, hn_r[:, v % 2, 0:w_], ALU.mult, ALU.mult)
                    ins.then_inc(hn_scaled, 1)

                def rotate(i):
                    r, target = r0 + i, units[i][2][0]
                    w_ = target.shape[1]
                    cos, sin = rope[i]
                    dve.wait_ge(hn_scaled, base + i + 1)
                    dve.tensor_tensor(target, hn_n[:, r % 2, 0:w_], cos, ALU.mult)
                    dve.wait_ge(hn_swapped, r + 1)
                    link(dve.tensor_tensor(hn_t[:, r % 2, 0:w_], (b6, b7)[r % 2][:, 0:w_], sin, ALU.mult))
                    dve.tensor_tensor(target, target, hn_t[:, r % 2, 0:w_], ALU.add).then_inc(hn_roped, 1)

                def gates(i):
                    dve.wait_ge(hn_scaled, base + i + 1)
                    for target in units[i][2]:
                        c = gated[0]
                        if chunk[0] >= 2:
                            dve.wait_ge(operand_split, op[0])
                        w_ = target.shape[1]
                        dve.tensor_tensor(hn_t[:, c % 2, 0:w_], target, gate[chunk[0]], ALU.mult).then_inc(hn_gated, 1)
                        gated[0] += 1
                        chunk[0] += 1
                        if chunk[0] >= 2:
                            low(chunk[0] - 2, c - 1)

                def low(k, c):
                    low_part(a_lo[:, k, ts], hn_t[:, c % 2, 0:ts.stop - ts.start], a_hi[:, k, ts])

                for i in range(n):
                    scale(i)
                    if rope is not None and i >= 1:
                        rotate(i - 1)
                if rope is not None:
                    rotate(n - 1)
                    ropes[0] += n
                if gate is not None:
                    for i in range(n):
                        gates(i)
                    low(chunk[0] - 1, gated[0] - 1)
                hn[0] += n

            at = [0]
            biased = [0]

            def attention(units):
                base, n = at[0], len(units)

                def maximum(i):
                    x, v = units[i], base + i
                    q, s, nk = slice(0, x["nq"]), v % 2, x["nk"]
                    dve.wait_ge(at_scored, v + 1)
                    logits = (b4, b5)[s][q, 0:nk]
                    if x["kind"]:
                        if v >= 2:
                            dve.wait_ge(at_exp, v - 1)
                        if x["kind"] == "window":
                            ins = dve.scalar_tensor_tensor(at_s[q, s, 0:nk], x["bias"][q], x["slope"], logits,
                                                           ALU.mult, ALU.add)
                        else:
                            ins = dve.tensor_tensor(at_s[q, s, 0:nk], logits, x["bias"], ALU.add)
                        link(ins)
                        logits = at_s[q, s, 0:nk]
                    if x["kind"] == "window":
                        link(dve.tensor_reduce(at_m[q, s], logits, AX.X, ALU.max))
                        dve.tensor_scalar(at_nm[q, s], at_m[q, s], sink[q, x["head"]:x["head"] + 1], -1.0, ALU.max,
                                          ALU.mult).then_inc(at_max, 1)
                    else:
                        dve.tensor_reduce(at_nm[q, s], logits, AX.X, ALU.max, negate=True).then_inc(at_max, 1)

                def normalise(i):
                    x, v = units[i], base + i
                    q, s = slice(0, x["nq"]), v % 2
                    dve.wait_ge(at_exp, v + 1)
                    if x["kind"] == "window":
                        link(dve.tensor_tensor(at_den[q, s], at_den[q, s], at_es[q, s], ALU.add))
                    link(dve.reciprocal(at_inv[q, s], at_den[q, s]))
                    dve.tensor_scalar(at_p[q, s, 0:x["nk"]], at_p[q, s, 0:x["nk"]], at_inv[q, s], None, ALU.mult)\
                        .then_inc(at_prob, 1)

                def result(i):
                    x = units[i]
                    low_part(attention_out(a_lo, x), attention_bank(x), attention_out(a_hi, x))

                maximum(0)
                for i in range(n):
                    if i + 1 < n:
                        maximum(i + 1)
                    normalise(i)
                    if i >= 1:
                        result(i - 1)
                result(n - 1)
                at[0] += n

            def residual(name, norm, ts):
                def evac(i, t, gt):
                    add_tile(4 * i + t, t, gt, ts)
                    if 4 * i + t >= 1:
                        finish_low(4 * i + t - 1, norm, ts)
                stream(name, evac)
                finish_low(KD - 1, norm, ts)

            ff = [0]

            def mlp_relu(name, norm, ts):
                first, base, f0 = phases[name].first, op[0], ff[0]

                def low(unit, t, g):
                    k = 4 * (unit % 2) + t
                    dve.wait_ge(operand_high, looped(base + 4 * unit + t + 1, 4 * LOOP_UNITS, g))
                    dve.tensor_tensor(a_lo[:, k, ts], ff_a[:, t % 2, ts], a_hi[:, k, ts].bitcast(F32), ALU.subtract)\
                        .then_inc(operand_split, 1)

                def up(b, unit, g=None):
                    for t in range(4):
                        gt, f = looped(tile_at[b] + t, LOOP_TILES, g), f0 + 4 * unit + t
                        if f >= 2:
                            dve.wait_ge(ff_ready, looped(f - 1, 4 * LOOP_UNITS, g))
                        scaled(ff_z[:, t % 2, ts], t, gt, ts)
                        if t >= 2:
                            low(unit, t - 2, g)
                        dve.wait_ge(operand_split, looped(base + 4 * unit + t - 1, 4 * LOOP_UNITS, g))
                        dve.wait_ge(tile_read, gt + 1)
                        dve.scalar_tensor_tensor(ff_a[:, t % 2, ts], ff_z[:, t % 2, ts], 0.0, ff_z[:, t % 2, ts],
                                                 ALU.max, ALU.mult).then_inc(ff_ready, 1)
                        split_low(b + 1, t - 1, g)
                    low(unit, 2, g)
                    low(unit, 3, g)

                up(first, 0)
                with dve.Fori(0, (N_UNITS - 2) // LOOP_UNITS) as g:
                    up(first + 1, 1, g)
                    down(first + 2, ts, g=g)
                    up(first + 3, 2, g)
                    down(first + 4, ts, g=g)
                last = first + phases[name].n - 3
                up(last, N_UNITS - 1)
                op[0] += D_FF // P
                ff[0] += D_FF // P
                down(last + 1, ts)
                down(last + 2, ts, norm)

            def down(b, ts, norm=None, g=None):
                for k in range(KD):
                    add_tile(k, k % 4, looped(tile_at[b] + k, LOOP_TILES, g), ts)
                    if norm is not None and k >= 1:
                        finish_low(k - 1, norm, ts)
                    if k % 2 == 1:
                        split_low(b + 1, k // 2 - 1, g)
                if norm is not None:
                    finish_low(KD - 1, norm, ts)

            ff_relu = 2 * D_FF // P

            def mlp_swiglu(name, norm, ts):
                b, n = phases[name].first, ts.stop - ts.start
                for i in range(D_FF2 // HALF):
                    for t in range(4):
                        gt = tile_at[b] + t
                        if t < 2:
                            dve.wait_ge(ff_ready, ff[0])
                        else:
                            dve.wait_ge(silu_ready, ff[0] - ff_relu + 1)
                        scaled(ff_z[:, t % 2, 0:n], t, gt, ts)
                        if t >= 2:
                            ff[0] += 1
                            dve.wait_ge(operand_split, op[0])
                            dve.wait_ge(tile_read, gt + 1)
                            dve.tensor_tensor(ff_a[:, t - 2, 0:n], ff_z[:, t - 2, 0:n], ff_s[:, t - 2, 0:n], ALU.mult)\
                                .then_inc(ff_ready, 1)
                        split_low(b + 1, t - 1)
                    for t in range(2):
                        k = 2 * (i % 4) + t
                        low_part(a_lo[:, k, ts], ff_a[:, t, 0:n], a_hi[:, k, ts])
                    b += 1
                    if i % 2 == 0 and i >= 2:
                        down(b, ts)
                        b += 1
                down(b, ts, norm)

            for q in range(3):
                split_low(0, q)
            dve.wait_ge(turned, 1)
            dve.tensor_copy(gains[:], tile_bank[0][:, 0:96])
            link(dve.tensor_copy(late[:], tile_bank[0][:, P:P + N_LATE_ROWS]))
            dve.tensor_scalar(col("b_q"), col("b_q"), 64.0 ** -0.5, None, ALU.mult)
            dve.tensor_scalar(col("c_q"), col("c_q"), 128.0 ** -0.5, None, ALU.mult)
            dve.tensor_scalar(col("ev_q"), col("ev_q"), 64.0 ** -0.5, None, ALU.mult)
            dve.tensor_scalar(late[:, LATE_ROWS["xa_q"]:LATE_ROWS["xa_q"] + 4],
                              late[:, LATE_ROWS["xa_q"]:LATE_ROWS["xa_q"] + 4], 256.0 ** -0.5, None,
                              ALU.mult).then_inc(turn_read, 1)
            for k in range(KD):
                dve.wait_ge(turned, k + 2)
                dve.tensor_copy(hidden[:, k], tile_bank[(k + 1) % 4][:, 0:T]).then_inc(turn_read, 1)
                finish_low(k, "attn0", slice(0, T))

            full = slice(0, T)
            dve.memset(xa[:, :, 0:2], 0.0)
            dve.memset(xa[:, :, PAD - 2:PAD], 0.0)
            rms_ready()

            def project_ab(i, t, gt):
                c = 4 * i + t
                if c >= 12:
                    scaled(za[:, c - 12], t, gt, full)
                    if c == 12:
                        turn_rs(rs_tok, 3)
                    return
                scaled(xa[:, c, 2:2 + T], t, gt, full)
                dve.wait_ge(tile_read, gt + 1)
                link(dve.tensor_scalar(qkv[:, c], xa[:, c, 0:T], col("conv", c), None, ALU.mult))
                for j in range(1, 5):
                    ins = dve.scalar_tensor_tensor(qkv[:, c], xa[:, c, j:j + T], col("conv", 12 * j + c), qkv[:, c],
                                                   ALU.mult, ALU.add)
                    if j < 4:
                        link(ins)
                ins.then_inc(M["conv_done"], 1)

            stream("ab_qkvz", project_ab)
            stream("ab_qb", lambda i, t, gt: scaled(qb[:, t], t, gt, full))

            def project_kvb(i, t, gt):
                if t == 0:
                    scaled(kb, t, gt, full)
                if t == 1:
                    dve.wait_ge(tile_summed, gt + 1)
                    dve.tensor_tensor(vb, tile_bank[1][:, 0:3 * P].rearrange("p (m d) -> p m d", m=3),
                                      rs_tok.unsqueeze(2).to_broadcast([P, 3, P]), ALU.mult).then_inc(tile_read, 1)
                if t == 2:
                    dve.wait_ge(tile_summed, gt + 1)
                    dve.tensor_tensor(hab, tile_bank[2][:, 0:48].rearrange("p (m d) -> p m d", m=3),
                                      rs_tok.unsqueeze(2).to_broadcast([P, 3, 16]), ALU.mult).then_inc(tile_read, 2)

            stream("ab_kvb", project_kvb)
            head_norms([([qb[:, i]], [col("b_q")], [qb[:, i]]) for i in range(4)] + [([kb], [col("b_k")], [kb])])
            dve.wait_ge(misc_in, 16 * N_MISC_LOADS)
            attention([dict(nq=TILES[m][1] - TILES[m][0], nk=T, kind="window", head=h, bias=early_table(f"ndist{m}"),
                            slope=2.0 ** (-(h + 1)), parts=slice(64 * (h % 2), 64 * (h % 2) + 64),
                            chunks=slice(4 + h // 2, 5 + h // 2), tokens=slice(*TILES[m])) for m, h in window_units()])
            head_norms([([qkv[:, i]], [P ** -0.5 if i < 4 else 1.0], [qkv[:, i]]) for i in range(8)])

            dve.tensor_tensor(d_tmp, hab[:, :, 8:16], dt_bias.unsqueeze(1).to_broadcast([P, 3, 8]), ALU.add)\
                .then_inc(M["d_first"], 1)
            dve.wait_ge(M["d_gate_exp"], 1)
            link(dve.tensor_scalar(beta, beta, 1.0, None, ALU.add))
            dve.reciprocal(beta, beta)
            dve.wait_ge(M["d_first"], 1)
            link(dve.scalar_tensor_tensor(d_tmp2, d_tmp, 0.0, d_tmp2, ALU.max, ALU.add))
            link(dve.tensor_scalar(d_tmp2, d_tmp2, -1.0, None, ALU.mult))
            dve.tensor_tensor(decay, d_tmp2, neg_a.unsqueeze(1).to_broadcast([P, 3, 8]), ALU.mult)\
                .then_inc(M["d_gates"], 1)
            dve.wait_ge(M["d_cum"], 1)
            dve.tensor_copy(gcc[0:NMETA, 0], b6[0:NMETA, 0:8])
            dve.tensor_copy(gcc[:, 1:3], b6[:, 8:24].rearrange("p (c h) -> p c h", c=2)).then_inc(M["d_cum_read"], 1)
            dve.wait_ge(M["d_cum_read"], 1)
            for j, (c, d) in enumerate(BATCHES):
                s, e = TILES[c]
                n, dh = e - s, slice(4 * d, 4 * d + 4)

                def heads(ap):
                    return ap.rearrange("p (h i) -> p h i", h=4)

                x, last_row = inverse(j), (n - 1) * (1 - d)
                dmn = heads(dm[0:n, 0:4 * n])
                dve.wait_ge(M["d_rows"], j + 1)
                rows = heads(b4[:, 0:4 * n])
                dve.tensor_tensor(d_tmp[0:n, c, dh], rows[0:n, :, last_row], gcc[0:n, c, dh], ALU.subtract)
                link(dve.tensor_tensor(dmn, rows[0:n], gcc[0:n, c, dh].unsqueeze(2).to_broadcast([n, 4, n]), ALU.subtract))
                neg = table(("neg_f", "neg_b")[d])[0:n, 0:n].unsqueeze(1).to_broadcast([n, 4, n])
                dve.tensor_tensor(dmn, dmn, neg, ALU.add).then_inc(M["d_diff"], 1)
                dve.wait_ge(M["d_egr"], j + 1)
                qd = heads(decayed_queries(c, d))
                link(dve.tensor_copy(egl[:, c, dh], qd[:, :, last_row]))
                dve.tensor_tensor(qd, qd, qkv[:, 0:4, s:e], ALU.mult)
                dve.wait_ge(M["d_gk"], j + 1)
                nnn = heads(nn[0:n, 0:4 * n])
                link(dve.tensor_tensor(nnn, heads(b5[0:n, 0:4 * n]),
                                       beta[0:n, c, dh].unsqueeze(2).to_broadcast([n, 4, n]), ALU.mult))
                dve.wait_ge(M["d_dm"], j + 1)
                dve.tensor_tensor(nnn, nnn, dmn, ALU.mult)
                dve.tensor_tensor(heads(inner_product(j)[0:n]), heads(b6[0:n, 0:4 * n]), dmn, ALU.mult)\
                    .then_inc(M["d_n"], 1)
                eye = ident[0:n, 0:n].unsqueeze(1).to_broadcast([n, 4, n])
                for level in range(n_levels(n)):
                    i = levels_before(j) + level
                    dve.wait_ge(M["d_y"], i + 1)
                    if level == 0:
                        dve.wait_ge(M["d_nb"], i + 1)
                        dve.tensor_tensor(heads(x[0:n]), eye, heads(nb_[0:n, 0:4 * n]), ALU.subtract)
                        dve.tensor_tensor(heads(xt[0:n, 0:4 * n]), eye, heads(b5[0:n, 0:4 * n]), ALU.subtract)\
                            .then_inc(M["d_x"], 1)
                        continue
                    dve.wait_ge(M["d_x"], i)
                    if level < n_levels(n) - 1:
                        dve.tensor_tensor(xt[0:n, 0:4 * n], xt[0:n, 0:4 * n], b6[0:n, 0:4 * n], ALU.subtract)
                    dve.tensor_tensor(x[0:n], x[0:n], b5[0:n, 0:4 * n], ALU.subtract).then_inc(M["d_x"], 1)
            dve.wait_ge(M["d_gate_exp"], 2)
            dve.wait_ge(M["d_copied"], 6)
            seen = set()
            for j, (c, d, first, lastone) in enumerate(SCAN):
                s, e = TILES[c]
                n, dh = e - s, slice(4 * d, 4 * d + 4)

                def by_head(ap):
                    return ap.rearrange("p (h i) -> p h i", h=4)

                r, vn, kd = (by_head(x[0:n]) for x in (scan_r, scan_v, scan_k))
                if j >= 1:
                    dve.wait_ge(M["d_v"], j)
                if first:
                    dve.tensor_copy(r, v_tok[0:n, c]).then_inc(M["d_r"], 1)
                else:
                    dve.wait_ge(M["d_ks"], j - 1)
                    link(dve.tensor_tensor(r, by_head(b4[0:n]), necc[0:n, c, dh].unsqueeze(2).to_broadcast([n, 4, P]),
                                           ALU.mult))
                    dve.tensor_tensor(r, v_tok[0:n, c], r, ALU.subtract).then_inc(M["d_r"], 1)
                if not lastone:
                    if j >= 1:
                        dve.wait_ge(M["d_s"], j)
                    dve.tensor_tensor(kd, k_tok[0:n, c], kdf[0:n, c, dh].unsqueeze(2).to_broadcast([n, 4, P]),
                                      ALU.mult).then_inc(M["d_kdec"], 1)
                dve.wait_ge(M["d_v"], j + 1)
                if j >= 1:
                    dve.wait_ge(M["d_o"], j)
                dve.tensor_tensor(vn, by_head(b5[0:n]), beta[0:n, c, dh].unsqueeze(2).to_broadcast([n, 4, P]), ALU.mult)\
                    .then_inc(M["d_vnew"], 1)
                dve.wait_ge(M["d_o"], j + 1)
                o = by_head(b6[:, 0:4 * n])
                if c in seen:
                    dve.wait_ge(M["d_o_read"], j)
                    dve.tensor_tensor(o_delta[:, :, s:e], o, o_delta[:, :, s:e], ALU.add).then_inc(M["d_o_read"], 1)
                else:
                    dve.tensor_copy(o_delta[:, :, s:e], o).then_inc(M["d_o_read"], 1)
                seen.add(c)
                if not lastone:
                    dve.wait_ge(M["d_s"], j + 1)
                    if first:
                        dve.tensor_copy(state[:, d], by_head(b7[:])).then_inc(M["d_s_read"], 1)
                    else:
                        dve.wait_ge(M["d_s_read"], j - 1)
                        link(dve.tensor_tensor(state[:, d], state[:, d],
                                               egl[:, c, dh].unsqueeze(2).to_broadcast([P, 4, P]), ALU.mult))
                        dve.tensor_tensor(state[:, d], state[:, d], by_head(b7[:]), ALU.add).then_inc(M["d_s_read"], 1)
            dve.wait_ge(M["silu_r"], 1)
            head_norms([([o_delta[:, h]], [col("a_out")], [o_delta[:, h]]) for h in range(4)],
                       gate=[za[:, h] for h in range(4)], ts=full)
            residual("ab_out", "mlp0", full)
            rms_ready()
            mlp_relu("mlp0", "attn1", full)

            def closing(first_turn):
                for i in range(4):
                    dve.wait_ge(turned, first_turn + i + 1)
                    dve.tensor_copy(out_rows[:, i // 2, i % 2 * BLOCK:(i % 2 + 1) * BLOCK],
                                    tile_bank[(first_turn + i) % 4][:]).then_inc(turn_read, 1)


            rms_ready()

            def project_c(i, t, gt):
                scaled(qc[:, 4 * i + t], t, gt, REAL)
                if i == 1 and t == 0:
                    turn_rs(rs_tok, 3)

            stream("c_q", project_c)
            for k in range(KD):
                dve.wait_ge(turned, 10 + k)
                dve.tensor_copy(memory[:, k], (b4, b5)[(9 + k) % 2][:, 0:SEQ]).then_inc(turn_read, 1)

            def project_ckv(i, t, gt):
                if t < 2:
                    scaled(kc[:, t], t, gt, full)
                    return
                dve.wait_ge(tile_summed, gt + 1)
                if t == 2:
                    dve.tensor_tensor(vc[:, 1:3], tile_bank[2][:].rearrange("p (m d) -> p m d", m=2),
                                      rs_tok[:, 1:3].unsqueeze(2).to_broadcast([P, 2, HALF]), ALU.mult).then_inc(tile_read, 1)
                else:
                    dve.tensor_scalar(vc[:, 0], tile_bank[3][:, 0:HALF], rs_tok[:, 0:1], None, ALU.mult)\
                        .then_inc(tile_read, 1)

            stream("c_kv", project_ckv)
            rms_ready()
            turn_rs(rs_mem_tok, 2)
            cos, sin = table("cos_c"), table("sin_c")
            head_norms([([qc[:, i]], [col("c_q")], [qc[:, i]]) for i in range(8)]
                       + [([kc[:, i]], [col("c_k")], [kc[:, i]]) for i in range(2)],
                       rope=[(cos[:, REAL], sin[:, REAL])] * 8 + [(cos, sin)] * 2)
            attention([dict(nq=P, nk=T, kind=None, parts=slice(0, P), chunks=slice(h, h + 1),
                            tokens=slice(16 + m * P, 16 + (m + 1) * P)) for m in range(2) for h in range(8)])
            residual("c_out", "mlp1", REAL)
            rms_ready()
            mlp_relu("mlp1", "mix0", REAL)

            for layer in range(2):
                rms_ready()

                def memory_low():
                    for k in range(KD):
                        op[0] += 1
                        dve.wait_ge(operand_high, op[0])
                        dve.scalar_tensor_tensor(a_lo[:, k, 0:SEQ], memory[:, k], gain(f"memkv{layer}", k),
                                                 a_hi[:, k, 0:SEQ].bitcast(F32), ALU.mult, ALU.subtract)\
                            .then_inc(operand_split, 1)

                def project_memory(i, t, gt):
                    if i < 2:
                        scaled(xk[:, 4 * i + t], t, gt, slice(0, SEQ), rs_mem)
                    else:
                        at_ = (i - 2) * BLOCK + t // 2 * HALF
                        scaled_tokens(xv[:, t % 2, at_:at_ + HALF], t, gt, rs_mem_tok[:, t % 2:t % 2 + 1])

                if layer == 0:
                    def project_ev(i, t, gt):
                        if i == 1 and t == 0:
                            turn_rs(rs_tok[:, 0:2], 2)
                        if i in (2, 4):
                            part = (mv, gv)[i // 4][:, t % 2, t // 2 * HALF:(t // 2 + 1) * HALF]
                            scaled_tokens(part, t, gt, rs_tok[:, t % 2:t % 2 + 1])
                        else:
                            scaled((mq, mk, None, gu)[i][:, t], t, gt, REAL)

                    stream("ev_in", project_ev, 0, 2)
                    memory_low()
                    stream("ev_in", project_ev, 2)
                    stream("xkv0", project_memory)
                    dve.wait_ge(late_in, 16 * N_LATE_LOADS)
                    ang, tmp, cosa = angle[:, 0], angle[:, 2], angle[:, 1]
                    link(dve.tensor_copy(tmp, pos_i.bitcast(I32)))
                    link(dve.tensor_scalar(ang, tmp, table("inv_freq"), None, ALU.mult))
                    link(dve.tensor_scalar(tmp, ang, 1.0 / (2.0 * PI), ROUND, ALU.mult, ALU.add))
                    link(dve.tensor_scalar(tmp, tmp, -ROUND, None, ALU.add))
                    for part in TWO_PI_PARTS:
                        link(dve.scalar_tensor_tensor(ang, tmp, -part, ang, ALU.mult, ALU.add))
                    link(dve.tensor_scalar(cosa, ang, PI / 2, None, ALU.add))
                    link(dve.tensor_scalar(tmp, cosa, PI, -2.0 * PI, ALU.is_gt, ALU.mult))
                    link(dve.tensor_tensor(cosa, cosa, tmp, ALU.add))
                    link(dve.tensor_scalar(ang, ang, PI_BELOW, -PI_BELOW, ALU.min, ALU.max))
                    dve.tensor_scalar(cosa, cosa, PI_BELOW, -PI_BELOW, ALU.min, ALU.max).then_inc(M["rope_angle"], 1)
                    dve.wait_ge(M["rope_sin"], 1)
                    head_norms([([x[:, i]], [col(g)], [x[:, i]]) for x, g in ((mq, "ev_q"), (mk, "ev_k")) for i in range(4)],
                               rope=[(cos_m, sin_m)] * 8)
                    zeros_at = C["zeros"][0]
                    causal = cst[:, zeros_at:zeros_at + 2 * P]
                    attention([dict(nq=P, nk=(m + 1) * P, kind="causal", bias=causal[:, (1 - m) * P:2 * P],
                                    parts=slice(64 * (h % 2), 64 * (h % 2) + 64), chunks=slice(h // 2, h // 2 + 1),
                                    tokens=slice(16 + m * P, 16 + (m + 1) * P)) for m in range(2) for h in range(8)])
                    for i in range(2):
                        dve.wait_ge(M["ws_turned"], i + 1)
                        dve.tensor_tensor(ws_t[:, 4 * i:4 * i + 4], (b4, b5)[i][:].rearrange("p (g i) -> p g i", g=4),
                                          table("tri_f").unsqueeze(1).to_broadcast([P, 4, P]), ALU.mult)\
                            .then_inc(M["ws_read"], 1)
                    dve.wait_ge(M["gelu"], 8)
                    groups = gv.rearrange("p m (g d) -> p (m g) d", d=64)
                    wide = [P, 16, 64]
                    link(dve.tensor_reduce(g_mu, groups, AX.X, ALU.add))
                    link(dve.tensor_scalar(g_mu, g_mu, 1.0 / 64, None, ALU.mult))
                    dve.tensor_tensor(groups, groups, g_mu.unsqueeze(2).to_broadcast(wide), ALU.subtract)\
                        .then_inc(M["g_stat"], 1)
                    dve.wait_ge(M["g_sq"], 1)
                    dve.tensor_reduce(g_var, gt.rearrange("p m (g d) -> p (m g) d", d=64), AX.X, ALU.add)\
                        .then_inc(M["g_stat"], 1)
                    dve.wait_ge(M["g_ln"], 1)
                    link(dve.tensor_tensor(groups, groups, g_var.unsqueeze(2).to_broadcast(wide), ALU.mult))
                    link(dve.tensor_tensor(gv, gv, ln_g.unsqueeze(1).to_broadcast([P, 2, BLOCK]), ALU.mult))
                    dve.tensor_tensor(gv, gv, ln_b.unsqueeze(1).to_broadcast([P, 2, BLOCK]), ALU.add).then_inc(M["g_n"], 1)
                    for c in range(2):
                        dve.wait_ge(M["g_mixed"], c + 1)
                        link(dve.tensor_tensor(g_out(c), (b4, b5)[c][:].rearrange("p (g i) -> p g i", g=4), b_s, ALU.add))
                        dve.tensor_tensor(g_out(c), g_out(c), gu[:, :, c * P:(c + 1) * P], ALU.mult).then_inc(M["g_read"], 1)
                    for c in range(2):
                        ts = slice(16 + c * P, 16 + (c + 1) * P)
                        dve.wait_ge(M["g_read"], c + 1)
                        low_part(a_lo[:, 4:8, ts], g_out(c), a_hi[:, 4:8, ts])
                else:
                    def project_od(i, t, gt):
                        if i == 1 and t == 0:
                            turn_rs(rs_tok[:, 0:2], 2)
                        if i in (2, 3):
                            at_ = (i - 2) * BLOCK + t // 2 * HALF
                            scaled_tokens(lv[:, t % 2, at_:at_ + HALF], t, gt, rs_tok[:, t % 2:t % 2 + 1])
                        elif i < 2:
                            scaled((lq, lk)[i][:, t], t, gt, REAL)
                        else:
                            scaled(lr[:, 4 * (i - 4) + t], t, gt, REAL)

                    stream("od_in", project_od, 0, 2)
                    memory_low()
                    stream("od_in", project_od, 2)
                    stream("xkv1", project_memory)
                    dve.wait_ge(M["l_low"], 1)
                    dve.tensor_tensor(squares[0:16, 0, 0:SEQ], b4[0:16, 0:SEQ], rs[0:16, REAL], ALU.mult)\
                        .then_inc(M["l_lowc"], 1)
                    for h in range(4):
                        dve.wait_ge(M["l_e1"], h + 1)
                        dve.tensor_scalar(la[:, h], (b5, b6)[h % 2][:, 0:SEQ], col("od_b", h), None, ALU.add)\
                            .then_inc(M["l_gate"], 1)
                    for h in range(4):
                        dve.wait_ge(M["l_exp"], h + 1)
                        link(dve.scalar_tensor_tensor(la[:, h], la[:, h], 0.0, l_tmp[:, h], ALU.min, ALU.subtract))
                    link(dve.tensor_scalar(la, la, 1.0 / 16, None, ALU.mult))
                    for h in range(4):
                        for c in range(4):
                            cs = slice(64 * c, 64 * c + 64)
                            ins = dve.tensor_tensor_scan(la[:, h, cs], ones[:, 0:64], la[:, h, cs], 0.0, ALU.mult, ALU.add)
                    ins.then_inc(M["l_scan"], 1)
                    dve.wait_ge(M["l_exp"], 5)
                    dve.scalar_tensor_tensor(lq.rearrange("p h t -> p (h t)"), lq.rearrange("p h t -> p (h t)"), 128.0 ** -0.5,
                                             l_tmp.rearrange("p h t -> p (h t)"), ALU.mult, ALU.mult)
                    dve.wait_ge(M["l_exp"], 6)
                    dve.tensor_tensor(ks_t, ks_t, lk, ALU.mult).then_inc(M["l_ks"], 1)
                    dve.wait_ge(M["l_exp"], 7)
                    dve.tensor_tensor(lk, lk, lo_t[:, 4:8], ALU.mult).then_inc(M["l_qk"], 1)
                    dve.wait_ge(M["l_att"], 1)
                    mats = att64.rearrange("p m h t -> p (m h) t")
                    cap = table("cap64").unsqueeze(1).to_broadcast([P, 8, 64])
                    ncap = table("ncap64").unsqueeze(1).to_broadcast([P, 8, 64])
                    link(dve.tensor_tensor(mats, b6[:].rearrange("p (m t) -> p m t", t=64), cap, ALU.min))
                    dve.tensor_tensor(mats, mats, ncap, ALU.max).then_inc(M["l_attc"], 1)
                    for c in range(4):
                        cs = slice(64 * c, 64 * c + 64)
                        dve.wait_ge(M["l_o"], c + 1)
                        dve.tensor_copy(lo_t[:, :, cs], b7[:].rearrange("p (r t) -> p r t", t=64)).then_inc(M["l_oc"], 1)
                        if c < 3:
                            dve.wait_ge(M["l_ds"], c + 1)
                            for half in range(2):
                                new = (b4, b5)[half][:].rearrange("p (h v) -> p h v", h=2)
                                part = l_state[:, 2 * half:2 * half + 2]
                                if c == 0:
                                    ins = dve.tensor_copy(part, new)
                                else:
                                    if half == 0:
                                        dve.wait_ge(M["l_dsr"], c)
                                    f = l_dec[:, 2 * half:2 * half + 2, c].unsqueeze(2).to_broadcast([P, 2, 256])
                                    link(dve.tensor_tensor(part, part, f, ALU.mult))
                                    ins = dve.tensor_tensor(part, part, new, ALU.add)
                            ins.then_inc(M["l_dsr"], 1)
                    dve.wait_ge(M["l_oc"], 4)
                    dve.wait_ge(M["silu_r"], 2)
                    head_norms([([lo_t[:, 2 * h + r] for r in range(2)], [col("od_o", 2 * h + r) for r in range(2)],
                                 [lo_t[:, 2 * h + r] for r in range(2)]) for h in range(4)],
                               gate=[lr[:, c] for c in range(8)], ts=REAL)
                residual(f"mix_out{layer}", f"memq{layer}", REAL)
                rms_ready()
                stream(f"xq{layer}", lambda i, t, gt: scaled(xq[:, 4 * i + t], t, gt, REAL))
                head_norms([([x[:, 2 * h + r] for r in range(2)], [col(g, 2 * layer + r) for r in range(2)],
                             [x[:, 2 * h + r] for r in range(2)]) for x, g in ((xk, "xa_k"), (xq, "xa_q")) for h in range(4)])
                attention([dict(nq=P, nk=SEQ, kind=None, parts=slice(0, P), chunks=slice(2 * h, 2 * h + 2),
                                tokens=slice(16 + m * P, 16 + (m + 1) * P)) for m in range(2) for h in range(4)])
                residual(f"x_out{layer}", f"ffn{layer}", REAL)
                rms_ready()
                mlp_swiglu(f"swiglu{layer}", "mix1" if layer == 0 else None, REAL)
            closing(17)

        @block.gpsimd
        def _(pool):
            fin = [0]

            def rows(target, at, n, source):
                pool.dma_start(target[at:at + n], source).then_inc(rows_in, 16)

            for i, name in enumerate(("attn_norm_g", "mlp_norm_g", "norm_mix_2", "norm_mem_q_2", "norm_mem_kv_2", "norm_ffn_2")):
                rows(gain_rows, 16 * i, 16, w[name].rearrange("l (k p) -> (l k) p", p=P))
            R = LATE_ROWS
            rows(late_rows, R["conv"], 60, w["conv_w_a"].rearrange("o j (t p) -> (o j t) p", p=P))
            for name, key in (("a_out", "a_out_norm_g"), ("c_q", "c_q_norm_g"), ("c_k", "c_k_norm_g")):
                rows(late_rows, R[name], 1, w[key])
            for name, key in (("b_q", "b_q_norm_g"), ("b_k", "b_k_norm_g"), ("ev_q", "ev_q_gain_2"), ("ev_k", "ev_k_gain_2")):
                for half in range(2):
                    rows(late_rows[:, 64 * half:64 * half + 64], R[name], 1, w[key])
            for name, key in (("xa_q", "xa_q_gain_2"), ("xa_k", "xa_k_gain_2")):
                rows(late_rows, R[name], 4, w[key].rearrange("l (r p) -> (l r) p", p=P))
            rows(late_rows, R["od_o"], 8, w["od_o_gain_2"].rearrange("o h (r p) -> (o h r) p", p=P))
            rows(late_rows, R["od_b"], 4, w["od_b_g_2"].rearrange("o (r p) -> (o r) p", p=P))

            def misc(target, source):
                pool.dma_start(target, source).then_inc(misc_in, 16)

            misc(early[:, 0:ew], w["early_tables"])
            misc(a_log, w["a_log"].rearrange("o d h -> (o d h)").partition_broadcast(P))
            misc(dt_bias, w["dt_bias"].rearrange("o d h -> (o d h)").partition_broadcast(P))
            misc(sink, w["b_sink"].rearrange("o h -> (o h)").partition_broadcast(P))
            misc(wg1, w["od_w_g1_2"][0].rearrange("(k p) r -> p k r", p=P))

            def add_squares(ts=slice(0, T)):
                n = fin[0] // KD
                if n >= 1:
                    pool.wait_ge(norm_summed, n)
                for k in range(KD):
                    f = fin[0]
                    fin[0] += 1
                    pool.wait_ge(squared, f + 1)
                    if k == 0:
                        pool.tensor_copy(square_sum[:, ts], squares[:, f % 2, ts]).then_inc(sum_added, 1)
                    else:
                        pool.wait_ge(sum_added, f)
                        pool.tensor_tensor(square_sum[:, ts], square_sum[:, ts], squares[:, f % 2, ts], ALU.add)\
                            .then_inc(sum_added, 1)

            add_squares()
            y = 0
            for j, (c, d) in enumerate(BATCHES):
                n = TILES[c][1] - TILES[c][0]
                pool.wait_ge(M["d_n"], j + 1)
                for level in range(n_levels(n)):
                    i = levels_before(j) + level
                    if i >= 1:
                        if level == 1:
                            pool.wait_ge(M["d_x"], i)
                        else:
                            pool.wait_ge(M["d_w"], y)
                    mask = early_table(f"level{level}")[0:n, 0:n].unsqueeze(1).to_broadcast([n, 4, n])
                    pool.tensor_tensor(nb_[0:n, 0:4 * n].rearrange("p (h i) -> p h i", h=4),
                                       nn[0:n, 0:4 * n].rearrange("p (h i) -> p h i", h=4), mask, ALU.mult)\
                        .then_inc(M["d_nb"], 1)
                    if level >= 1:
                        y += 1
            add_squares()
            add_squares()
            pool.dma_start(mem_rows, w["mem_2"][0].rearrange("(m p) d -> p m d", p=P)).then_inc(mem_in, 16)

            def later(target, source):
                pool.dma_start(target, source).then_inc(late_in, 16)

            later(ln_g, w["ev_ln_g_2"].rearrange("o g d -> (o g d)").partition_broadcast(P))
            later(ln_b, w["ev_ln_b_2"].rearrange("o g d -> (o g d)").partition_broadcast(P))
            for half in range(2):
                later(b_s[64 * half:64 * half + 64],
                      w["ev_b_s_2"][0].rearrange("(t two) i -> two t i", two=2)[half].partition_broadcast(64))
            later(pos_i.bitcast(I32), w["positions_2"].rearrange("o t -> (o t)").partition_broadcast(P))
            add_squares(slice(0, SEQ))
            pool.wait_ge(turn_read, 1 + 2 * KD)
            pool.dma_start(ws_rows.rearrange("p a (b j) -> p (a b) j", j=P), w["ev_w_s_2"][0].rearrange("g i j -> i g j"))\
                .then_inc(ws_in, 16)
            for norm in ("mlp1", "mix0", "memq0"):
                add_squares(REAL)
            pool.dma_start(wg2[0:16], w["od_w_g2_2"][0]).then_inc(wg_in, 16)
            for norm in ("ffn0", "mix1", "memq1", "ffn1"):
                add_squares(REAL)
            pool.wait_ge(turn_read, 1 + 2 * KD + 4)
            pool.dma_start(out[0].rearrange("(m p) d -> p m d", p=P), out_rows).then_inc(out_sent, 16)
            pool.wait_ge(out_sent, 16)


_INS = """x meta_tokens attn_norm_g mlp_norm_g w_in_ab conv_w_a a_log dt_bias a_out_norm_g b_q_norm_g b_k_norm_g b_sink
w_out_ab w_qkv_c c_q_norm_g c_k_norm_g w_out_c w_ff1 w_ff2 mem_2 positions_2 norm_mix_2 norm_mem_q_2 norm_mem_kv_2
norm_ffn_2 ev_w_in_2 ev_q_gain_2 ev_k_gain_2 ev_w_s_2 ev_b_s_2 ev_ln_g_2 ev_ln_b_2 ev_w_out_2 od_w_in_2 od_w_g1_2
od_w_g2_2 od_b_g_2 od_o_gain_2 od_w_out_2 xa_w_q_2 xa_w_kv_2 xa_q_gain_2 xa_k_gain_2 xa_w_out_2 ffn_w_gu_2
ffn_w_down_2""".split()


def kernel(**inputs):
    import concourse.bacc as _bacc
    from concourse.bass_utils import run_bass_kernel_spmd as _run

    nc = _bacc.Bacc("TRN2", target_bir_lowering=False, num_devices=1)
    arrays, w = {}, {}
    (tables, _), (early, _) = shape_constants()
    for name, a in [(n, inputs[n]) for n in _INS] + [("shape_tables", tables), ("early_tables", early)]:
        a = np.ascontiguousarray(a)
        arrays[f"in_{name}_dram"] = a
        w[name] = nc.dram_tensor(f"in_{name}_dram", a.shape, mybir.dt.from_np(a.dtype), kind="ExternalInput").ap()
    out = nc.dram_tensor("out_dram", (1, SEQ, D), F32, kind="ExternalOutput").ap()
    program(nc, w, out)
    return _run(nc, [arrays], core_ids=[0]).results[0]["out_dram"]
```

```python
from contextlib import ExitStack

import numpy as np

import concourse.bass as bass
from concourse import mybir

F32, F32R, I32 = mybir.dt.float32, mybir.dt.float32r, mybir.dt.int32
ALU, ACT, AX = mybir.AluOpType, mybir.ActivationFunctionType, mybir.AxisListType

P = 128
D = 1024
KD = D // P
NMETA, SEQ, GRID_W = 16, 256, 64
T = NMETA + SEQ
REAL = slice(NMETA, T)
TILES = [(0, NMETA), (NMETA, NMETA + P), (NMETA + P, T)]
WINDOW = 128
BLOCK = 512
HALF = BLOCK // 2
EPS = 1e-6
BIG = 1e30
HUGE = 3e38
D_FF = 4 * D
D_FF2 = 2816
UNIT = BLOCK
N_UNITS = D_FF // UNIT
A_HEADS = 4
LEVELS = 7
PI = float(np.pi)


def shape_constants():
    i = np.arange(P)
    tables = {}
    tables["ident"] = np.eye(P)
    tables["ones"] = np.ones((P, P))
    tables["blk64"] = (i[:, None] // 64 == i[None, :] // 64)
    swap = np.zeros((P, P))
    swap[i[::2] + 1, i[::2]] = -1.0
    swap[i[::2], i[::2] + 1] = 1.0
    tables["swap_pairs"] = swap
    swap = np.zeros((P, P))
    for base in (0, 64):
        for m in range(8):
            swap[base + m + 8, base + m] = -1.0
            swap[base + m, base + m + 8] = 1.0
    tables["swap_halves"] = swap
    upto = i[:, None] <= i[None, :]
    tables["tri_f"] = upto
    tables["tri_b"] = upto.T
    tables["neg_f"] = np.where(upto, 0.0, -BIG)
    tables["zeros"] = np.zeros((P, P))
    tables["neg_b"] = np.where(upto.T, 0.0, -BIG)
    cap = np.where((i[:, None] % 64) <= np.arange(64)[None, :], HUGE, 0.0)
    tables["cap64"] = cap
    tables["ncap64"] = -cap
    meta = np.arange(NMETA) - NMETA
    row = np.concatenate([meta, np.repeat(np.arange(SEQ // GRID_W), GRID_W)]).astype(np.float32)
    col = np.concatenate([meta, np.tile(np.arange(GRID_W), SEQ // GRID_W)]).astype(np.float32)
    freq = (np.float32(10000.0) ** (-np.arange(0, 64, 2, dtype=np.float32) / np.float32(64))).astype(np.float32)
    ang = np.concatenate([row[:, None] * freq, col[:, None] * freq], axis=-1).astype(np.float32)
    ang = np.repeat(ang, 2, axis=1).T.astype(np.float64)
    tables["cos_c"] = np.cos(ang)
    tables["sin_c"] = np.sin(ang)
    inv = (np.float32(500000.0) ** (-np.arange(8, dtype=np.float32) * np.float32(2.0) / np.float32(16))).astype(np.float32)
    tables["inv_freq"] = np.where(i % 64 < 16, inv[i % 8], 0.0)[:, None]
    tables["eps"] = np.full((P, 1), EPS)
    early = {}
    for level in range(LEVELS):
        b = 1 << level
        early[f"level{level}"] = ((i[:, None] // (2 * b) == i[None, :] // (2 * b))
                                  & (i[:, None] // b != i[None, :] // b))
    keys = np.arange(T)
    for m, (a, b) in enumerate(TILES):
        q = a + np.minimum(i, b - a - 1)
        dist = np.abs(q[:, None] - keys[None, :])
        early[f"ndist{m}"] = np.where(keys[None, :] < NMETA, 0.0, np.where(dist <= WINDOW, -dist, -BIG))

    def pack(named):
        at, place = 0, {}
        for name, table in named.items():
            place[name] = (at, table.shape[1])
            at += table.shape[1]
        return np.concatenate([np.asarray(t, np.float32) for t in named.values()], axis=1), place

    return pack(tables), pack(early)


class Phase:

    def __init__(self, first, blocks, up=None, down=None, token_blocks=(), done=None):
        self.first, self.blocks, self.n, self.up, self.down = first, blocks, len(blocks), up, down
        self.token_blocks, self.done = token_blocks, done


def weight_plan(w):
    phases, at = {}, 0

    def cols(x, c, width=BLOCK, rows=slice(None), into=0):
        return (into, width, x[rows, c:c + width].rearrange("(k p) n -> p k n", p=P))

    def add(name, blocks, **more):
        nonlocal at
        phases[name] = Phase(at, blocks, **more)
        at += len(blocks)

    x = w["w_in_ab"][0]
    add("ab_qkvz", [[cols(x, c)] for c in range(0, 2048, BLOCK)])
    add("ab_qb", [[cols(x, 2064)]])
    add("ab_kvb", [[cols(x, 2576, 256), cols(x, 2048, 128, into=256)]])
    add("ab_out", [[cols(w["w_out_ab"][0], c)] for c in (0, BLOCK)])

    def relu_mlp(layer):
        up = w["w_ff1"][layer].rearrange("(k p) (g n) -> g p k n", p=P, n=UNIT)
        down = w["w_ff2"][layer].rearrange("(g k p) n -> g p k n", p=P, k=UNIT // P)
        blocks = [[(0, BLOCK, up[0])]]
        for i in range(N_UNITS):
            if i + 1 < N_UNITS:
                blocks.append([(0, BLOCK, up[i + 1])])
            blocks.append([(None, 0, down[i])])
        add(f"mlp{layer}", blocks, up=up, down=down)

    relu_mlp(0)
    x = w["w_qkv_c"][0]
    add("c_q", [[cols(x, c)] for c in (0, BLOCK)])
    add("c_kv", [[cols(x, 1024)]], done=(1, 2, 4, 4))
    add("c_out", [[cols(w["w_out_c"][0], c)] for c in (0, BLOCK)])
    relu_mlp(1)

    def second(layer):
        if layer == 0:
            add("ev_in", [[cols(w["ev_w_in_2"][0], c)] for c in range(0, 2560, BLOCK)], token_blocks=(2, 4))
        else:
            add("od_in", [[cols(w["od_w_in_2"][0], c)] for c in range(0, 3072, BLOCK)], token_blocks=(2, 3))
        add(f"xkv{layer}", [[cols(w["xa_w_kv_2"][layer], c)] for c in range(0, 2048, BLOCK)], token_blocks=(2, 3))
        out = w["ev_w_out_2"][0] if layer == 0 else w["od_w_out_2"][0]
        add(f"mix_out{layer}", [[cols(out, c)] for c in (0, BLOCK)])
        add(f"xq{layer}", [[cols(w["xa_w_q_2"][layer], c)] for c in (0, BLOCK)])
        add(f"x_out{layer}", [[cols(w["xa_w_out_2"][layer], c)] for c in (0, BLOCK)])
        gu, down = w["ffn_w_gu_2"][layer], w["ffn_w_down_2"][layer]
        blocks = []
        for c in range(0, D_FF2, HALF):
            blocks.append([cols(gu, c, HALF), cols(gu, D_FF2 + c, HALF, into=HALF)])
            if c % UNIT == 0 and c >= UNIT:
                blocks.append([(None, 0, down[c - UNIT:c].rearrange("(k p) n -> p k n", p=P))])
        blocks.append([(None, 0, down[D_FF2 // UNIT * UNIT:].rearrange("(k p) n -> p k n", p=P))])
        add(f"swiglu{layer}", blocks)

    for layer in range(2):
        second(layer)
    return phases, at


NORMS = ["attn0", "attn1", "mlp0", "mlp1", "mix0", "mix1", "memq0", "memq1", "memkv0", "memkv1", "ffn0", "ffn1"]
LATE_ROWS = {"conv": 0, "a_out": 60, "b_q": 61, "b_k": 62, "c_q": 63, "c_k": 64, "ev_q": 65, "ev_k": 66,
             "xa_q": 67, "xa_k": 71, "od_o": 75, "od_b": 83}
N_LATE_ROWS = 87
N_GAIN_LOADS, N_ROW_LOADS, N_MISC_LOADS, N_LATE_LOADS = 6, 16, 5, 5
ROUND = 1.5 * 2.0 ** 23
PI_BELOW = float(np.nextafter(np.float32(PI), np.float32(0)))
TWO_PI_PARTS = [6.28125, 0.0019350051879882812, 3.0199159819122e-07]


def program(nc, w, out):
    phases, n_blocks = weight_plan(w)
    (_, C), (_, E) = shape_constants()
    (cw, ew) = (sum(n for _, n in C.values()), sum(n for _, n in E.values()))
    with ExitStack() as ctx:
        def sb(name, shape, dtype=F32):
            return ctx.enter_context(nc.sbuf_tensor(name, shape, dtype))

        def sem(name):
            return ctx.enter_context(nc.semaphore(name))

        raw = sb("raw", [P, 2, KD, BLOCK])
        w_hi = sb("w_hi", [P, 4, KD * P], F32R)
        w_lo = sb("w_lo", [P, 4, KD * P], F32R)
        hidden = sb("hidden", [P, KD, T])
        u_hi, u_lo = sb("u_hi", [P, KD, T], F32R), sb("u_lo", [P, KD, T], F32R)
        a_hi, a_lo = sb("a_hi", [P, KD, T], F32R), sb("a_lo", [P, KD, T], F32R)
        cst = sb("cst", [P, cw])
        early = sb("early", [P, KD * SEQ])
        gains = sb("gains", [P, 8 * len(NORMS)])
        late = sb("late", [P, N_LATE_ROWS])
        rs = sb("rs", [P, T])[:]
        rs_tok = sb("rs_tok", [P, 3])[:]
        rs_mem, rs_mem_tok = sb("rs_mem", [P, SEQ])[:], sb("rs_mem_tok", [P, 2])[:]
        squares, square_sum = sb("squares", [P, 2, T]), sb("square_sum", [P, T])
        work = sb("work", [P, 2656])
        att = sb("att", [P, 2128])
        mx = sb("mx", [P, 14304])
        small = sb("small", [P, 768])
        psum = [ctx.enter_context(nc.psum_tensor(f"ps{i}", [P, 512], F32)) for i in range(8)]
        tile_bank, b4, b5, b6, b7 = psum[:4], psum[4], psum[5], psum[6], psum[7]

        def area(tensor, at, *shape):
            n = int(np.prod(shape))
            ap = tensor[:, at:at + n]
            if len(shape) == 2:
                ap = ap.rearrange("p (a b) -> p a b", a=shape[0])
            if len(shape) == 3:
                ap = ap.rearrange("p (a b c) -> p a b c", a=shape[0], b=shape[1])
            return ap

        def table(name):
            at, n = C[name]
            return cst[:, at:at + n]

        def early_table(name):
            at, n = E[name]
            return early[:, at:at + n]

        ident, ones, blk64, eps = table("ident"), table("ones"), table("blk64"), table("eps")
        memory = area(early, 0, KD, SEQ)

        def gain(norm, k):
            c = 8 * NORMS.index(norm) + k
            return gains[:, c:c + 1]

        def col(name, k=0):
            c = LATE_ROWS[name] + k
            return late[:, c:c + 1]

        ff_z, ff_s, ff_a = area(work, 0, 2, T), area(work, 544, 2, T), area(work, 1088, 2, T)
        hn_sq, hn_r, hn_n, hn_t = area(work, 0, 2, 512), area(work, 1024, 2, T), area(work, 1568, 2, T), area(work, 2112, 2, T)
        at_s, at_p, at_pt = area(att, 0, 2, T), area(att, 544, 3, T), area(att, 1360, 2, 3, P)
        at_m, at_nm, at_den, at_es, at_inv = (area(small, 2 * i, 2, 1) for i in range(5))
        x_rows, meta_rows = area(mx, 0, 2, D), area(mx, 2 * D, D)
        gain_rows, late_rows = area(mx, 3 * D, P), area(mx, 3 * D + P, P)
        mem_rows = area(mx, 8192, 2, D)
        PAD = T + 4
        xa = area(mx, 0, 12, PAD)
        v_tok, k_tok = area(mx, 0, 3, 4, P), area(mx, 1536, 3, 4, P)
        za = area(mx, 3312, 4, T)
        qb, kb, kdup, vb = area(mx, 4400, 4, T), area(mx, 5488, T), area(mx, 5760, 2, T), area(mx, 6304, 3, P)
        qkv = area(mx, 6688, 12, T)
        o_delta = qkv[:, 8:12]
        inner = area(mx, 9952, 2176 + 2176)
        qe_f, qe_b = area(mx, 5488, 1152), area(att, 0, 1152)
        state = area(mx, 4400, 2, 4, P)
        dm, nn, xt, nb_ = zip(*([area(work, 512 * i, 512) for i in range(4)],
                                [area(att, 1152, 512), area(early, 896, 512), area(early, 1408, 512), area(work, 2048, 512)]))
        wt = scan_r = dm
        scan_v, scan_k = nn, xt
        hab, beta, decay = area(small, 16, 3, 16), area(small, 64, 3, 8), area(small, 88, 3, 8)
        gcc, necc, kdf = area(small, 112, 3, 8), area(small, 136, 3, 8), area(small, 160, 3, 8)
        egl = area(small, 184, 3, 8)
        d_tmp, d_tmp2 = area(small, 208, 3, 8), area(small, 232, 3, 8)
        a_log, dt_bias, sink = area(small, 256, 8), area(small, 264, 8), area(small, 272, 8)
        neg_a = area(small, 280, 8)
        qc, kc, vc = area(mx, 0, 8, SEQ), area(mx, 2048, 2, T), area(mx, 2592, 3, SEQ)
        xk, xv, xq = area(mx, 0, 8, SEQ), area(mx, 2048, 2, D), area(mx, 4096, 8, SEQ)
        mq, mk, mv = area(mx, 4096, 4, SEQ), area(mx, 5120, 4, SEQ), area(mx, 6144, 2, BLOCK)
        gu, gv, gt = area(mx, 7168, 4, SEQ), area(mx, 8192, 2, BLOCK), area(mx, 9216, 2, BLOCK)
        ws_rows, ws_t = gt, area(mx, 10240, 8, P)
        ln_g, ln_b, b_s = area(mx, 11264, BLOCK), area(mx, 11776, BLOCK), area(mx, 12288, 4, P)
        cos_m, sin_m = area(mx, 12800, SEQ), area(mx, 13056, SEQ)
        angle = area(att, 0, 4, SEQ)
        pos_i = area(mx, 13312, SEQ)
        lq, lk, lv, lr = area(mx, 4096, 4, SEQ), area(mx, 5120, 4, SEQ), area(mx, 6144, 2, D), area(mx, 8192, 8, SEQ)
        la, lo_t = area(mx, 10240, 4, SEQ), area(mx, 11264, 8, SEQ)
        wg1, wg2 = area(small, 300, KD, 16), area(mx, 13312, BLOCK)
        kst, att64 = area(att, 0, 2, 4, P), area(att, 1024, 2, 4, 64)
        l_state, l_tmp, ks_t = area(work, 0, 4, 256), area(work, 1024, 4, SEQ), lo_t[:, 0:4]
        g_mu, g_var, l_dec = area(small, 16, 16), area(small, 32, 16), area(small, 48, 4, 4)
        out_rows = area(mx, 0, 2, D)

        x_in, ident_in, cst_in, gains_in, rows_in, misc_in, late_in, mem_in, ws_in, wg_in = (
            sem(n) for n in "x_in ident_in cst_in gains_in rows_in misc_in late_in mem_in ws_in wg_in".split())
        raw_in = [sem("raw_in0"), sem("raw_in1")]
        high_split, low_split = sem("high_split"), sem("low_split")
        tile_summed, tile_read = sem("tile_summed"), sem("tile_read")
        turned, turn_read = sem("turned"), sem("turn_read")
        operand_high, operand_split = sem("operand_high"), sem("operand_split")
        squared, sum_added = sem("squared"), sem("sum_added")
        norm_summed, norm_ln, rs_ready = sem("norm_summed"), sem("norm_ln"), sem("rs_ready")
        rs_turned, rs_tok_ready = sem("rs_turned"), sem("rs_tok_ready")
        ff_ready, silu_ready = sem("ff_ready"), sem("silu_ready")
        hn_squared, hn_summed, hn_ln, hn_rs, hn_scaled = (
            sem(n) for n in "hn_squared hn_summed hn_ln hn_rs hn_scaled".split())
        hn_swapped, hn_roped, hn_gated = sem("hn_swapped"), sem("hn_roped"), sem("hn_gated")
        at_scored, at_biased, at_max, at_exp, at_prob = (
            sem(n) for n in "at_scored at_biased at_max at_exp at_prob".split())
        at_turned, at_copied, at_summed = sem("at_turned"), sem("at_copied"), sem("at_summed")
        dve_step, act_step, out_sent = sem("dve_step"), sem("act_step"), sem("out_sent")
        M = {n: sem(n) for n in (
            "ab_turned ab_turn_read conv_done d_copied d_cum d_cum_read d_diff d_dm d_egr d_first d_gate_exp d_gates d_gk d_kdec "
            "d_ks d_n d_nb d_o d_o_read d_r d_rows d_s d_s_read d_turned d_v d_vnew d_w d_w_copied d_x d_y "
            "g_ln g_mixed g_n g_read g_sq g_stat gelu kv_dup l_att l_attc l_ds l_dsr l_e1 l_exp l_gate l_ks "
            "l_kst l_kstc l_low l_lowc l_o l_oc l_qk l_scan rope_angle rope_sin silu_done silu_r ws_read "
            "ws_turned ").split()}

        landed_at, tile_at, wide, quarter_done, so_far = [], [0], [], [], [0, 0]
        for ph in phases.values():
            for i, loads in enumerate(ph.blocks):
                so_far[len(landed_at) % 2] += 16 * len(loads)
                landed_at.append(so_far[len(landed_at) % 2])
                wide.append(loads[0][0] is None)
                done = ph.done or ((2, 4, 6, 8) if wide[-1] else (2, 2, 4, 4) if i in ph.token_blocks else (1, 2, 3, 4))
                quarter_done.append([tile_at[-1] + n for n in done])
                tile_at.append(tile_at[-1] + (8 if wide[-1] else 4))
        LOOP_BLOCKS, LOOP_TILES, LOOP_LANDED, LOOP_UNITS = 4, 24, 32, 2

        def looped(count, per_iteration, g):
            return count if g is None else per_iteration * g + count

        def raw_quarter(b, q):
            slot = raw[:, b % 2]
            if wide[b]:
                slot = slot.rearrange("p (k two) n -> p k (two n)", two=2)
            n = (2 if wide[b] else 1) * P
            return slot[:, :, q * n:(q + 1) * n]

        def quarter(part, b, q):
            return part[:, q].rearrange("p (k n) -> p k n", n=(2 if wide[b] else 1) * P)

        def attention_out(operand, x):
            return operand[x["parts"], x["chunks"], x["tokens"]]

        def attention_bank(x, v):
            n = x["chunks"].stop - x["chunks"].start
            return tile_bank[v % 3][x["parts"], 0:n * P].rearrange("p (c q) -> p c q", q=P)[:, :, 0:x["nq"]]

        def g_out(c):
            return gt[:, c].rearrange("p (g i) -> p g i", g=4)

        def ev_fill(i):
            return 4 + 3 * i // 2, 4 + 3 * (i + 1) // 2

        def window_units():
            for m in range(3):
                for h in range(8):
                    yield m, h

        BATCHES = [(c, d) for c in range(3) for d in range(2)]
        SCAN = [((0, i), (1, 2 - i)) for i in range(3)]
        DELTA_BANKS = ((b4, b5, b6, b7), tuple(tile_bank))

        def n_levels(n):
            return n.bit_length() - 1

        def level_at(c, level, d):
            return 2 * sum(n_levels(e - s) for s, e in TILES[:c]) + 2 * level + d

        def step_at(c, level, d):
            return level_at(c, level, d) - 2 * (c + 1)

        def batch_place(j):
            return sum(4 * (TILES[c][1] - TILES[c][0]) for c, _ in BATCHES[:j])

        def batch_size(j):
            c = BATCHES[j][0]
            return 4 * (TILES[c][1] - TILES[c][0])

        def inverse(j):
            return inner[:, 2176 + batch_place(j):2176 + batch_place(j) + batch_size(j)]

        def inner_product(j):
            return inner[:, batch_place(j):batch_place(j) + batch_size(j)]

        def decayed_queries(c, d):
            s, e = TILES[c]
            return (qe_f, qe_b)[d][:, 4 * s:4 * e]

        def delta_turns():
            for source in (8, 4):
                for m in range(3):
                    yield m, source

        def ws_rows_at(g):
            return ws_rows[:, g // 4, g % 4 * P:(g % 4 + 1) * P]

        def first_of(name):
            return phases[name].first

        block = ctx.enter_context(nc.Block())

        @block.sync
        def _(sp):
            sp.dma_start(x_rows, w["x"][0].rearrange("(m p) d -> p m d", p=P)).then_inc(x_in, 16)
            for i, name in enumerate(("attn_norm_g", "mlp_norm_g", "norm_mix_2", "norm_mem_q_2", "norm_mem_kv_2", "norm_ffn_2")):
                sp.dma_start(gain_rows[16 * i:16 * i + 16], w[name].rearrange("l (k p) -> (l k) p", p=P))\
                    .then_inc(gains_in, 16)
            sp.dma_start(meta_rows[0:NMETA], w["meta_tokens"]).then_inc(x_in, 16)
            sp.dma_start(ident, w["shape_tables"][:, 0:P]).then_inc(ident_in, 16)

            def load(b, loads, g=None):
                if b >= 2:
                    sp.wait_ge(low_split, looped(4 * (b - 1), 4 * LOOP_BLOCKS, g))
                for into, width, source in loads:
                    chunks = source.shape[1]
                    slot = raw[:, b % 2]
                    if wide[b]:
                        target = slot.rearrange("p (k two) n -> p k (two n)", two=2)[:, 0:chunks]
                    else:
                        target = slot[:, 0:chunks, into:into + width]
                    sp.dma_start(target, source).then_inc(raw_in[b % 2], 16)

            for name, ph in phases.items():
                if ph.up is not None:
                    load(ph.first, ph.blocks[0])
                    with sp.Fori(0, (N_UNITS - 2) // LOOP_UNITS) as g:
                        load(ph.first + 1, [(0, BLOCK, ph.up[2 * g + 1])], g)
                        load(ph.first + 2, [(None, 0, ph.down[2 * g])], g)
                        load(ph.first + 3, [(0, BLOCK, ph.up[2 * g + 2])], g)
                        load(ph.first + 4, [(None, 0, ph.down[2 * g + 1])], g)
                    for i in range(ph.n - 3, ph.n):
                        load(ph.first + i, ph.blocks[i])
                else:
                    for i, loads in enumerate(ph.blocks):
                        load(ph.first + i, loads)
                        if ph.first + i == 0:
                            sp.dma_start(cst[:, P:cw], w["shape_tables"][:, P:cw]).then_inc(cst_in, 16)

        @block.tensor
        def _(pe):
            op = [0]

            def split_ready(b, q, g=None):
                pe.wait_ge(low_split, looped(4 * b + q + 1, 4 * LOOP_BLOCKS, g))

            def transposed_tile(q, x, ts, bank, ready=None):
                n = ts.stop - ts.start
                for k in range(KD):
                    if ready is not None:
                        pe.wait_ge(operand_split, ready + k + 1)
                    for i, (wx, ux) in enumerate(((w_hi, 0), (w_hi, 1), (w_lo, 0))):
                        mm = pe.matmul(bank[:, 0:n], wx[:, q, k * P:(k + 1) * P], x[ux][:, k, ts],
                                       start=k == 0 and i == 0, stop=k == KD - 1 and i == 2)
                return mm

            def token_tile(q, n_quarters, n, x, ts, bank, at):
                for k in range(KD):
                    for i, (ux, wx) in enumerate(((0, w_hi), (0, w_lo), (1, w_hi))):
                        mm = pe.matmul(bank[:, at:at + n_quarters * n].rearrange("p (q n) -> p q n", n=n), x[ux][:, k, ts],
                                       wx[:, q:q + n_quarters, k * P:k * P + n],
                                       start=k == 0 and i == 0, stop=k == KD - 1 and i == 2)
                return mm

            def bank_free(b, t, g=None):
                if tile_at[b] + t >= 4:
                    pe.wait_ge(tile_read, looped(tile_at[b] + t - 3, LOOP_TILES, g))

            def block_t(b, x, ts, ready=None, norm=None, then=None, g=None):
                for t in range(4):
                    if t == 2 and norm is not None:
                        norm_sum(norm)
                        if then is not None:
                            then()
                    tile_t(b, t, x, ts, ready if t == 0 else None, g)

            def tile_t(b, t, x, ts, ready=None, g=None):
                split_ready(b, t, g)
                bank_free(b, t, g)
                transposed_tile(t, x, ts, tile_bank[t], ready).then_inc(tile_summed, 1)

            def block_wide(b, unit, chunks, ts, ready, g=None):
                n = ts.stop - ts.start
                for t in range(8):
                    if t % 2 == 0:
                        split_ready(b, t // 2, g)
                    bank_free(b, t, g)
                    cols = slice(t % 2 * P, (t % 2 + 1) * P)
                    hi, lo = quarter(w_hi, b, t // 2), quarter(w_lo, b, t // 2)
                    for k in range(chunks):
                        if t == 0:
                            pe.wait_ge(operand_split, looped(ready + k + 1, 4 * LOOP_UNITS, g))
                        at_k = 4 * (unit % 2) + k
                        pe.matmul(tile_bank[t % 4][:, 0:n], hi[:, k, cols], a_hi[:, at_k, ts], start=k == 0, stop=False)
                        pe.matmul(tile_bank[t % 4][:, 0:n], hi[:, k, cols], a_lo[:, at_k, ts], start=False, stop=False)
                        mm = pe.matmul(tile_bank[t % 4][:, 0:n], lo[:, k, cols], a_hi[:, at_k, ts], start=False,
                                       stop=k == chunks - 1)
                    mm.then_inc(tile_summed, 1)

            def block_v(b, x, offset):
                for t in range(4):
                    tile_v(b, t, x, offset)

            def tile_v(b, t, x, offset):
                if t % 2 == 0:
                    split_ready(b, t + 1)
                bank_free(b, t)
                at_ = offset + t % 2 * P
                token_tile(t // 2 * 2, 2, P, x, slice(at_, at_ + P), tile_bank[t], 0).then_inc(tile_summed, 1)

            u, a = (u_hi, u_lo), (a_hi, a_lo)

            norms = [0]

            def norm_sum(ts=slice(0, T)):
                n = norms[0]
                norms[0] += 1
                pe.wait_ge(sum_added, 8 * (n + 1))
                pe.matmul(b7[:, 0:ts.stop - ts.start], ones, square_sum[:, ts], start=True, stop=True)\
                    .then_inc(norm_summed, 1)

            turns = [0]

            def norm_turn(source, starts):
                pe.wait_ge(rs_ready, norms[0])
                if turns[0]:
                    pe.wait_ge(rs_tok_ready, turns[0])
                for i, s in enumerate(starts):
                    mm = pe.transpose(b6[:, i * P:(i + 1) * P], source[:, s:s + P], ident)
                turns[0] += 1
                mm.then_inc(rs_turned, 1)

            hn = [0]
            ropes = [0]

            def hn_sum(u_, tiles, n, matrix):
                pe.wait_ge(hn_squared, u_ + 1)
                if u_ >= 2:
                    pe.wait_ge(hn_ln, u_ - 1)
                for i in range(tiles):
                    mm = pe.matmul((b4, b5)[u_ % 2][:, 0:n], matrix, hn_sq[:, u_ % 2, i * n:(i + 1) * n],
                                   start=i == 0, stop=i == tiles - 1)
                mm.then_inc(hn_summed, 1)

            def hn_swap(u_, r, n, swap):
                pe.wait_ge(hn_scaled, u_ + 1)
                if r >= 2:
                    pe.wait_ge(hn_roped, r - 1)
                pe.matmul((b6, b7)[r % 2][:, 0:n], swap, hn_n[:, r % 2, 0:n], start=True, stop=True)\
                    .then_inc(hn_swapped, 1)

            def head_norms(units, swap=None, between=None):
                base, r0 = hn[0], ropes[0]
                for i, (tiles, n, matrix) in enumerate(units):
                    hn_sum(base + i, tiles, n, matrix)
                    if swap is not None and i >= 1:
                        hn_swap(base + i - 1, r0 + i - 1, units[i - 1][1], swap)
                    if between is not None:
                        between(i)
                if swap is not None:
                    hn_swap(base + len(units) - 1, r0 + len(units) - 1, units[-1][1], swap)
                    ropes[0] += len(units)
                hn[0] += len(units)

            at = [0]

            def attention(units, following):
                base, split0, n = at[0], op[0], len(units)

                def scores(i):
                    x, v = units[i], base + i
                    if v >= 2:
                        pe.wait_ge(at_exp, v - 1)
                    for c, (q, k) in enumerate(zip(x["q"], x["k"])):
                        mm = pe.matmul((b4, b5)[v % 2][0:x["nq"], 0:x["nk"]], q, k, start=c == 0,
                                       stop=c == len(x["q"]) - 1)
                    mm.then_inc(at_scored, 1)

                def turn(i):
                    x, v = units[i], base + i
                    pe.wait_ge(at_prob, v + 1)
                    if v >= 2:
                        pe.wait_ge(at_copied, v - 1)
                    for c, (rows, first, _) in enumerate(x["keys"]):
                        mm = pe.transpose((b6, b7)[v % 2][0:rows, c * P:c * P + x["nq"]],
                                          at_p[0:x["nq"], v % 3, first:first + rows], ident[0:x["nq"], 0:x["nq"]])
                    mm.then_inc(at_turned, 1)

                def values(i):
                    x, v = units[i], base + i
                    pe.wait_ge(at_copied, v + 1)
                    if i >= 3:
                        pe.wait_ge(operand_split, split0 + i - 2)
                    nv = len(x["keys"][0][2])
                    for r in range(nv):
                        for c, (rows, _, vs) in enumerate(x["keys"]):
                            mm = pe.matmul(tile_bank[v % 3][x["parts"], r * P:r * P + x["nq"]], vs[r],
                                           at_pt[0:rows, v % 2, c, 0:x["nq"]], start=c == 0,
                                           stop=c == len(x["keys"]) - 1)
                    mm.then_inc(at_summed, 1)

                pe.wait_ge(tile_read, tile_at[first_of(following)])
                for k in range(n + 5):
                    if k < n:
                        scores(k)
                    if 0 <= k - 3 < n:
                        turn(k - 3)
                    if k >= 5:
                        values(k - 5)
                at[0] += n
                op[0] += n

            def out_product(name, ts):
                pe.wait_ge(operand_split, op[0])
                for i in range(phases[name].n):
                    block_t(phases[name].first + i, a, ts)

            def mlp_relu(name, ts):
                first, ready = phases[name].first, hidden_ready()
                base = op[0]
                block_t(first, u, ts, ready=ready, norm=ts)
                with pe.Fori(0, (N_UNITS - 2) // LOOP_UNITS) as g:
                    block_t(first + 1, u, ts, g=g)
                    block_wide(first + 2, 0, 4, ts, base, g)
                    block_t(first + 3, u, ts, g=g)
                    block_wide(first + 4, 1, 4, ts, base + 4, g)
                last = first + phases[name].n - 3
                block_t(last, u, ts)
                for i in (N_UNITS - 2, N_UNITS - 1):
                    block_wide(last + i - N_UNITS + 3, i, 4, ts, base + 4 * i)
                op[0] += D_FF // P

            def mlp_swiglu(name, ts):
                b, ready = phases[name].first, hidden_ready()
                base = op[0]
                for i in range(D_FF2 // HALF):
                    block_t(b, u, ts, ready=ready if i == 0 else None, norm=ts if i == 0 else None)
                    b += 1
                    if i % 2 == 0 and i >= 2:
                        block_wide(b, i // 2 - 1, 4, ts, base + 2 * i - 4)
                        b += 1
                block_wide(b, D_FF2 // UNIT, D_FF2 % UNIT // P, ts, base + D_FF2 // UNIT * 4)
                op[0] += D_FF2 // P

            def hidden_ready():
                op[0] += KD
                return op[0] - KD

            def gated_delta():
                for i, (m, source) in enumerate(delta_turns()):
                    s, e = TILES[m]
                    if i >= 2:
                        pe.wait_ge(M["d_copied"], i - 1)
                    if i == 0:
                        pe.wait_ge(hn_scaled, hn[0])
                    for h in range(A_HEADS):
                        mm = pe.transpose((b4, b5)[i % 2][0:e - s, h * P:(h + 1) * P],
                                          qkv[:, source + h, s:e], ident)
                    mm.then_inc(M["d_turned"], 1)
                pe.wait_ge(M["d_gates"], 1)
                for c, (s, e) in enumerate(TILES):
                    n = e - s
                    for d in range(2):
                        mm = pe.matmul(b6[0:n, 8 * c + 4 * d:8 * c + 4 * d + 4], table(("tri_f", "tri_b")[d])[0:n, 0:n],
                                       decay[0:n, c, 4 * d:4 * d + 4], start=True, stop=True)
                mm.then_inc(M["d_cum"], 1)
                pe.wait_ge(M["d_cum_read"], 1)
                pe.wait_ge(M["d_copied"], 6)
                for c, (s, e) in enumerate(TILES):
                    n = e - s
                    hs = [slice(h * n, (h + 1) * n) for h in range(A_HEADS)]
                    last = n_levels(e - s) - 1
                    for d in range(2):
                        rows, kk, kq, _ = DELTA_BANKS[d]
                        if c >= 1:
                            pe.wait_ge(M["d_egr"], 2 * (c - 1) + d + 1)
                            pe.wait_ge(M["d_n"], 2 * (c - 1) + d + 1)
                            pe.wait_ge(M["d_x"], level_at(c, 0, d) - 1)
                        for h in range(A_HEADS):
                            g = decay[0:n, c, 4 * d + h:4 * d + h + 1].to_broadcast([n, P])
                            mm = pe.matmul(rows[:, hs[h]], g, table(("tri_f", "tri_b")[d])[0:n, 0:n], start=True, stop=True)
                        mm.then_inc(M["d_rows"], 1)
                        for h in range(A_HEADS):
                            pe.matmul(kk[0:n, hs[h]], qkv[:, 4 + h, s:e], qkv[:, 4 + h, s:e], start=True, stop=True)
                        for h in range(A_HEADS):
                            mm = pe.matmul(kq[0:n, hs[h]], qkv[:, 4 + h, s:e], qkv[:, h, s:e], start=True, stop=True)
                        mm.then_inc(M["d_gk"], 1)
                    for d in range(2):
                        pe.wait_ge(M["d_nb"], level_at(c, 0, d) + 1)
                        pe.wait_ge(M["d_n"], 2 * c + d + 1)
                        for h in hs:
                            mm = pe.transpose(DELTA_BANKS[d][1][0:n, h], nb_[d][0:n, h], ident[0:n, 0:n])
                        mm.then_inc(M["d_y"], 1)
                    for level in range(1, last + 1):
                        for d in range(2):
                            pe.wait_ge(M["d_nb"], level_at(c, level, d) + 1)
                            pe.wait_ge(M["d_x"], level_at(c, level - 1, d) + 1)
                            for h in hs:
                                mm = pe.matmul(DELTA_BANKS[d][3][0:n, h], nb_[d][0:n, h], xt[d][0:n, h], start=True, stop=True)
                            mm.then_inc(M["d_w"], 1)
                        for d in range(2):
                            x = inverse(2 * c + d)
                            _, xnx, xnx_t, _ = DELTA_BANKS[d]
                            pe.wait_ge(M["d_w_copied"], step_at(c, level, d) + 1)
                            for h in hs:
                                mm = pe.matmul(xnx[0:n, h], wt[d][0:n, h], x[0:n, h], start=True, stop=True)
                            if level < last:
                                for h in hs:
                                    mm = pe.matmul(xnx_t[0:n, h], x[0:n, h], wt[d][0:n, h], start=True, stop=True)
                            mm.then_inc(M["d_y"], 1)
                pe.wait_ge(M["d_x"], level_at(3, 0, 0))
                for i, pair in enumerate(SCAN):
                    before = [2 * (i - 1) + d + 1 for d in range(2)]
                    if i >= 1:
                        for d, c in pair:
                            s, e = TILES[c]
                            pe.wait_ge(M["d_s_read"], before[d])
                            for h in range(A_HEADS):
                                mm = pe.matmul(DELTA_BANKS[d][0][0:e - s, h * P:(h + 1) * P], qkv[:, 4 + h, s:e],
                                               state[:, d, h], start=True, stop=True)
                            mm.then_inc(M["d_ks"], 1)
                    for d, c in pair:
                        n = TILES[c][1] - TILES[c][0]
                        x = inverse(2 * c + d)
                        pe.wait_ge(M["d_r"], 2 * i + d + 1)
                        if i >= 1:
                            pe.wait_ge(M["d_vnew"], before[d])
                        for h in range(A_HEADS):
                            mm = pe.matmul(DELTA_BANKS[d][1][0:n, h * P:(h + 1) * P], x[0:n, h * n:(h + 1) * n],
                                           scan_r[d][0:n, h * P:(h + 1) * P], start=True, stop=True)
                        mm.then_inc(M["d_v"], 1)
                    for d, c in pair:
                        n = TILES[c][1] - TILES[c][0]
                        qx, qe = inner_product(2 * c + d), decayed_queries(c, d)
                        _, _, out_bank, state_bank = DELTA_BANKS[d]
                        pe.wait_ge(M["d_vnew"], 2 * i + d + 1)
                        if i >= 1:
                            pe.wait_ge(M["d_o_read"], before[d])
                        for h in range(A_HEADS):
                            o = out_bank[:, h * n:(h + 1) * n]
                            mm = pe.matmul(o, scan_v[d][0:n, h * P:(h + 1) * P], qx[0:n, h * n:(h + 1) * n],
                                           start=True, stop=i == 0)
                            if i >= 1:
                                mm = pe.matmul(o, state[:, d, h], qe[:, h * n:(h + 1) * n], start=False, stop=True)
                        mm.then_inc(M["d_o"], 1)
                        if i < 2:
                            pe.wait_ge(M["d_kdec"], 2 * i + d + 1)
                            for h in range(A_HEADS):
                                mm = pe.matmul(state_bank[:, h * P:(h + 1) * P], scan_k[d][0:n, h * P:(h + 1) * P],
                                               scan_v[d][0:n, h * P:(h + 1) * P], start=True, stop=True)
                            mm.then_inc(M["d_s"], 1)
                pe.wait_ge(M["d_o_read"], 6)

            def spatial_gating():
                pe.wait_ge(ws_in, 16)
                for i in range(2):
                    for g in range(4):
                        mm = pe.transpose((b4, b5)[i][:, g * P:(g + 1) * P], ws_rows_at(4 * i + g), ident)
                    mm.then_inc(M["ws_turned"], 1)
                pe.wait_ge(M["ws_read"], 2)
                pe.wait_ge(M["g_n"], 1)
                for c in range(2):
                    for g in range(8):
                        half = slice(64 * (g % 2), 64 * (g % 2) + 64)
                        mm = pe.matmul((b4, b5)[c][half, g // 2 * P:(g // 2 + 1) * P], gv[:, c, g * 64:(g + 1) * 64],
                                       ws_t[:, g], start=True, stop=True)
                    mm.then_inc(M["g_mixed"], 1)

            def linear_attention(memory_tiles):
                pe.wait_ge(wg_in, 16)
                for i in range(2 * KD):
                    mm = pe.matmul(b4[0:16, 0:SEQ], wg1[:, i % KD], u[i // KD][:, i % KD, REAL].bitcast(F32),
                                   start=i == 0, stop=i == 2 * KD - 1)
                mm.then_inc(M["l_low"], 1)
                memory_tiles(0, 2)
                pe.wait_ge(M["l_lowc"], 1)
                for h in range(4):
                    if h >= 2:
                        pe.wait_ge(M["l_gate"], h - 1)
                    pe.matmul((b5, b6)[h % 2][:, 0:SEQ], wg2[0:16, h * P:(h + 1) * P], squares[0:16, 0, 0:SEQ],
                              start=True, stop=True).then_inc(M["l_e1"], 1)
                memory_tiles(2, 8)
                pe.wait_ge(M["l_ks"], 1)
                pe.wait_ge(M["l_gate"], 4)
                for m in range(2):
                    for h in range(4):
                        mm = pe.transpose((b4, b5)[m][:, h * P:(h + 1) * P], ks_t[:, h, m * P:(m + 1) * P], ident)
                    mm.then_inc(M["l_kst"], 1)
                pe.wait_ge(M["l_qk"], 1)
                for c in range(4):
                    half, cs = slice(64 * (c % 2), 64 * (c % 2) + 64), slice(64 * c, 64 * c + 64)
                    for h in range(4):
                        at_c = (c // 2 * 4 + h) * 64
                        mm = pe.matmul(b6[half, at_c:at_c + 64], lk[:, h, cs], lq[:, h, cs], start=True, stop=True)
                mm.then_inc(M["l_att"], 1)
                memory_tiles(8, 10)
                pe.wait_ge(M["l_attc"], 1)
                pe.wait_ge(M["l_kstc"], 2)
                for c in range(4):
                    half, cs = slice(64 * (c % 2), 64 * (c % 2) + 64), slice(64 * c, 64 * c + 64)
                    m = c // 2
                    if c >= 1:
                        pe.wait_ge(M["l_oc"], c)
                        pe.wait_ge(M["l_dsr"], c)
                    for h in range(4):
                        for r in range(2):
                            vs = slice((2 * h + r) * P, (2 * h + r + 1) * P)
                            o = b7[:, (2 * h + r) * 64:(2 * h + r + 1) * 64]
                            mm = pe.matmul(o, lv[half, m, vs], att64[half, m, h], start=True, stop=c == 0)
                            if c >= 1:
                                mm = pe.matmul(o, l_state[:, h, r * P:(r + 1) * P], lq[:, h, cs], start=False, stop=True)
                    mm.then_inc(M["l_o"], 1)
                    if c < 3:
                        for h in range(4):
                            mm = pe.matmul((b4, b5)[h // 2][:, h % 2 * 256:(h % 2 + 1) * 256], kst[half, m, h],
                                           lv[half, m, h * 256:(h + 1) * 256], start=True, stop=True)
                        mm.then_inc(M["l_ds"], 1)
                        memory_tiles(10 + 2 * c, 12 + 2 * c)
                pe.wait_ge(M["l_oc"], 4)

            def closing():
                pe.wait_ge(tile_read, tile_at[n_blocks])
                for m in range(2):
                    for k4 in range(2):
                        turn_rows(tile_bank, [(k * P, P, hidden[:, 4 * k4 + k, NMETA + m * P:NMETA + (m + 1) * P]) for k in range(4)])

            pe.wait_ge(ident_in, 16)
            n_turn = [0]

            def turn_rows(banks, jobs):
                n = n_turn[0]
                if n >= len(banks):
                    pe.wait_ge(turn_read, n - len(banks) + 1)
                for lo, rows, source in jobs:
                    mm = pe.transpose(banks[n % len(banks)][:, lo:lo + rows], source, ident[0:rows, 0:rows])
                mm.then_inc(turned, 1)
                n_turn[0] += 1

            pe.wait_ge(gains_in, 16 * N_GAIN_LOADS)
            turn_rows(tile_bank, [(0, 96, gain_rows[0:96])])
            pe.wait_ge(x_in, 32)
            for k in range(KD):
                ks = slice(k * P, (k + 1) * P)
                turn_rows(tile_bank, [(0, NMETA, meta_rows[0:NMETA, ks])]
                          + [(NMETA + m * P, P, x_rows[:, m, ks]) for m in range(2)])
            pe.wait_ge(turn_read, n_turn[0])

            def turn_late_rows():
                pe.wait_ge(rows_in, 16 * N_ROW_LOADS)
                turn_rows((b4,), [(0, N_LATE_ROWS, late_rows[0:N_LATE_ROWS])])

            full = slice(0, T)
            pe.wait_ge(cst_in, 16)
            block_t(first_of("ab_qkvz"), u, full, ready=hidden_ready(), norm=full, then=turn_late_rows)
            for i in range(1, 4):
                block_t(first_of("ab_qkvz") + i, u, slice(0, T))
            block_t(first_of("ab_qb"), u, slice(0, T))
            b = first_of("ab_kvb")
            for t in range(3):
                split_ready(b, t if t < 2 else 3)
                bank_free(b, t)
                transposed_tile(t, u, full, tile_bank[t]).then_inc(tile_summed, 1 if t < 2 else 2)
            pe.wait_ge(tile_read, tile_at[b + 1])
            for m, (s, e) in enumerate(TILES):
                pe.transpose(b6[0:e - s, m * P:(m + 1) * P], hn_t[:, 0, s:e], ident)
                mm = pe.transpose(b7[0:e - s, m * 16:(m + 1) * 16], hn_t[0:16, 1, s:e], ident[0:16, 0:16])
            mm.then_inc(M["ab_turned"], 1)

            head_norms([(1, T, blk64)] * 5)
            pe.wait_ge(hn_scaled, hn[0])
            pe.wait_ge(M["kv_dup"], 1)
            pe.wait_ge(M["ab_turn_read"], 1)
            units = []
            for m, h in window_units():
                lo, hi = TILES[m]
                half = slice(64 * (h % 2), 64 * (h % 2) + 64)
                g = h // 4
                units.append(dict(
                    q=[qb[half, h // 2, lo:hi]], k=[kdup[half, g]], nq=hi - lo, nk=T, parts=half,
                    keys=[(e - s, s, [vb[0:e - s, c, 64 * g:64 * g + 64]]) for c, (s, e) in enumerate(TILES)]))
            attention(units, "ab_out")

            pe.wait_ge(M["silu_done"], 12)
            head_norms([(1, T, ones)] * 8)
            gated_delta()
            head_norms([(1, T, ones)] * 4)
            op[0] += 4
            out_product("ab_out", slice(0, T))
            mlp_relu("mlp0", full)

            ready = hidden_ready()
            for i in range(2):
                block_t(first_of("c_q") + i, u, REAL, ready=ready if i == 0 else None, norm=full if i == 0 else None)
                if i == 0:
                    norm_turn(rs, [0, 16, 144])
            pe.wait_ge(mem_in, 16)
            for k in range(KD):
                turn_rows((b4, b5), [(m * P, P, mem_rows[:, m, k * P:k * P + P]) for m in range(2)])
            b = first_of("c_kv")
            for t in range(2):
                split_ready(b, t)
                bank_free(b, t)
                transposed_tile(t, u, slice(0, T), tile_bank[t]).then_inc(tile_summed, 1)
            split_ready(b, 3)
            bank_free(b, 2)
            for m, s in enumerate((16, 144)):
                mm = token_tile(2, 2, P, u, slice(s, s + P), tile_bank[2], m * HALF)
            mm.then_inc(tile_summed, 1)
            bank_free(b, 3)
            token_tile(2, 2, P, u, slice(0, P), tile_bank[3], 0).then_inc(tile_summed, 1)
            norm_sum(slice(0, SEQ))
            norm_turn(rs_mem, [0, P])
            pe.wait_ge(turn_read, n_turn[0])
            pe.wait_ge(rs_tok_ready, turns[0])
            head_norms([(1, SEQ, ones)] * 8 + [(1, T, ones)] * 2, table("swap_pairs"))
            pe.wait_ge(hn_roped, ropes[0])
            pe.wait_ge(tile_read, tile_at[b + 1])
            units = []
            for m in range(2):
                for h in range(8):
                    g = h // 4
                    units.append(dict(
                        q=[qc[:, h, m * P:m * P + P]], k=[kc[:, g]], nq=P, nk=T, parts=slice(0, P),
                        keys=[(e - s, s, [vc[0:e - s, c, g * P:g * P + P]]) for c, (s, e) in enumerate(TILES)]))
            attention(units, "c_out")
            out_product("c_out", REAL)
            mlp_relu("mlp1", REAL)

            for layer in range(2):
                ready = hidden_ready()
                name = ("ev_in", "od_in")[layer]
                b = first_of(name)
                if layer == 0:
                    block_t(b, u, REAL, ready=ready, norm=REAL)
                    norm_turn(rs, [16, 144])
                    block_t(b + 1, u, REAL)
                    block_v(b + 2, u, NMETA)
                    block_t(b + 3, u, REAL)
                    block_v(b + 4, u, NMETA)
                else:
                    block_t(b, u, REAL, ready=ready, norm=REAL)
                    norm_turn(rs, [16, 144])
                    block_t(b + 1, u, REAL)
                    block_v(b + 2, u, NMETA)
                    block_v(b + 3, u, NMETA)
                    block_t(b + 4, u, REAL)
                    block_t(b + 5, u, REAL)
                op[0] += KD
                pe.wait_ge(operand_split, op[0])

                def memory_tiles(lo, hi):
                    for n in range(lo, hi):
                        b, t = first_of(f"xkv{layer}") + n // 4, n % 4
                        if n < 8:
                            tile_t(b, t, a, slice(0, SEQ))
                        else:
                            tile_v(b, t, a, 0)

                if layer == 0:
                    memory_tiles(0, 4)
                    head_norms([(1, SEQ, blk64)] * 8, table("swap_halves"), between=lambda i: memory_tiles(*ev_fill(i)))
                    pe.wait_ge(hn_roped, ropes[0])
                    units = []
                    for m in range(2):
                        for h in range(8):
                            half = slice(64 * (h % 2), 64 * (h % 2) + 64)
                            units.append(dict(
                                q=[mq[half, h // 2, m * P:m * P + P]], k=[mk[half, h // 2, 0:(m + 1) * P]], nq=P,
                                nk=(m + 1) * P, parts=half,
                                keys=[(P, c * P, [mv[:, c, 64 * h:64 * h + 64]]) for c in range(m + 1)]))
                    attention(units, "mix_out0")
                    spatial_gating()
                    op[0] += 2
                else:
                    linear_attention(memory_tiles)
                    head_norms([(2, SEQ, ones)] * 4)
                    op[0] += 8
                out_product(f"mix_out{layer}", REAL)
                b = first_of(f"xq{layer}")
                block_t(b, u, REAL, ready=hidden_ready(), norm=REAL)
                head_norms([(2, SEQ, ones)] * 4, between=lambda t: tile_t(b + 1, t, u, REAL))
                head_norms([(2, SEQ, ones)] * 4)
                pe.wait_ge(hn_scaled, hn[0])
                units = []
                for m in range(2):
                    for h in range(4):
                        units.append(dict(
                            q=[xq[:, 2 * h + c, m * P:m * P + P] for c in range(2)],
                            k=[xk[:, 2 * h + c] for c in range(2)], nq=P, nk=SEQ, parts=slice(0, P),
                            keys=[(P, c * P, [xv[:, c, (2 * h + r) * P:(2 * h + r + 1) * P] for r in range(2)])
                                  for c in range(2)]))
                attention(units, f"x_out{layer}")
                out_product(f"x_out{layer}", REAL)
                mlp_swiglu(f"swiglu{layer}", REAL)
            closing()

        @block.scalar
        def _(act):
            op, fin, step = [0], [0], [0]

            def link(ins):
                step[0] += 1
                ins.then_inc(act_step, 1)
                act.wait_ge(act_step, step[0])

            def split_high(b, q, g=None):
                if b >= n_blocks:
                    return
                if q == 0:
                    act.wait_ge(raw_in[b % 2], looped(landed_at[b], LOOP_LANDED, g))
                if b >= 1:
                    act.wait_ge(tile_summed, looped(quarter_done[b - 1][q], LOOP_TILES, g))
                act.activation(quarter(w_hi, b, q), raw_quarter(b, q), ACT.Copy).then_inc(high_split, 1)

            def stream(name, evac, start=0, n=None):
                ph = phases[name]
                for i in range(start, ph.n if n is None else start + n):
                    for t in range(4):
                        evac(i, t)
                        split_high(ph.first + i + 1, t)

            def nothing(i, t):
                pass

            def finish_chunk(k, norm, ready, ts, source=None):
                f = fin[0]
                fin[0] += 1
                x = hidden[:, k, ts] if source is None else source
                act.wait_ge(*ready)
                act.activation(u_hi[:, k, ts], x, ACT.Copy, scale=gain(norm, k)).then_inc(operand_high, 1)
                op[0] += 1
                if f >= 2:
                    act.wait_ge(sum_added, f - 1)
                act.activation(squares[:, f % 2, ts], x, ACT.Square).then_inc(squared, 1)

            norms = [0]

            def norm_rs(target, n, scale=1.0 / D):
                norms[0] += 1
                act.wait_ge(norm_summed, norms[0])
                act.activation(target, b7[:, 0:n], ACT.Ln, bias=eps, scale=scale).then_inc(norm_ln, 1)
                act.wait_ge(norm_ln, norms[0])
                act.activation(target, target, ACT.Exp, scale=-0.5).then_inc(rs_ready, 1)

            hn = [0]

            def head_norms(units, between=None):
                base, n = hn[0], len(units)

                def square(i):
                    source, columns, _, tokens, wait = units[i]
                    v = base + i
                    act.wait_ge(*wait)
                    if v >= 2:
                        act.wait_ge(hn_summed, v - 1)
                    act.activation(hn_sq[:, v % 2, 0:columns], source, ACT.Square).then_inc(hn_squared, 1)

                def scale(i):
                    _, _, mean, tokens, _ = units[i]
                    v = base + i
                    act.wait_ge(hn_summed, v + 1)
                    if v >= 2:
                        act.wait_ge(hn_scaled, v - 1)
                    act.activation(hn_r[:, v % 2, 0:tokens], (b4, b5)[v % 2][:, 0:tokens], ACT.Ln, bias=eps,
                                   scale=mean).then_inc(hn_ln, 1)
                    act.wait_ge(hn_ln, v + 1)
                    act.activation(hn_r[:, v % 2, 0:tokens], hn_r[:, v % 2, 0:tokens], ACT.Exp, scale=-0.5)\
                        .then_inc(hn_rs, 1)

                square(0)
                for i in range(n):
                    if i + 1 < n:
                        square(i + 1)
                    scale(i)
                    if between is not None:
                        between(i)
                hn[0] += n

            at = [0]

            def attention(units):
                base, n = at[0], len(units)

                def exponent(i):
                    x, v = units[i], base + i
                    q, s = slice(0, x["nq"]), v % 2
                    act.wait_ge(at_max, v + 1)
                    if v >= 3:
                        act.wait_ge(at_turned, v - 2)
                    if v >= 2:
                        act.wait_ge(at_prob, v - 1)
                    logits = at_s[q, s, 0:x["nk"]] if x["kind"] else (b4, b5)[s][q, 0:x["nk"]]
                    if x["kind"] == "window":
                        act.activation(at_es[q, s], sink[q, x["head"]:x["head"] + 1], ACT.Exp, bias=at_nm[q, s])
                    act.activation(at_p[q, v % 3, 0:x["nk"]], logits, ACT.Exp, bias=at_nm[q, s], accum_out=at_den[q, s])\
                        .then_inc(at_exp, 1)

                def copy(i):
                    x, v = units[i], base + i
                    act.wait_ge(at_turned, v + 1)
                    if v >= 2:
                        act.wait_ge(at_summed, v - 1)
                    rows = x["rows"]
                    c = 0
                    while c < len(rows):
                        e = c
                        while e < len(rows) and rows[e] == rows[c]:
                            e += 1
                        ins = act.activation(at_pt[0:rows[c], v % 2, c:e, 0:x["nq"]],
                                             (b6, b7)[v % 2][0:rows[c], c * P:e * P].rearrange("p (c q) -> p c q", q=P)[:, :, 0:x["nq"]],
                                             ACT.Copy)
                        c = e
                    ins.then_inc(at_copied, 1)

                def result(i):
                    x, v = units[i], base + i
                    act.wait_ge(at_summed, v + 1)
                    act.activation(attention_out(a_hi, x), attention_bank(x, v), ACT.Copy).then_inc(operand_high, 1)
                    op[0] += 1

                for k in range(n + 5):
                    if 0 <= k - 3 < n:
                        copy(k - 3)
                    if k >= 5:
                        result(k - 5)
                    if k < n:
                        exponent(k)
                at[0] += n

            def residual(name, norm, ts):
                def evac(i, t):
                    finish_chunk(4 * i + t, norm, (tile_read, tile_at[phases[name].first + i] + t + 1), ts)
                stream(name, evac)

            ff = [0]

            def mlp_relu(name, norm, ts):
                first, base, f0 = phases[name].first, op[0], ff[0]

                def up(b, unit, g=None):
                    for t in range(4):
                        act.wait_ge(ff_ready, looped(f0 + 4 * unit + t + 1, 4 * LOOP_UNITS, g))
                        act.activation(a_hi[:, 4 * (unit % 2) + t, ts], ff_a[:, t % 2, ts], ACT.Copy).then_inc(operand_high, 1)
                        split_high(b + 1, t, g)

                def down(b, g=None):
                    for q in range(4):
                        split_high(b + 1, q, g)

                up(first, 0)
                with act.Fori(0, (N_UNITS - 2) // LOOP_UNITS) as g:
                    up(first + 1, 1, g)
                    down(first + 2, g)
                    up(first + 3, 2, g)
                    down(first + 4, g)
                last = first + phases[name].n - 3
                up(last, N_UNITS - 1)
                down(last + 1)
                op[0] = base + D_FF // P
                ff[0] += D_FF // P
                closing_down(last + 2, norm, ts)

            def closing_down(b, norm, ts):
                for k in range(KD):
                    if norm is not None:
                        finish_chunk(k, norm, (tile_read, tile_at[b] + k + 1), ts)
                    if k % 2 == 1:
                        split_high(b + 1, k // 2)

            def mlp_swiglu(name, norm, ts):
                b, n = phases[name].first, ts.stop - ts.start
                for i in range(D_FF2 // HALF):
                    for t in range(4):
                        if t < 2:
                            act.wait_ge(tile_read, tile_at[b] + t + 1)
                            act.activation(ff_s[:, t, 0:n], ff_z[:, t, 0:n], ACT.Silu).then_inc(silu_ready, 1)
                        else:
                            ff[0] += 1
                            act.wait_ge(ff_ready, ff[0])
                            act.activation(a_hi[:, 2 * (i % 4) + t - 2, ts], ff_a[:, t - 2, 0:n], ACT.Copy)\
                                .then_inc(operand_high, 1)
                            op[0] += 1
                        split_high(b + 1, t)
                    b += 1
                    if i % 2 == 0 and i >= 2:
                        for q in range(4):
                            split_high(b + 1, q)
                        b += 1
                log_and_exp()
                closing_down(b, norm, ts)

            def log_and_exp():
                nc.scalar.preload_act_table_set("natural_log_exp_and_others")

            log_and_exp()
            for k in range(KD):
                finish_chunk(k, "attn0", (turn_read, k + 2), slice(0, T))
            for q in range(4):
                split_high(0, q)
            act.wait_ge(cst_in, 16)
            norm_rs(rs, T)

            def conv(first_slot):
                def silu(i, t):
                    slot = first_slot + 4 * i + t
                    if slot % 2 == 0 and slot >= 2:
                        c = slot // 2 - 1
                        act.wait_ge(M["conv_done"], c + 1)
                        act.activation(qkv[:, c], qkv[:, c], ACT.Silu).then_inc(M["silu_done"], 1)
                return silu

            stream("ab_qkvz", conv(0))
            stream("ab_qb", conv(16))
            stream("ab_kvb", conv(20))
            conv(24)(0, 0)
            log_and_exp()
            b = tile_at[phases["ab_qb"].first]
            head_norms([(qb[:, i], T, 1.0 / 64, T, (tile_read, b + i + 1)) for i in range(4)]
                       + [(kb, T, 1.0 / 64, T, (tile_read, b + 5))])
            act.wait_ge(hn_scaled, hn[0])
            for g in range(2):
                for half in range(2):
                    ins = act.activation(kdup[64 * half:64 * half + 64, g], kb[64 * g:64 * g + 64], ACT.Copy)
            ins.then_inc(M["kv_dup"], 1)
            act.wait_ge(misc_in, 16 * N_MISC_LOADS)
            attention([dict(nq=TILES[m][1] - TILES[m][0], nk=T, kind="window", head=h, rows=[16, P, P],
                            parts=slice(64 * (h % 2), 64 * (h % 2) + 64), chunks=slice(4 + h // 2, 5 + h // 2),
                            tokens=slice(*TILES[m])) for m, h in window_units()])
            act.wait_ge(M["silu_done"], 12)
            head_norms([(qkv[:, i], T, 1.0, T, (M["silu_done"], 12)) for i in range(8)])

            act.activation(neg_a, a_log, ACT.Exp)
            act.wait_ge(M["d_first"], 1)
            act.activation(beta, hab[:, :, 0:8], ACT.Exp, scale=-1.0)
            link(act.activation(d_tmp2, d_tmp, ACT.Abs))
            link(act.activation(d_tmp2, d_tmp2, ACT.Exp, scale=-1.0))
            act.activation(d_tmp2, d_tmp2, ACT.Ln, bias=ones[:, 0:1]).then_inc(M["d_gate_exp"], 1)
            for i, (m, source) in enumerate(delta_turns()):
                n = TILES[m][1] - TILES[m][0]
                act.wait_ge(M["d_turned"], i + 1)
                act.activation((v_tok if source == 8 else k_tok)[0:n, m], (b4, b5)[i % 2][0:n, 0:4 * P].rearrange(
                    "p (h d) -> p h d", h=4), ACT.Copy).then_inc(M["d_copied"], 1)
            act.wait_ge(M["d_cum_read"], 1)
            act.activation(necc[0:NMETA, 0], gcc[0:NMETA, 0], ACT.Exp)
            act.activation(necc[:, 1:3], gcc[:, 1:3], ACT.Exp).then_inc(M["d_gate_exp"], 1)
            for c, (s, e) in enumerate(TILES):
                n = e - s
                for d in range(2):
                    dh, both = slice(4 * d, 4 * d + 4), dm[d][0:n, 0:4 * n]
                    act.wait_ge(M["d_diff"], 2 * c + d + 1)
                    act.activation(decayed_queries(c, d), DELTA_BANKS[d][0][:, 0:4 * n], ACT.Exp).then_inc(M["d_egr"], 1)
                    act.activation(kdf[0:n, c, dh], d_tmp[0:n, c, dh], ACT.Exp)
                    act.activation(both, both, ACT.Exp).then_inc(M["d_dm"], 1)
                for level in range(1, n_levels(n)):
                    for d in range(2):
                        act.wait_ge(M["d_w"], step_at(c, level, d) + 1)
                        act.activation(wt[d][0:n, 0:4 * n], DELTA_BANKS[d][3][0:n, 0:4 * n], ACT.Copy)\
                            .then_inc(M["d_w_copied"], 1)
            act.wait_ge(tile_read, tile_at[phases["ab_qkvz"].first] + 16)
            act.activation(za, za, ACT.Silu).then_inc(M["silu_r"], 1)
            log_and_exp()

            def gated_norms(units, chunk_of):
                head_norms(units)
                for c in chunk_of:
                    gated[0] += 1
                    act.wait_ge(hn_gated, gated[0])
                    act.activation(a_hi[:, c, gts], hn_t[:, (gated[0] - 1) % 2, 0:gts.stop - gts.start], ACT.Copy)\
                        .then_inc(operand_high, 1)
                    op[0] += 1

            gated, gts = [0], slice(0, T)
            gated_norms([(o_delta[:, h], T, 1.0 / P, T, (M["d_o_read"], 6)) for h in range(4)], range(4))
            residual("ab_out", "mlp0", slice(0, T))
            norm_rs(rs, T)
            mlp_relu("mlp0", "attn1", slice(0, T))

            norm_rs(rs, T)
            stream("c_q", nothing)
            for k in range(KD):
                f = fin[0]
                fin[0] += 1
                act.wait_ge(turn_read, 11 + k)
                act.wait_ge(sum_added, f - 1)
                act.activation(squares[:, f % 2, 0:SEQ], memory[:, k], ACT.Square).then_inc(squared, 1)
            stream("c_kv", nothing)
            norm_rs(rs_mem, SEQ)
            b = tile_at[phases["c_q"].first]
            head_norms([(qc[:, i], SEQ, 1.0 / P, SEQ, (tile_read, b + i + 1)) for i in range(8)]
                       + [(kc[:, i], T, 1.0 / P, T, (tile_read, b + 9 + i)) for i in range(2)])
            attention([dict(nq=P, nk=T, kind=None, rows=[16, P, P], parts=slice(0, P), chunks=slice(h, h + 1),
                            tokens=slice(16 + m * P, 16 + (m + 1) * P)) for m in range(2) for h in range(8)])
            residual("c_out", "mlp1", REAL)
            norm_rs(rs[:, REAL], SEQ)
            mlp_relu("mlp1", "mix0", REAL)

            for layer in range(2):
                def memory_operand():
                    for k in range(KD):
                        act.activation(a_hi[:, k, 0:SEQ], memory[:, k], ACT.Copy, scale=gain(f"memkv{layer}", k))\
                            .then_inc(operand_high, 1)
                        op[0] += 1

                norm_rs(rs[:, REAL], SEQ)
                def memory_tiles(lo, hi):
                    for n in range(lo, hi):
                        split_high(phases[f"xkv{layer}"].first + n // 4 + 1, n % 4)

                if layer == 0:
                    first = tile_at[phases["ev_in"].first]

                    def gelu(i, t):
                        if i == 3:
                            act.wait_ge(tile_read, first + 4 * i + t + 1)
                            act.activation(gu[:, t], gu[:, t], ACT.Gelu).then_inc(M["gelu"], 1)
                        if i == 4:
                            act.wait_ge(tile_read, first + 4 * i + t + 1)
                            part = gv[:, t % 2, t // 2 * HALF:(t // 2 + 1) * HALF]
                            act.activation(part, part, ACT.Gelu).then_inc(M["gelu"], 1)

                    stream("ev_in", gelu, 0, 2)
                    memory_operand()
                    stream("ev_in", gelu, 2)
                    act.wait_ge(M["rope_angle"], 1)
                    act.activation(sin_m, angle[:, 0], ACT.Sin)
                    act.activation(cos_m, angle[:, 1], ACT.Sin).then_inc(M["rope_sin"], 1)
                    log_and_exp()
                    memory_tiles(0, 4)
                    head_norms([(x[:, i], SEQ, 1.0 / 64, SEQ, (tile_read, first + 4 * j + i + 1))
                                for j, x in enumerate((mq, mk)) for i in range(4)],
                               between=lambda i: memory_tiles(*ev_fill(i)))
                    attention([dict(nq=P, nk=(m + 1) * P, kind="causal", rows=[P] * (m + 1),
                                    parts=slice(64 * (h % 2), 64 * (h % 2) + 64), chunks=slice(h // 2, h // 2 + 1),
                                    tokens=slice(16 + m * P, 16 + (m + 1) * P)) for m in range(2) for h in range(8)])
                    act.wait_ge(M["g_stat"], 1)
                    act.wait_ge(M["ws_turned"], 2)
                    act.activation(gt, gv, ACT.Square).then_inc(M["g_sq"], 1)
                    act.wait_ge(M["g_stat"], 2)
                    link(act.activation(g_var, g_var, ACT.Ln, bias=eps, scale=1.0 / 64))
                    act.activation(g_var, g_var, ACT.Exp, scale=-0.5).then_inc(M["g_ln"], 1)
                    for c in range(2):
                        act.wait_ge(M["g_read"], c + 1)
                        act.activation(a_hi[:, 4:8, 16 + c * P:16 + (c + 1) * P], g_out(c), ACT.Copy)\
                            .then_inc(operand_high, 1)
                        op[0] += 1
                else:
                    first = tile_at[phases["od_in"].first]
                    stream("od_in", nothing, 0, 2)
                    memory_operand()
                    stream("od_in", nothing, 2)
                    act.wait_ge(tile_read, first + 24)
                    act.activation(lr, lr, ACT.Silu).then_inc(M["silu_r"], 1)
                    log_and_exp()
                    memory_tiles(0, 2)
                    for h in range(4):
                        act.wait_ge(M["l_gate"], h + 1)
                        link(act.activation(l_tmp[:, h], la[:, h], ACT.Abs))
                        link(act.activation(l_tmp[:, h], l_tmp[:, h], ACT.Exp, scale=-1.0))
                        act.activation(l_tmp[:, h], l_tmp[:, h], ACT.Ln, bias=ones[:, 0:1]).then_inc(M["l_exp"], 1)
                    memory_tiles(2, 4)
                    act.wait_ge(M["l_scan"], 1)
                    act.activation(l_tmp, la, ACT.Exp).then_inc(M["l_exp"], 1)
                    memory_tiles(4, 5)
                    for h in range(4):
                        for c in range(4):
                            cs = slice(64 * c, 64 * c + 64)
                            ins = act.activation(ks_t[:, h, cs], la[:, h, cs], ACT.Exp, scale=-1.0,
                                                 bias=la[:, h, 64 * c + 63:64 * c + 64])
                    ins.then_inc(M["l_exp"], 1)
                    act.activation(l_dec, la.rearrange("p h (c t) -> p h c t", t=64)[:, :, :, 63], ACT.Exp)
                    act.activation(lo_t[:, 4:8], la, ACT.Exp, scale=-1.0).then_inc(M["l_exp"], 1)
                    memory_tiles(5, 8)
                    for m in range(2):
                        act.wait_ge(M["l_kst"], m + 1)
                        act.activation(kst[:, m], (b4, b5)[m][:, 0:4 * P].rearrange("p (h d) -> p h d", h=4), ACT.Copy)\
                            .then_inc(M["l_kstc"], 1)
                    memory_tiles(8, 16)
                    gts = REAL
                    gated_norms([(lo_t[:, 2 * h:2 * h + 2].rearrange("p a t -> p (a t)"), 2 * SEQ, 1.0 / 256, SEQ,
                                  (M["l_oc"], 4)) for h in range(4)], range(8))
                residual(f"mix_out{layer}", f"memq{layer}", REAL)
                norm_rs(rs[:, REAL], SEQ)
                stream(f"xq{layer}", nothing, 0, 1)
                for x, name, fill in ((xk, "xkv", True), (xq, "xq", False)):
                    first, after = tile_at[phases[f"{name}{layer}"].first], phases[f"xq{layer}"].first + 2
                    head_norms([(x[:, 2 * h:2 * h + 2].rearrange("p a t -> p (a t)"), 2 * SEQ, 1.0 / 256, SEQ,
                                 (tile_read, first + 2 * h + 2)) for h in range(4)],
                               between=(lambda t: split_high(after, t)) if fill else None)
                attention([dict(nq=P, nk=SEQ, kind=None, rows=[P, P], parts=slice(0, P), chunks=slice(2 * h, 2 * h + 2),
                                tokens=slice(16 + m * P, 16 + (m + 1) * P)) for m in range(2) for h in range(4)])
                residual(f"x_out{layer}", f"ffn{layer}", REAL)
                norm_rs(rs[:, REAL], SEQ)
                mlp_swiglu(f"swiglu{layer}", "mix1" if layer == 0 else None, REAL)

        @block.vector
        def _(dve):
            op, fin, step = [0], [0], [0]

            def link(ins):
                step[0] += 1
                ins.then_inc(dve_step, 1)
                dve.wait_ge(dve_step, step[0])

            def split_low(b, q, g=None):
                b, q = (b, q) if q >= 0 else (b - 1, 3)
                if b >= n_blocks:
                    return
                dve.wait_ge(high_split, looped(4 * b + q + 1, 4 * LOOP_BLOCKS, g))
                dve.tensor_tensor(quarter(w_lo, b, q), raw_quarter(b, q), quarter(w_hi, b, q).bitcast(F32), ALU.subtract)\
                    .then_inc(low_split, 1)

            def stream(name, evac, start=0, n=None):
                ph = phases[name]
                for i in range(start, ph.n if n is None else start + n):
                    b = ph.first + i
                    for t in range(4):
                        evac(i, t, tile_at[b] + t)
                        split_low(b + 1, t - 1)

            def low_part(target, source, high):
                op[0] += 1
                dve.wait_ge(operand_high, op[0])
                dve.tensor_tensor(target, source, high.bitcast(F32), ALU.subtract).then_inc(operand_split, 1)

            def finish_low(k, norm, ts, source=None):
                op[0] += 1
                dve.wait_ge(operand_high, op[0])
                dve.scalar_tensor_tensor(u_lo[:, k, ts], hidden[:, k, ts], gain(norm, k),
                                         u_hi[:, k, ts].bitcast(F32), ALU.mult, ALU.subtract).then_inc(operand_split, 1)

            norms, turns = [0], [0]

            def rms_ready():
                norms[0] += 1
                dve.wait_ge(rs_ready, norms[0])

            def turn_rs(target, n):
                turns[0] += 1
                dve.wait_ge(rs_turned, turns[0])
                dve.tensor_copy(target, b6[:, 0:n * P].rearrange("p (m c) -> p m c", c=P)[:, :, 0]).then_inc(rs_tok_ready, 1)
                dve.wait_ge(rs_tok_ready, turns[0])

            def scaled(target, t, gt, ts, scale=None):
                dve.wait_ge(tile_summed, gt + 1)
                n = ts.stop - ts.start
                dve.tensor_tensor(target, tile_bank[t][:, 0:n], rs[:, ts] if scale is None else scale, ALU.mult)\
                    .then_inc(tile_read, 1)

            def scaled_tokens(target, t, gt, column):
                dve.wait_ge(tile_summed, gt + 1)
                dve.tensor_scalar(target, tile_bank[t][:, 0:HALF], column, None, ALU.mult).then_inc(tile_read, 1)

            def add_tile(k, t, gt, ts, first=False):
                dve.wait_ge(tile_summed, gt + 1)
                dve.wait_ge(tile_read, gt)
                dve.tensor_tensor(hidden[:, k, ts], tile_bank[t][:, 0:ts.stop - ts.start], hidden[:, k, ts], ALU.add)\
                    .then_inc(tile_read, 1)

            hn, ropes, gated = [0], [0], [0]

            def head_norms(units, rope=None, gate=None, ts=slice(0, T), between=None):
                base, r0, n = hn[0], ropes[0], len(units)
                chunk = [0]

                def scale(i):
                    sources, gains_, targets = units[i]
                    v = base + i
                    dve.wait_ge(hn_rs, v + 1)
                    if rope is not None and r0 + i >= 2:
                        dve.wait_ge(hn_swapped, r0 + i - 1)
                    for source, g, target in zip(sources, gains_, targets):
                        w_ = source.shape[1]
                        if rope is not None:
                            target = hn_n[:, (r0 + i) % 2, 0:w_]
                        ins = dve.scalar_tensor_tensor(target, source, g, hn_r[:, v % 2, 0:w_], ALU.mult, ALU.mult)
                    ins.then_inc(hn_scaled, 1)

                def rotate(i):
                    r, target = r0 + i, units[i][2][0]
                    w_ = target.shape[1]
                    cos, sin = rope[i]
                    dve.wait_ge(hn_scaled, base + i + 1)
                    dve.tensor_tensor(target, hn_n[:, r % 2, 0:w_], cos, ALU.mult)
                    dve.wait_ge(hn_swapped, r + 1)
                    link(dve.tensor_tensor(hn_t[:, r % 2, 0:w_], (b6, b7)[r % 2][:, 0:w_], sin, ALU.mult))
                    dve.tensor_tensor(target, target, hn_t[:, r % 2, 0:w_], ALU.add).then_inc(hn_roped, 1)

                def gates(i):
                    dve.wait_ge(hn_scaled, base + i + 1)
                    for target in units[i][2]:
                        c = gated[0]
                        if chunk[0] >= 2:
                            dve.wait_ge(operand_split, op[0])
                        w_ = target.shape[1]
                        dve.tensor_tensor(hn_t[:, c % 2, 0:w_], target, gate[chunk[0]], ALU.mult).then_inc(hn_gated, 1)
                        gated[0] += 1
                        chunk[0] += 1
                        if chunk[0] >= 2:
                            low(chunk[0] - 2, c - 1)

                def low(k, c):
                    low_part(a_lo[:, k, ts], hn_t[:, c % 2, 0:ts.stop - ts.start], a_hi[:, k, ts])

                for i in range(n):
                    scale(i)
                    if rope is not None and i >= 1:
                        rotate(i - 1)
                    if between is not None:
                        between(i)
                if rope is not None:
                    rotate(n - 1)
                    ropes[0] += n
                if gate is not None:
                    for i in range(n):
                        gates(i)
                    low(chunk[0] - 1, gated[0] - 1)
                hn[0] += n

            at = [0]

            def attention(units):
                base, n = at[0], len(units)

                def maximum(i):
                    x, v = units[i], base + i
                    q, s, nk = slice(0, x["nq"]), v % 2, x["nk"]
                    dve.wait_ge(at_scored, v + 1)
                    logits = (b4, b5)[s][q, 0:nk]
                    if x["kind"]:
                        if v >= 2:
                            dve.wait_ge(at_exp, v - 1)
                        if x["kind"] == "window":
                            ins = dve.scalar_tensor_tensor(at_s[q, s, 0:nk], x["bias"][q], x["slope"], logits,
                                                           ALU.mult, ALU.add)
                        else:
                            ins = dve.tensor_tensor(at_s[q, s, 0:nk], logits, x["bias"], ALU.add)
                        link(ins)
                        logits = at_s[q, s, 0:nk]
                    if x["kind"] == "window":
                        link(dve.tensor_reduce(at_m[q, s], logits, AX.X, ALU.max))
                        dve.tensor_scalar(at_nm[q, s], at_m[q, s], sink[q, x["head"]:x["head"] + 1], -1.0, ALU.max,
                                          ALU.mult).then_inc(at_max, 1)
                    else:
                        dve.tensor_reduce(at_nm[q, s], logits, AX.X, ALU.max, negate=True).then_inc(at_max, 1)

                def normalise(i):
                    x, v = units[i], base + i
                    q, s = slice(0, x["nq"]), v % 2
                    dve.wait_ge(at_exp, v + 1)
                    if x["kind"] == "window":
                        link(dve.tensor_tensor(at_den[q, s], at_den[q, s], at_es[q, s], ALU.add))
                    link(dve.reciprocal(at_inv[q, s], at_den[q, s]))
                    probs = at_p[q, v % 3, 0:x["nk"]]
                    dve.tensor_scalar(probs, probs, at_inv[q, s], None, ALU.mult)\
                        .then_inc(at_prob, 1)

                def result(i):
                    x = units[i]
                    low_part(attention_out(a_lo, x), attention_bank(x, base + i), attention_out(a_hi, x))

                for k in range(n + 6):
                    if k < n:
                        maximum(k)
                    if 0 <= k - 1 < n:
                        normalise(k - 1)
                    if k >= 6:
                        result(k - 6)
                at[0] += n

            def residual(name, norm, ts):
                def evac(i, t, gt):
                    add_tile(4 * i + t, t, gt, ts)
                    if 4 * i + t >= 1:
                        finish_low(4 * i + t - 1, norm, ts)
                stream(name, evac)
                finish_low(KD - 1, norm, ts)

            ff = [0]

            def mlp_relu(name, norm, ts):
                first, base, f0 = phases[name].first, op[0], ff[0]

                def low(unit, t, g):
                    k = 4 * (unit % 2) + t
                    dve.wait_ge(operand_high, looped(base + 4 * unit + t + 1, 4 * LOOP_UNITS, g))
                    dve.tensor_tensor(a_lo[:, k, ts], ff_a[:, t % 2, ts], a_hi[:, k, ts].bitcast(F32), ALU.subtract)\
                        .then_inc(operand_split, 1)

                def up(b, unit, g=None):
                    for t in range(4):
                        gt, f = looped(tile_at[b] + t, LOOP_TILES, g), f0 + 4 * unit + t
                        if f >= 2:
                            dve.wait_ge(ff_ready, looped(f - 1, 4 * LOOP_UNITS, g))
                        scaled(ff_z[:, t % 2, ts], t, gt, ts)
                        if t >= 2:
                            low(unit, t - 2, g)
                        dve.wait_ge(operand_split, looped(base + 4 * unit + t - 1, 4 * LOOP_UNITS, g))
                        dve.wait_ge(tile_read, gt + 1)
                        dve.scalar_tensor_tensor(ff_a[:, t % 2, ts], ff_z[:, t % 2, ts], 0.0, ff_z[:, t % 2, ts],
                                                 ALU.max, ALU.mult).then_inc(ff_ready, 1)
                        split_low(b + 1, t - 1, g)
                    low(unit, 2, g)
                    low(unit, 3, g)

                up(first, 0)
                with dve.Fori(0, (N_UNITS - 2) // LOOP_UNITS) as g:
                    up(first + 1, 1, g)
                    down(first + 2, ts, g=g)
                    up(first + 3, 2, g)
                    down(first + 4, ts, g=g)
                last = first + phases[name].n - 3
                up(last, N_UNITS - 1)
                op[0] += D_FF // P
                ff[0] += D_FF // P
                down(last + 1, ts)
                down(last + 2, ts, norm)

            def down(b, ts, norm=None, g=None):
                for k in range(KD):
                    add_tile(k, k % 4, looped(tile_at[b] + k, LOOP_TILES, g), ts)
                    if norm is not None and k >= 1:
                        finish_low(k - 1, norm, ts)
                    if k % 2 == 1:
                        split_low(b + 1, k // 2 - 1, g)
                if norm is not None:
                    finish_low(KD - 1, norm, ts)

            ff_relu = 2 * D_FF // P

            def mlp_swiglu(name, norm, ts):
                b, n = phases[name].first, ts.stop - ts.start
                for i in range(D_FF2 // HALF):
                    for t in range(4):
                        gt = tile_at[b] + t
                        if t < 2:
                            dve.wait_ge(ff_ready, ff[0])
                        else:
                            dve.wait_ge(silu_ready, ff[0] - ff_relu + 1)
                        scaled(ff_z[:, t % 2, 0:n], t, gt, ts)
                        if t >= 2:
                            ff[0] += 1
                            dve.wait_ge(operand_split, op[0])
                            dve.wait_ge(tile_read, gt + 1)
                            dve.tensor_tensor(ff_a[:, t - 2, 0:n], ff_z[:, t - 2, 0:n], ff_s[:, t - 2, 0:n], ALU.mult)\
                                .then_inc(ff_ready, 1)
                        split_low(b + 1, t - 1)
                    for t in range(2):
                        k = 2 * (i % 4) + t
                        low_part(a_lo[:, k, ts], ff_a[:, t, 0:n], a_hi[:, k, ts])
                    b += 1
                    if i % 2 == 0 and i >= 2:
                        down(b, ts)
                        b += 1
                down(b, ts, norm)

            dve.wait_ge(turned, 1)
            dve.tensor_copy(gains[:], tile_bank[0][:, 0:96]).then_inc(turn_read, 1)
            for k in range(KD):
                dve.wait_ge(turned, k + 2)
                dve.tensor_copy(hidden[:, k], tile_bank[(k + 1) % 4][:, 0:T]).then_inc(turn_read, 1)
                if k >= 1:
                    finish_low(k - 1, "attn0", slice(0, T))
            finish_low(KD - 1, "attn0", slice(0, T))
            for q in range(3):
                split_low(0, q)
            dve.wait_ge(turned, KD + 2)
            link(dve.tensor_copy(late[:], b4[:, 0:N_LATE_ROWS]))
            dve.tensor_scalar(col("b_q"), col("b_q"), 64.0 ** -0.5, None, ALU.mult)
            dve.tensor_scalar(col("c_q"), col("c_q"), 128.0 ** -0.5, None, ALU.mult)
            dve.tensor_scalar(col("ev_q"), col("ev_q"), 64.0 ** -0.5, None, ALU.mult)
            dve.tensor_scalar(late[:, LATE_ROWS["xa_q"]:LATE_ROWS["xa_q"] + 4],
                              late[:, LATE_ROWS["xa_q"]:LATE_ROWS["xa_q"] + 4], 256.0 ** -0.5, None,
                              ALU.mult).then_inc(turn_read, 1)

            full = slice(0, T)
            dve.memset(xa[:, :, 0:2], 0.0)
            dve.memset(hab, 0.0)
            link(dve.memset(xa[:, :, PAD - 2:PAD], 0.0))
            rms_ready()

            def conv_after(slot):
                if slot % 2 == 0:
                    return
                c = slot // 2
                dve.wait_ge(tile_read, tile_at[phases["ab_qkvz"].first] + c + 1)
                link(dve.tensor_scalar(qkv[:, c], xa[:, c, 0:T], col("conv", c), None, ALU.mult))
                for j in range(1, 5):
                    ins = dve.scalar_tensor_tensor(qkv[:, c], xa[:, c, j:j + T], col("conv", 12 * j + c), qkv[:, c],
                                                   ALU.mult, ALU.add)
                    if j < 4:
                        link(ins)
                ins.then_inc(M["conv_done"], 1)

            def project_ab(i, t, gt):
                c = 4 * i + t
                scaled(za[:, c - 12] if c >= 12 else xa[:, c, 2:2 + T], t, gt, full)
                conv_after(c)

            def project_qb(i, t, gt):
                scaled(qb[:, t], t, gt, full)
                conv_after(16 + t)

            def project_kvb(i, t, gt):
                if t < 2:
                    scaled((kb, hn_t[:, 0])[t], t, gt, full)
                if t == 2:
                    dve.wait_ge(tile_summed, gt + 1)
                    dve.tensor_tensor(hn_t[0:16, 1], tile_bank[2][0:16, 0:T], rs[0:16], ALU.mult).then_inc(tile_read, 2)
                conv_after(20 + t)

            stream("ab_qkvz", project_ab)
            stream("ab_qb", project_qb)
            stream("ab_kvb", project_kvb)
            dve.wait_ge(M["ab_turned"], 1)
            dve.tensor_copy(vb[0:NMETA, 0], b6[0:NMETA, 0:P])
            dve.tensor_copy(vb[:, 1:3], b6[:, P:3 * P].rearrange("p (m d) -> p m d", m=2))
            dve.tensor_copy(hab[0:NMETA, 0], b7[0:NMETA, 0:16])
            dve.tensor_copy(hab[:, 1:3], b7[:, 16:48].rearrange("p (m d) -> p m d", m=2)).then_inc(M["ab_turn_read"], 1)
            dve.wait_ge(M["ab_turn_read"], 1)
            head_norms([([qb[:, i]], [col("b_q")], [qb[:, i]]) for i in range(4)] + [([kb], [col("b_k")], [kb])])
            dve.wait_ge(misc_in, 16 * N_MISC_LOADS)
            attention([dict(nq=TILES[m][1] - TILES[m][0], nk=T, kind="window", head=h, bias=early_table(f"ndist{m}"),
                            slope=2.0 ** (-(h + 1)), parts=slice(64 * (h % 2), 64 * (h % 2) + 64),
                            chunks=slice(4 + h // 2, 5 + h // 2), tokens=slice(*TILES[m])) for m, h in window_units()])
            head_norms([([qkv[:, i]], [P ** -0.5 if i < 4 else 1.0], [qkv[:, i]]) for i in range(8)])

            dve.tensor_tensor(d_tmp, hab[:, :, 8:16], dt_bias.unsqueeze(1).to_broadcast([P, 3, 8]), ALU.add)\
                .then_inc(M["d_first"], 1)
            dve.wait_ge(M["d_gate_exp"], 1)
            link(dve.tensor_scalar(beta, beta, 1.0, None, ALU.add))
            dve.reciprocal(beta, beta)
            dve.wait_ge(M["d_first"], 1)
            link(dve.scalar_tensor_tensor(d_tmp2, d_tmp, 0.0, d_tmp2, ALU.max, ALU.add))
            link(dve.tensor_scalar(d_tmp2, d_tmp2, -1.0, None, ALU.mult))
            dve.tensor_tensor(decay, d_tmp2, neg_a.unsqueeze(1).to_broadcast([P, 3, 8]), ALU.mult)\
                .then_inc(M["d_gates"], 1)
            dve.wait_ge(M["d_cum"], 1)
            dve.tensor_copy(gcc[0:NMETA, 0], b6[0:NMETA, 0:8])
            dve.tensor_copy(gcc[:, 1:3], b6[:, 8:24].rearrange("p (c h) -> p c h", c=2)).then_inc(M["d_cum_read"], 1)
            dve.wait_ge(M["d_cum_read"], 1)

            def by_head(ap):
                return ap.rearrange("p (h i) -> p h i", h=4)

            for c, (s, e) in enumerate(TILES):
                n = e - s
                for d in range(2):
                    dh = slice(4 * d, 4 * d + 4)
                    dmn, gc = by_head(dm[d][0:n, 0:4 * n]), gcc[0:n, c, dh]
                    dve.wait_ge(M["d_rows"], 2 * c + d + 1)
                    rows = by_head(DELTA_BANKS[d][0][:, 0:4 * n])
                    dve.tensor_tensor(d_tmp[0:n, c, dh], rows[0:n, :, (n - 1) * (1 - d)], gc, ALU.subtract)
                    link(dve.tensor_tensor(dmn, rows[0:n], gc.unsqueeze(2).to_broadcast([n, 4, n]), ALU.subtract))
                    neg = table(("neg_f", "neg_b")[d])[0:n, 0:n].unsqueeze(1).to_broadcast([n, 4, n])
                    dve.tensor_tensor(dmn, dmn, neg, ALU.add).then_inc(M["d_diff"], 1)
                for d in range(2):
                    j, dh = 2 * c + d, slice(4 * d, 4 * d + 4)
                    _, kk, kq, _ = DELTA_BANKS[d]
                    dmn, nnn, qd = by_head(dm[d][0:n, 0:4 * n]), by_head(nn[d][0:n, 0:4 * n]), by_head(decayed_queries(c, d))
                    dve.wait_ge(M["d_egr"], j + 1)
                    link(dve.tensor_copy(egl[:, c, dh], qd[:, :, (n - 1) * (1 - d)]))
                    dve.tensor_tensor(qd, qd, qkv[:, 0:4, s:e], ALU.mult)
                    dve.wait_ge(M["d_gk"], j + 1)
                    link(dve.tensor_tensor(nnn, by_head(kk[0:n, 0:4 * n]),
                                           beta[0:n, c, dh].unsqueeze(2).to_broadcast([n, 4, n]), ALU.mult))
                    dve.wait_ge(M["d_dm"], j + 1)
                    dve.tensor_tensor(nnn, nnn, dmn, ALU.mult)
                    dve.tensor_tensor(by_head(inner_product(j)[0:n]), by_head(kq[0:n, 0:4 * n]), dmn, ALU.mult)\
                        .then_inc(M["d_n"], 1)
                eye = ident[0:n, 0:n].unsqueeze(1).to_broadcast([n, 4, n])
                for level in range(n_levels(n)):
                    for d in range(2):
                        i, x, xtd = level_at(c, level, d), inverse(2 * c + d), xt[d][0:n, 0:4 * n]
                        _, xnx, xnx_t, _ = DELTA_BANKS[d]
                        dve.wait_ge(M["d_y"], i + 1)
                        if level == 0:
                            dve.wait_ge(M["d_nb"], i + 1)
                            dve.tensor_tensor(by_head(x[0:n]), eye, by_head(nb_[d][0:n, 0:4 * n]), ALU.subtract)
                            dve.tensor_tensor(by_head(xtd), eye, by_head(xnx[0:n, 0:4 * n]), ALU.subtract)\
                                .then_inc(M["d_x"], 1)
                            continue
                        dve.wait_ge(M["d_x"], i - 1)
                        if level < n_levels(n) - 1:
                            dve.tensor_tensor(xtd, xtd, xnx_t[0:n, 0:4 * n], ALU.subtract)
                        dve.tensor_tensor(x[0:n], x[0:n], xnx[0:n, 0:4 * n], ALU.subtract).then_inc(M["d_x"], 1)
            dve.wait_ge(M["d_gate_exp"], 2)
            dve.wait_ge(M["d_copied"], 6)
            seen = set()
            for i, pair in enumerate(SCAN):
                before = [2 * (i - 1) + d + 1 for d in range(2)]
                for d, c in pair:
                    n, dh = TILES[c][1] - TILES[c][0], slice(4 * d, 4 * d + 4)
                    r, kd = by_head(scan_r[d][0:n]), by_head(scan_k[d][0:n])
                    if i == 0:
                        dve.tensor_copy(r, v_tok[0:n, c]).then_inc(M["d_r"], 1)
                    else:
                        dve.wait_ge(M["d_v"], before[d])
                        dve.wait_ge(M["d_ks"], before[d])
                        link(dve.tensor_tensor(r, by_head(DELTA_BANKS[d][0][0:n]),
                                               necc[0:n, c, dh].unsqueeze(2).to_broadcast([n, 4, P]), ALU.mult))
                        dve.tensor_tensor(r, v_tok[0:n, c], r, ALU.subtract).then_inc(M["d_r"], 1)
                    if i < 2:
                        if i >= 1:
                            dve.wait_ge(M["d_s"], before[d])
                        dve.tensor_tensor(kd, k_tok[0:n, c], kdf[0:n, c, dh].unsqueeze(2).to_broadcast([n, 4, P]),
                                          ALU.mult).then_inc(M["d_kdec"], 1)
                for d, c in pair:
                    n, dh = TILES[c][1] - TILES[c][0], slice(4 * d, 4 * d + 4)
                    dve.wait_ge(M["d_v"], 2 * i + d + 1)
                    if i >= 1:
                        dve.wait_ge(M["d_o"], before[d])
                    dve.tensor_tensor(by_head(scan_v[d][0:n]), by_head(DELTA_BANKS[d][1][0:n]),
                                      beta[0:n, c, dh].unsqueeze(2).to_broadcast([n, 4, P]), ALU.mult).then_inc(M["d_vnew"], 1)
                for d, c in pair:
                    (s, e), dh = TILES[c], slice(4 * d, 4 * d + 4)
                    _, _, out_bank, state_bank = DELTA_BANKS[d]
                    dve.wait_ge(M["d_o"], 2 * i + d + 1)
                    o = by_head(out_bank[:, 0:4 * (e - s)])
                    if c in seen:
                        dve.wait_ge(M["d_o_read"], 2 * i + d)
                        dve.tensor_tensor(o_delta[:, :, s:e], o, o_delta[:, :, s:e], ALU.add).then_inc(M["d_o_read"], 1)
                    else:
                        dve.tensor_copy(o_delta[:, :, s:e], o).then_inc(M["d_o_read"], 1)
                    seen.add(c)
                    if i < 2:
                        dve.wait_ge(M["d_s"], 2 * i + d + 1)
                        if i == 0:
                            dve.tensor_copy(state[:, d], by_head(state_bank[:])).then_inc(M["d_s_read"], 1)
                        else:
                            dve.wait_ge(M["d_s_read"], before[d])
                            link(dve.tensor_tensor(state[:, d], state[:, d],
                                                   egl[:, c, dh].unsqueeze(2).to_broadcast([P, 4, P]), ALU.mult))
                            dve.tensor_tensor(state[:, d], state[:, d], by_head(state_bank[:]), ALU.add)\
                                .then_inc(M["d_s_read"], 1)
            dve.wait_ge(M["silu_r"], 1)
            head_norms([([o_delta[:, h]], [col("a_out")], [o_delta[:, h]]) for h in range(4)],
                       gate=[za[:, h] for h in range(4)], ts=full)
            residual("ab_out", "mlp0", full)
            rms_ready()
            mlp_relu("mlp0", "attn1", full)

            def closing(first_turn):
                for i in range(4):
                    dve.wait_ge(turned, first_turn + i + 1)
                    dve.tensor_copy(out_rows[:, i // 2, i % 2 * BLOCK:(i % 2 + 1) * BLOCK],
                                    tile_bank[(first_turn + i) % 4][:]).then_inc(turn_read, 1)


            rms_ready()

            def project_c(i, t, gt):
                scaled(qc[:, 4 * i + t], t, gt, REAL)
                if i == 1 and t == 0:
                    turn_rs(rs_tok, 3)

            stream("c_q", project_c)
            for k in range(KD):
                dve.wait_ge(turned, 11 + k)
                dve.tensor_copy(memory[:, k], (b4, b5)[(10 + k) % 2][:, 0:SEQ]).then_inc(turn_read, 1)

            def project_ckv(i, t, gt):
                if t < 2:
                    scaled(kc[:, t], t, gt, full)
                    return
                dve.wait_ge(tile_summed, gt + 1)
                if t == 2:
                    dve.tensor_tensor(vc[:, 1:3], tile_bank[2][:].rearrange("p (m d) -> p m d", m=2),
                                      rs_tok[:, 1:3].unsqueeze(2).to_broadcast([P, 2, HALF]), ALU.mult).then_inc(tile_read, 1)
                else:
                    dve.tensor_scalar(vc[:, 0], tile_bank[3][:, 0:HALF], rs_tok[:, 0:1], None, ALU.mult)\
                        .then_inc(tile_read, 1)

            stream("c_kv", project_ckv)
            rms_ready()
            turn_rs(rs_mem_tok, 2)
            cos, sin = table("cos_c"), table("sin_c")
            head_norms([([qc[:, i]], [col("c_q")], [qc[:, i]]) for i in range(8)]
                       + [([kc[:, i]], [col("c_k")], [kc[:, i]]) for i in range(2)],
                       rope=[(cos[:, REAL], sin[:, REAL])] * 8 + [(cos, sin)] * 2)
            attention([dict(nq=P, nk=T, kind=None, parts=slice(0, P), chunks=slice(h, h + 1),
                            tokens=slice(16 + m * P, 16 + (m + 1) * P)) for m in range(2) for h in range(8)])
            residual("c_out", "mlp1", REAL)
            rms_ready()
            mlp_relu("mlp1", "mix0", REAL)

            for layer in range(2):
                rms_ready()

                def memory_low():
                    for k in range(KD):
                        op[0] += 1
                        dve.wait_ge(operand_high, op[0])
                        dve.scalar_tensor_tensor(a_lo[:, k, 0:SEQ], memory[:, k], gain(f"memkv{layer}", k),
                                                 a_hi[:, k, 0:SEQ].bitcast(F32), ALU.mult, ALU.subtract)\
                            .then_inc(operand_split, 1)

                def project_memory(i, t, gt):
                    if i < 2:
                        scaled(xk[:, 4 * i + t], t, gt, slice(0, SEQ), rs_mem)
                    else:
                        at_ = (i - 2) * BLOCK + t // 2 * HALF
                        scaled_tokens(xv[:, t % 2, at_:at_ + HALF], t, gt, rs_mem_tok[:, t % 2:t % 2 + 1])

                def memory_tiles(lo, hi):
                    for n in range(lo, hi):
                        i, t = n // 4, n % 4
                        b = phases[f"xkv{layer}"].first + i
                        project_memory(i, t, tile_at[b] + t)
                        split_low(b + 1, t - 1)

                if layer == 0:
                    def project_ev(i, t, gt):
                        if i == 1 and t == 0:
                            turn_rs(rs_tok[:, 0:2], 2)
                        if i in (2, 4):
                            part = (mv, gv)[i // 4][:, t % 2, t // 2 * HALF:(t // 2 + 1) * HALF]
                            scaled_tokens(part, t, gt, rs_tok[:, t % 2:t % 2 + 1])
                        else:
                            scaled((mq, mk, None, gu)[i][:, t], t, gt, REAL)

                    stream("ev_in", project_ev, 0, 2)
                    memory_low()
                    stream("ev_in", project_ev, 2)
                    dve.wait_ge(late_in, 16 * N_LATE_LOADS)
                    ang, tmp, cosa = angle[:, 0], angle[:, 2], angle[:, 1]
                    link(dve.tensor_copy(tmp, pos_i.bitcast(I32)))
                    link(dve.tensor_scalar(ang, tmp, table("inv_freq"), None, ALU.mult))
                    link(dve.tensor_scalar(tmp, ang, 1.0 / (2.0 * PI), ROUND, ALU.mult, ALU.add))
                    link(dve.tensor_scalar(tmp, tmp, -ROUND, None, ALU.add))
                    for part in TWO_PI_PARTS:
                        link(dve.scalar_tensor_tensor(ang, tmp, -part, ang, ALU.mult, ALU.add))
                    link(dve.tensor_scalar(cosa, ang, PI / 2, None, ALU.add))
                    link(dve.tensor_scalar(tmp, cosa, PI, -2.0 * PI, ALU.is_gt, ALU.mult))
                    link(dve.tensor_tensor(cosa, cosa, tmp, ALU.add))
                    link(dve.tensor_scalar(ang, ang, PI_BELOW, -PI_BELOW, ALU.min, ALU.max))
                    dve.tensor_scalar(cosa, cosa, PI_BELOW, -PI_BELOW, ALU.min, ALU.max).then_inc(M["rope_angle"], 1)
                    memory_tiles(0, 4)
                    dve.wait_ge(M["rope_sin"], 1)
                    head_norms([([x[:, i]], [col(g)], [x[:, i]]) for x, g in ((mq, "ev_q"), (mk, "ev_k")) for i in range(4)],
                               rope=[(cos_m, sin_m)] * 8, between=lambda i: memory_tiles(*ev_fill(i)))
                    zeros_at = C["zeros"][0]
                    causal = cst[:, zeros_at:zeros_at + 2 * P]
                    attention([dict(nq=P, nk=(m + 1) * P, kind="causal", bias=causal[:, (1 - m) * P:2 * P],
                                    parts=slice(64 * (h % 2), 64 * (h % 2) + 64), chunks=slice(h // 2, h // 2 + 1),
                                    tokens=slice(16 + m * P, 16 + (m + 1) * P)) for m in range(2) for h in range(8)])
                    for i in range(2):
                        dve.wait_ge(M["ws_turned"], i + 1)
                        dve.tensor_tensor(ws_t[:, 4 * i:4 * i + 4], (b4, b5)[i][:].rearrange("p (g i) -> p g i", g=4),
                                          table("tri_f").unsqueeze(1).to_broadcast([P, 4, P]), ALU.mult)\
                            .then_inc(M["ws_read"], 1)
                    dve.wait_ge(M["gelu"], 8)
                    groups = gv.rearrange("p m (g d) -> p (m g) d", d=64)
                    wide = [P, 16, 64]
                    link(dve.tensor_reduce(g_mu, groups, AX.X, ALU.add))
                    link(dve.tensor_scalar(g_mu, g_mu, 1.0 / 64, None, ALU.mult))
                    dve.tensor_tensor(groups, groups, g_mu.unsqueeze(2).to_broadcast(wide), ALU.subtract)\
                        .then_inc(M["g_stat"], 1)
                    dve.wait_ge(M["g_sq"], 1)
                    dve.tensor_reduce(g_var, gt.rearrange("p m (g d) -> p (m g) d", d=64), AX.X, ALU.add)\
                        .then_inc(M["g_stat"], 1)
                    dve.wait_ge(M["g_ln"], 1)
                    link(dve.tensor_tensor(groups, groups, g_var.unsqueeze(2).to_broadcast(wide), ALU.mult))
                    link(dve.tensor_tensor(gv, gv, ln_g.unsqueeze(1).to_broadcast([P, 2, BLOCK]), ALU.mult))
                    dve.tensor_tensor(gv, gv, ln_b.unsqueeze(1).to_broadcast([P, 2, BLOCK]), ALU.add).then_inc(M["g_n"], 1)
                    for c in range(2):
                        dve.wait_ge(M["g_mixed"], c + 1)
                        link(dve.tensor_tensor(g_out(c), (b4, b5)[c][:].rearrange("p (g i) -> p g i", g=4), b_s, ALU.add))
                        dve.tensor_tensor(g_out(c), g_out(c), gu[:, :, c * P:(c + 1) * P], ALU.mult).then_inc(M["g_read"], 1)
                    for c in range(2):
                        ts = slice(16 + c * P, 16 + (c + 1) * P)
                        dve.wait_ge(M["g_read"], c + 1)
                        low_part(a_lo[:, 4:8, ts], g_out(c), a_hi[:, 4:8, ts])
                else:
                    def project_od(i, t, gt):
                        if i == 1 and t == 0:
                            turn_rs(rs_tok[:, 0:2], 2)
                        if i in (2, 3):
                            at_ = (i - 2) * BLOCK + t // 2 * HALF
                            scaled_tokens(lv[:, t % 2, at_:at_ + HALF], t, gt, rs_tok[:, t % 2:t % 2 + 1])
                        elif i < 2:
                            scaled((lq, lk)[i][:, t], t, gt, REAL)
                        else:
                            scaled(lr[:, 4 * (i - 4) + t], t, gt, REAL)

                    stream("od_in", project_od, 0, 2)
                    memory_low()
                    stream("od_in", project_od, 2)
                    dve.wait_ge(M["l_low"], 1)
                    dve.tensor_tensor(squares[0:16, 0, 0:SEQ], b4[0:16, 0:SEQ], rs[0:16, REAL], ALU.mult)\
                        .then_inc(M["l_lowc"], 1)
                    memory_tiles(0, 2)
                    for h in range(4):
                        dve.wait_ge(M["l_e1"], h + 1)
                        dve.tensor_scalar(la[:, h], (b5, b6)[h % 2][:, 0:SEQ], col("od_b", h), None, ALU.add)\
                            .then_inc(M["l_gate"], 1)
                    memory_tiles(2, 4)
                    for h in range(4):
                        dve.wait_ge(M["l_exp"], h + 1)
                        link(dve.scalar_tensor_tensor(la[:, h], la[:, h], 0.0, l_tmp[:, h], ALU.min, ALU.subtract))
                    link(dve.tensor_scalar(la, la, 1.0 / 16, None, ALU.mult))
                    for h in range(4):
                        for c in range(4):
                            cs = slice(64 * c, 64 * c + 64)
                            ins = dve.tensor_tensor_scan(la[:, h, cs], ones[:, 0:64], la[:, h, cs], 0.0, ALU.mult, ALU.add)
                    ins.then_inc(M["l_scan"], 1)
                    memory_tiles(4, 5)
                    dve.wait_ge(M["l_exp"], 5)
                    dve.scalar_tensor_tensor(lq.rearrange("p h t -> p (h t)"), lq.rearrange("p h t -> p (h t)"), 128.0 ** -0.5,
                                             l_tmp.rearrange("p h t -> p (h t)"), ALU.mult, ALU.mult)
                    memory_tiles(5, 6)
                    dve.wait_ge(M["l_exp"], 6)
                    dve.tensor_tensor(ks_t, ks_t, lk, ALU.mult).then_inc(M["l_ks"], 1)
                    dve.wait_ge(M["l_exp"], 7)
                    dve.tensor_tensor(lk, lk, lo_t[:, 4:8], ALU.mult).then_inc(M["l_qk"], 1)
                    memory_tiles(6, 8)
                    dve.wait_ge(M["l_att"], 1)
                    mats = att64.rearrange("p m h t -> p (m h) t")
                    cap = table("cap64").unsqueeze(1).to_broadcast([P, 8, 64])
                    ncap = table("ncap64").unsqueeze(1).to_broadcast([P, 8, 64])
                    link(dve.tensor_tensor(mats, b6[:].rearrange("p (m t) -> p m t", t=64), cap, ALU.min))
                    dve.tensor_tensor(mats, mats, ncap, ALU.max).then_inc(M["l_attc"], 1)
                    memory_tiles(8, 10)
                    for c in range(4):
                        cs = slice(64 * c, 64 * c + 64)
                        dve.wait_ge(M["l_o"], c + 1)
                        dve.tensor_copy(lo_t[:, :, cs], b7[:].rearrange("p (r t) -> p r t", t=64)).then_inc(M["l_oc"], 1)
                        if c < 3:
                            dve.wait_ge(M["l_ds"], c + 1)
                            for half in range(2):
                                new = (b4, b5)[half][:].rearrange("p (h v) -> p h v", h=2)
                                part = l_state[:, 2 * half:2 * half + 2]
                                if c == 0:
                                    ins = dve.tensor_copy(part, new)
                                else:
                                    if half == 0:
                                        dve.wait_ge(M["l_dsr"], c)
                                    f = l_dec[:, 2 * half:2 * half + 2, c].unsqueeze(2).to_broadcast([P, 2, 256])
                                    link(dve.tensor_tensor(part, part, f, ALU.mult))
                                    ins = dve.tensor_tensor(part, part, new, ALU.add)
                            ins.then_inc(M["l_dsr"], 1)
                            memory_tiles(10 + 2 * c, 12 + 2 * c)
                    dve.wait_ge(M["l_oc"], 4)
                    dve.wait_ge(M["silu_r"], 2)
                    head_norms([([lo_t[:, 2 * h + r] for r in range(2)], [col("od_o", 2 * h + r) for r in range(2)],
                                 [lo_t[:, 2 * h + r] for r in range(2)]) for h in range(4)],
                               gate=[lr[:, c] for c in range(8)], ts=REAL)
                residual(f"mix_out{layer}", f"memq{layer}", REAL)
                rms_ready()
                def project_xq(i, t, gt):
                    scaled(xq[:, 4 * i + t], t, gt, REAL)

                def second_xq(t):
                    b = phases[f"xq{layer}"].first + 1
                    project_xq(1, t, tile_at[b] + t)
                    split_low(b + 1, t - 1)

                stream(f"xq{layer}", project_xq, 0, 1)
                for x, g, between in ((xk, "xa_k", second_xq), (xq, "xa_q", None)):
                    head_norms([([x[:, 2 * h + r] for r in range(2)], [col(g, 2 * layer + r) for r in range(2)],
                                 [x[:, 2 * h + r] for r in range(2)]) for h in range(4)], between=between)
                attention([dict(nq=P, nk=SEQ, kind=None, parts=slice(0, P), chunks=slice(2 * h, 2 * h + 2),
                                tokens=slice(16 + m * P, 16 + (m + 1) * P)) for m in range(2) for h in range(4)])
                residual(f"x_out{layer}", f"ffn{layer}", REAL)
                rms_ready()
                mlp_swiglu(f"swiglu{layer}", "mix1" if layer == 0 else None, REAL)
            closing(2 + 2 * KD)

        @block.gpsimd
        def _(pool):
            fin = [0]

            def rows(target, at, n, source):
                pool.dma_start(target[at:at + n], source).then_inc(rows_in, 16)

            R = LATE_ROWS
            rows(late_rows, R["conv"], 60, w["conv_w_a"].rearrange("o j (t p) -> (o j t) p", p=P))
            for name, key in (("a_out", "a_out_norm_g"), ("c_q", "c_q_norm_g"), ("c_k", "c_k_norm_g")):
                rows(late_rows, R[name], 1, w[key])
            for name, key in (("b_q", "b_q_norm_g"), ("b_k", "b_k_norm_g"), ("ev_q", "ev_q_gain_2"), ("ev_k", "ev_k_gain_2")):
                for half in range(2):
                    rows(late_rows[:, 64 * half:64 * half + 64], R[name], 1, w[key])
            for name, key in (("xa_q", "xa_q_gain_2"), ("xa_k", "xa_k_gain_2")):
                rows(late_rows, R[name], 4, w[key].rearrange("l (r p) -> (l r) p", p=P))
            rows(late_rows, R["od_o"], 8, w["od_o_gain_2"].rearrange("o h (r p) -> (o h r) p", p=P))
            rows(late_rows, R["od_b"], 4, w["od_b_g_2"].rearrange("o (r p) -> (o r) p", p=P))

            def misc(target, source):
                pool.dma_start(target, source).then_inc(misc_in, 16)

            misc(early[:, 0:ew], w["early_tables"])
            misc(a_log, w["a_log"].rearrange("o d h -> (o d h)").partition_broadcast(P))
            misc(dt_bias, w["dt_bias"].rearrange("o d h -> (o d h)").partition_broadcast(P))
            misc(sink, w["b_sink"].rearrange("o h -> (o h)").partition_broadcast(P))
            misc(wg1, w["od_w_g1_2"][0].rearrange("(k p) r -> p k r", p=P))

            def add_squares(ts=slice(0, T)):
                n = fin[0] // KD
                if n >= 1:
                    pool.wait_ge(norm_summed, n)
                for k in range(KD):
                    f = fin[0]
                    fin[0] += 1
                    pool.wait_ge(squared, f + 1)
                    if k == 0:
                        pool.tensor_copy(square_sum[:, ts], squares[:, f % 2, ts]).then_inc(sum_added, 1)
                    else:
                        pool.wait_ge(sum_added, f)
                        pool.tensor_tensor(square_sum[:, ts], square_sum[:, ts], squares[:, f % 2, ts], ALU.add)\
                            .then_inc(sum_added, 1)

            add_squares()
            for c, (s, e) in enumerate(TILES):
                n = e - s
                for level in range(n_levels(n)):
                    mask = early_table(f"level{level}")[0:n, 0:n].unsqueeze(1).to_broadcast([n, 4, n])
                    for d in range(2):
                        if level == 0:
                            pool.wait_ge(M["d_n"], 2 * c + d + 1)
                            if c >= 1:
                                pool.wait_ge(M["d_w"], step_at(c, 1, d) - 1)
                        elif level == 1:
                            pool.wait_ge(M["d_x"], level_at(c, 0, d) + 1)
                        else:
                            pool.wait_ge(M["d_w"], step_at(c, level - 1, d) + 1)
                        pool.tensor_tensor(nb_[d][0:n, 0:4 * n].rearrange("p (h i) -> p h i", h=4),
                                           nn[d][0:n, 0:4 * n].rearrange("p (h i) -> p h i", h=4), mask, ALU.mult)\
                            .then_inc(M["d_nb"], 1)
            add_squares()
            add_squares()
            pool.dma_start(mem_rows, w["mem_2"][0].rearrange("(m p) d -> p m d", p=P)).then_inc(mem_in, 16)

            def later(target, source):
                pool.dma_start(target, source).then_inc(late_in, 16)

            later(ln_g, w["ev_ln_g_2"].rearrange("o g d -> (o g d)").partition_broadcast(P))
            later(ln_b, w["ev_ln_b_2"].rearrange("o g d -> (o g d)").partition_broadcast(P))
            for half in range(2):
                later(b_s[64 * half:64 * half + 64],
                      w["ev_b_s_2"][0].rearrange("(t two) i -> two t i", two=2)[half].partition_broadcast(64))
            later(pos_i.bitcast(I32), w["positions_2"].rearrange("o t -> (o t)").partition_broadcast(P))
            add_squares(slice(0, SEQ))
            pool.wait_ge(turn_read, 2 + 2 * KD)
            pool.dma_start(ws_rows.rearrange("p a (b j) -> p (a b) j", j=P), w["ev_w_s_2"][0].rearrange("g i j -> i g j"))\
                .then_inc(ws_in, 16)
            for norm in ("mlp1", "mix0", "memq0"):
                add_squares(REAL)
            pool.dma_start(wg2[0:16], w["od_w_g2_2"][0]).then_inc(wg_in, 16)
            for norm in ("ffn0", "mix1", "memq1", "ffn1"):
                add_squares(REAL)
            pool.wait_ge(turn_read, 2 + 2 * KD + 4)
            pool.dma_start(out[0].rearrange("(m p) d -> p m d", p=P), out_rows).then_inc(out_sent, 16)
            pool.wait_ge(out_sent, 16)


_INS = """x meta_tokens attn_norm_g mlp_norm_g w_in_ab conv_w_a a_log dt_bias a_out_norm_g b_q_norm_g b_k_norm_g b_sink
w_out_ab w_qkv_c c_q_norm_g c_k_norm_g w_out_c w_ff1 w_ff2 mem_2 positions_2 norm_mix_2 norm_mem_q_2 norm_mem_kv_2
norm_ffn_2 ev_w_in_2 ev_q_gain_2 ev_k_gain_2 ev_w_s_2 ev_b_s_2 ev_ln_g_2 ev_ln_b_2 ev_w_out_2 od_w_in_2 od_w_g1_2
od_w_g2_2 od_b_g_2 od_o_gain_2 od_w_out_2 xa_w_q_2 xa_w_kv_2 xa_q_gain_2 xa_k_gain_2 xa_w_out_2 ffn_w_gu_2
ffn_w_down_2""".split()


def kernel(**inputs):
    import concourse.bacc as _bacc
    from concourse.bass_utils import run_bass_kernel_spmd as _run

    nc = _bacc.Bacc("TRN2", target_bir_lowering=False, num_devices=1)
    arrays, w = {}, {}
    (tables, _), (early, _) = shape_constants()
    for name, a in [(n, inputs[n]) for n in _INS] + [("shape_tables", tables), ("early_tables", early)]:
        a = np.ascontiguousarray(a)
        arrays[f"in_{name}_dram"] = a
        w[name] = nc.dram_tensor(f"in_{name}_dram", a.shape, mybir.dt.from_np(a.dtype), kind="ExternalInput").ap()
    out = nc.dram_tensor("out_dram", (1, SEQ, D), F32, kind="ExternalOutput").ap()
    program(nc, w, out)
    return _run(nc, [arrays], core_ids=[0]).results[0]["out_dram"]
```
